# Optimizing a Trainium2 kernel written in Bass

```python
import jax, jax.numpy as jnp
from jax import lax
import numpy as np
import math

D_MODEL = 1024
BATCH = 1
SEQ = 512
DEPTH = 1

CHUNK = 64
N_LEFT_CHUNKS = 8
BAND = (N_LEFT_CHUNKS + 1) * CHUNK
A_HEADS = 8
A_HEAD_DIM = 64
A_WIDTH = A_HEADS * A_HEAD_DIM
REL_CLIP = 256
B_HEADS = 8
B_HEAD_DIM = 64
B_WIDTH = B_HEADS * B_HEAD_DIM
IDX_HEADS = 8
IDX_DIM = 32
TOPK_MAX = 256
Q_BLOCK = 128
ROPE_THETA = 500000.0
ROT_DIM_B = B_HEAD_DIM // 4
ROT_DIM_IDX = IDX_DIM // 4
EPS = 1e-6
NEG = -1e30

SPLIT_SIZES = (
    A_WIDTH, A_WIDTH, A_WIDTH, A_WIDTH,
    B_WIDTH, B_HEAD_DIM, B_HEAD_DIM, B_WIDTH,
    IDX_HEADS * IDX_DIM, IDX_DIM, IDX_HEADS,
    D_MODEL, D_MODEL,
)
IN_WIDTH = sum(SPLIT_SIZES)


def rms_norm(x, g):
    xf = x.astype(jnp.float32)
    y = xf * lax.rsqrt(jnp.mean(xf * xf, axis=-1, keepdims=True) + EPS)
    return (y * g.astype(jnp.float32)).astype(x.dtype)

def partial_rope(x, rot_dim):
    S = x.shape[1]
    half = rot_dim // 2
    inv = ROPE_THETA ** (-jnp.arange(half, dtype=jnp.float32) / half)
    ang = jnp.arange(S, dtype=jnp.float32)[:, None] * inv[None, :]
    cos = jnp.cos(ang)[None, :, None, :].astype(x.dtype)
    sin = jnp.sin(ang)[None, :, None, :].astype(x.dtype)
    x1, x2, xp = x[..., :half], x[..., half:rot_dim], x[..., rot_dim:]
    return jnp.concatenate([x1 * cos - x2 * sin, x2 * cos + x1 * sin, xp], axis=-1)

def chunked_relpos_attention(q, k, v, rel_bias):
    B, S, H, d = q.shape
    n_chunks = S // CHUNK
    pad = N_LEFT_CHUNKS * CHUNK
    k_pad = jnp.pad(k, ((0, 0), (pad, 0), (0, 0), (0, 0)))
    v_pad = jnp.pad(v, ((0, 0), (pad, 0), (0, 0), (0, 0)))
    i = jnp.arange(CHUNK)[:, None]
    j = jnp.arange(BAND)[None, :]
    dist = pad + i - j
    bias = rel_bias.astype(jnp.float32)[:, jnp.clip(dist, -REL_CLIP, REL_CLIP) + REL_CLIP]
    scale = d ** -0.5

    def one_chunk(c):
        start = c * CHUNK
        qc = lax.dynamic_slice_in_dim(q, start, CHUNK, axis=1)
        kc = lax.dynamic_slice_in_dim(k_pad, start, BAND, axis=1)
        vc = lax.dynamic_slice_in_dim(v_pad, start, BAND, axis=1)
        s = jnp.einsum('bqhd,bkhd->bhqk', qc, kc).astype(jnp.float32) * scale + bias[None]
        valid = (start - pad + j) >= 0
        s = jnp.where(valid[None, None], s, NEG)
        p = jax.nn.softmax(s, axis=-1).astype(v.dtype)
        return jnp.einsum('bhqk,bkhd->bqhd', p, vc)

    out = lax.map(one_chunk, jnp.arange(n_chunks))
    return out.transpose(1, 0, 2, 3, 4).reshape(B, S, H * d)

def dsa_sparse_attention(q, k, v, iq, ik, iw):
    B, S, H, d = q.shape
    top_k = min(TOPK_MAX, S // 4)
    n_blocks = S // Q_BLOCK
    key_chunk = jnp.arange(S) // CHUNK
    scale = d ** -0.5
    gather = jax.vmap(lambda a, idx: a[idx])

    def one_block(blk):
        start = blk * Q_BLOCK
        qb = lax.dynamic_slice_in_dim(q, start, Q_BLOCK, axis=1)
        iqb = lax.dynamic_slice_in_dim(iq, start, Q_BLOCK, axis=1)
        iwb = lax.dynamic_slice_in_dim(iw, start, Q_BLOCK, axis=1)
        q_chunk = (start + jnp.arange(Q_BLOCK)) // CHUNK
        logits = jax.nn.relu(jnp.einsum('bqhd,bsd->bqhs', iqb, ik))
        score = jnp.einsum('bqhs,bqh->bqs', logits, iwb).astype(jnp.float32)
        adm = key_chunk[None, :] <= q_chunk[:, None]
        score = jnp.where(adm[None], score, -jnp.inf)
        _, idx = lax.top_k(score, top_k)
        sel_valid = (idx // CHUNK) <= q_chunk[None, :, None]
        ks = gather(k, idx)
        vs = gather(v, idx)
        s = jnp.einsum('bqhd,bqkd->bqhk', qb, ks).astype(jnp.float32) * scale
        s = jnp.where(sel_valid[:, :, None, :], s, NEG)
        p = jax.nn.softmax(s, axis=-1).astype(v.dtype)
        return jnp.einsum('bqhk,bqkd->bqhd', p, vs)

    out = lax.map(one_block, jnp.arange(n_blocks))
    return out.transpose(1, 0, 2, 3, 4).reshape(B, S, H * d)

def first_inputs(seed: int = 0) -> dict:
    key = jax.random.key(seed)
    ks = jax.random.split(key, 10)
    nrm = jax.random.normal
    return {
        "x": nrm(ks[0], (BATCH, SEQ, D_MODEL), jnp.float32),
        "norm_gain": 1.0 + 0.05 * nrm(ks[1], (DEPTH, D_MODEL), jnp.float32),
        "w_in": nrm(ks[2], (DEPTH, D_MODEL, IN_WIDTH), jnp.float32) * D_MODEL ** -0.5,
        "b_merge": 0.05 * nrm(ks[3], (DEPTH, 2, D_MODEL), jnp.float32),
        "rel_bias": 0.2 * nrm(ks[4], (DEPTH, A_HEADS, 2 * REL_CLIP + 1), jnp.float32),
        "w_branch_a": nrm(ks[5], (DEPTH, A_WIDTH, D_MODEL), jnp.float32) * A_WIDTH ** -0.5,
        "w_branch_b": nrm(ks[6], (DEPTH, B_WIDTH, D_MODEL), jnp.float32) * B_WIDTH ** -0.5,
        "w_out": nrm(ks[7], (DEPTH, D_MODEL, D_MODEL), jnp.float32) * D_MODEL ** -0.5,
        "final_norm_gain": 1.0 + 0.05 * nrm(ks[8], (D_MODEL,), jnp.float32),
    }

def first_block(x, norm_gain, w_in, b_merge, rel_bias, w_branch_a, w_branch_b, w_out, final_norm_gain):
    B, S, _ = x.shape
    offsets = [int(o) for o in np.cumsum(SPLIT_SIZES)[:-1]]
    h = x
    for layer in range(DEPTH):
        xn = rms_norm(h, norm_gain[layer])
        proj = xn @ w_in[layer]
        qa, ka, va, ga, qb, kb, vb, gb, iq, ik, iw, za, zb = jnp.split(proj, offsets, axis=-1)
        qa = qa.reshape(B, S, A_HEADS, A_HEAD_DIM)
        ka = ka.reshape(B, S, A_HEADS, A_HEAD_DIM)
        va = va.reshape(B, S, A_HEADS, A_HEAD_DIM)
        ya = chunked_relpos_attention(qa, ka, va, rel_bias[layer]) * jax.nn.silu(ga)
        qb = partial_rope(qb.reshape(B, S, B_HEADS, B_HEAD_DIM), ROT_DIM_B)
        kb = partial_rope(kb[:, :, None, :], ROT_DIM_B)[:, :, 0]
        iq = partial_rope(iq.reshape(B, S, IDX_HEADS, IDX_DIM), ROT_DIM_IDX)
        ik = partial_rope(ik[:, :, None, :], ROT_DIM_IDX)[:, :, 0]
        iw = iw * (IDX_HEADS ** -0.5 * IDX_DIM ** -0.5)
        yb = dsa_sparse_attention(qb, kb, vb, iq, ik, iw) * jax.nn.silu(gb)
        gate_a = jax.nn.sigmoid(za + b_merge[layer, 0])
        gate_b = jax.nn.sigmoid(zb + b_merge[layer, 1])
        merged = gate_a * (ya @ w_branch_a[layer]) + gate_b * (yb @ w_branch_b[layer])
        h = h + merged @ w_out[layer]
    return rms_norm(h, final_norm_gain)


DEPTH_2 = 2

N_MIXERS = 2
N_LRU_LAYERS = (DEPTH_2 + 1) // 2
N_FOX_LAYERS = DEPTH_2 // 2
LRU_WIDTH = 1536
LRU_BLOCKS = 12
LRU_BLOCK_W = LRU_WIDTH // LRU_BLOCKS
CONV_WIDTH = 4
LRU_C = 8.0
FOX_HEADS = 16
FOX_HEAD_DIM = 64
FOX_WIDTH = FOX_HEADS * FOX_HEAD_DIM
NEG_INF = -1e30


def rms_norm_2(x, g):
    xf = x.astype(jnp.float32)
    y = xf * lax.rsqrt(jnp.mean(xf * xf, axis=-1, keepdims=True) + EPS)
    return (y * g.astype(jnp.float32)).astype(x.dtype)

def causal_depthwise_conv(x, w, b):
    c = x.shape[-1]
    y = lax.conv_general_dilated(
        x, w[:, None, :].astype(x.dtype), window_strides=(1,),
        padding=[(CONV_WIDTH - 1, 0)],
        dimension_numbers=("NWC", "WIO", "NWC"),
        feature_group_count=c)
    return y + b.astype(x.dtype)

def block_diag_linear(x, w, b):
    bsz, s, _ = x.shape
    xb = x.reshape(bsz, s, LRU_BLOCKS, LRU_BLOCK_W)
    y = jnp.einsum("bsnc,ncd->bsnd", xb, w.astype(x.dtype))
    return y.reshape(bsz, s, LRU_WIDTH) + b.astype(x.dtype)

def lru_mixer(h, w_in, conv_w, conv_b, wa, ba, wx, bx, a_param, w_out):
    u = h @ w_in.astype(h.dtype)
    xb, gate = u[..., :LRU_WIDTH], u[..., LRU_WIDTH:]
    xc = causal_depthwise_conv(xb, conv_w, conv_b)
    r = jax.nn.sigmoid(block_diag_linear(xc, wa, ba).astype(jnp.float32))
    i = jax.nn.sigmoid(block_diag_linear(xc, wx, bx).astype(jnp.float32))
    log_a = -LRU_C * r * jax.nn.softplus(-a_param.astype(jnp.float32))
    a = jnp.exp(log_a)
    mult = jnp.sqrt(-jnp.expm1(2.0 * log_a))
    bterm = mult * (i * xc.astype(jnp.float32))

    def combine(lhs, rhs):
        a1, b1 = lhs
        a2, b2 = rhs
        return a1 * a2, a2 * b1 + b2

    _, hs = lax.associative_scan(combine, (a, bterm), axis=1)
    y = hs.astype(h.dtype) * jax.nn.silu(gate)
    return y @ w_out.astype(h.dtype)

def fox_mixer(h, w_in, b_f, w_out):
    bsz, s, _ = h.shape
    u = h @ w_in.astype(h.dtype)
    q = u[..., 0 * FOX_WIDTH:1 * FOX_WIDTH].reshape(bsz, s, FOX_HEADS, FOX_HEAD_DIM)
    k = u[..., 1 * FOX_WIDTH:2 * FOX_WIDTH].reshape(bsz, s, FOX_HEADS, FOX_HEAD_DIM)
    v = u[..., 2 * FOX_WIDTH:3 * FOX_WIDTH].reshape(bsz, s, FOX_HEADS, FOX_HEAD_DIM)
    gate = u[..., 3 * FOX_WIDTH:4 * FOX_WIDTH]
    f_logit = u[..., 4 * FOX_WIDTH:].astype(jnp.float32) + b_f.astype(jnp.float32)
    cum = jnp.cumsum(jax.nn.log_sigmoid(f_logit), axis=1)
    ck = jnp.transpose(cum, (0, 2, 1))
    scale = 1.0 / math.sqrt(FOX_HEAD_DIM)
    n_blocks = s // Q_BLOCK
    qb = jnp.transpose(q.reshape(bsz, n_blocks, Q_BLOCK, FOX_HEADS, FOX_HEAD_DIM), (1, 0, 2, 3, 4))
    cqb = jnp.transpose(cum.reshape(bsz, n_blocks, Q_BLOCK, FOX_HEADS), (1, 0, 3, 2))
    starts = jnp.arange(n_blocks, dtype=jnp.int32) * Q_BLOCK
    kpos = jnp.arange(s, dtype=jnp.int32)
    kf = k.astype(jnp.float32)
    vf = v.astype(jnp.float32)

    def one_block(args):
        q_blk, cq_blk, start = args
        qpos = start + jnp.arange(Q_BLOCK, dtype=jnp.int32)
        logits = jnp.einsum("bqhd,bkhd->bhqk", q_blk.astype(jnp.float32), kf) * scale
        logits = logits + (cq_blk[..., :, None] - ck[:, :, None, :])
        mask = kpos[None, :] <= qpos[:, None]
        logits = jnp.where(mask[None, None], logits, NEG_INF)
        p = jax.nn.softmax(logits, axis=-1)
        return jnp.einsum("bhqk,bkhd->bqhd", p, vf)

    o = lax.map(one_block, (qb, cqb, starts))
    o = jnp.transpose(o, (1, 0, 2, 3, 4)).reshape(bsz, s, FOX_WIDTH).astype(h.dtype)
    y = o * jax.nn.silu(gate)
    return y @ w_out.astype(h.dtype)

def second_inputs(seed: int = 0) -> dict:
    key = jax.random.key(seed)
    ks = jax.random.split(key, 16)
    f32 = jnp.float32
    nl, nf = N_LRU_LAYERS, N_FOX_LAYERS
    x = jax.random.normal(ks[0], (BATCH, SEQ, D_MODEL), f32)
    norm_g = 1.0 + 0.05 * jax.random.normal(ks[1], (DEPTH_2, D_MODEL), f32)
    final_g = 1.0 + 0.05 * jax.random.normal(ks[2], (D_MODEL,), f32)
    lru_w_in = jax.random.normal(ks[3], (nl, D_MODEL, 2 * LRU_WIDTH), f32) * D_MODEL ** -0.5
    lru_conv_w = jax.random.normal(ks[4], (nl, CONV_WIDTH, LRU_WIDTH), f32) * CONV_WIDTH ** -0.5
    lru_conv_b = 0.02 * jax.random.normal(ks[5], (nl, LRU_WIDTH), f32)
    lru_wa = jax.random.normal(ks[6], (nl, LRU_BLOCKS, LRU_BLOCK_W, LRU_BLOCK_W), f32) * LRU_BLOCK_W ** -0.5
    lru_ba = 0.02 * jax.random.normal(ks[7], (nl, LRU_WIDTH), f32)
    lru_wx = jax.random.normal(ks[8], (nl, LRU_BLOCKS, LRU_BLOCK_W, LRU_BLOCK_W), f32) * LRU_BLOCK_W ** -0.5
    lru_bx = 0.02 * jax.random.normal(ks[9], (nl, LRU_WIDTH), f32)
    a_c = jax.random.uniform(ks[10], (nl, LRU_WIDTH), f32, minval=0.9, maxval=0.999)
    a0 = a_c ** (1.0 / LRU_C)
    lru_a_param = jnp.log(a0) - jnp.log1p(-a0)
    lru_w_out = jax.random.normal(ks[11], (nl, LRU_WIDTH, D_MODEL), f32) * LRU_WIDTH ** -0.5
    fox_w_in = jax.random.normal(ks[12], (nf, D_MODEL, 4 * FOX_WIDTH + FOX_HEADS), f32) * D_MODEL ** -0.5
    fox_b_f = 3.0 + 0.5 * jax.random.normal(ks[13], (nf, FOX_HEADS), f32)
    fox_w_out = jax.random.normal(ks[14], (nf, FOX_WIDTH, D_MODEL), f32) * FOX_WIDTH ** -0.5
    return {"x": x, "norm_g": norm_g, "final_g": final_g,
            "lru_w_in": lru_w_in, "lru_conv_w": lru_conv_w, "lru_conv_b": lru_conv_b,
            "lru_wa": lru_wa, "lru_ba": lru_ba, "lru_wx": lru_wx, "lru_bx": lru_bx,
            "lru_a_param": lru_a_param, "lru_w_out": lru_w_out,
            "fox_w_in": fox_w_in, "fox_b_f": fox_b_f, "fox_w_out": fox_w_out}

def second_block(x, norm_g, final_g, lru_w_in, lru_conv_w, lru_conv_b, lru_wa, lru_ba,
              lru_wx, lru_bx, lru_a_param, lru_w_out, fox_w_in, fox_b_f, fox_w_out):
    for i in range(DEPTH_2):
        h = rms_norm_2(x, norm_g[i])
        j = i // N_MIXERS
        if i % N_MIXERS == 0:
            x = x + lru_mixer(h, lru_w_in[j], lru_conv_w[j], lru_conv_b[j], lru_wa[j], lru_ba[j],
                              lru_wx[j], lru_bx[j], lru_a_param[j], lru_w_out[j])
        else:
            x = x + fox_mixer(h, fox_w_in[j], fox_b_f[j], fox_w_out[j])
    return rms_norm_2(x, final_g)


def setup_inputs(seed=0):
    out = dict(first_inputs(seed))
    for name, value in second_inputs(seed + 1).items():
        if name != "x":
            out[name + "_2"] = value
    return out


def reference(
    x, norm_gain, w_in, b_merge, rel_bias, w_branch_a, w_branch_b, w_out, final_norm_gain,
    norm_g_2, final_g_2, lru_w_in_2, lru_conv_w_2, lru_conv_b_2, lru_wa_2, lru_ba_2, lru_wx_2,
    lru_bx_2, lru_a_param_2, lru_w_out_2, fox_w_in_2, fox_b_f_2, fox_w_out_2,
):
    x = first_block(
        x, norm_gain, w_in, b_merge, rel_bias, w_branch_a, w_branch_b, w_out, final_norm_gain,
    )
    return second_block(
        x, norm_g_2, final_g_2, lru_w_in_2, lru_conv_w_2, lru_conv_b_2, lru_wa_2, lru_ba_2,
        lru_wx_2, lru_bx_2, lru_a_param_2, lru_w_out_2, fox_w_in_2, fox_b_f_2, fox_w_out_2,
    )


_drawn_inputs = setup_inputs


def setup_inputs(seed=0):
    import zlib

    import numpy as np

    out = dict(_drawn_inputs(seed))
    spreads = {}
    factors = {'norm_gain': 4.272,
     'b_merge': 8.0,
     'rel_bias': 6.996,
     'lru_ba_2': 35.425,
     'lru_bx_2': 22.708}
    for name, (base, spread) in spreads.items():
        noise = np.random.default_rng([zlib.crc32(name.encode()), seed]).standard_normal(out[name].shape)
        drawn = base * np.exp(spread * noise) if base else spread * noise
        out[name] = __import__('jax').numpy.asarray(drawn.astype(out[name].dtype))
    for name, factor in factors.items():
        out[name] = (out[name] * factor).astype(out[name].dtype)
    return out
```

```python
from contextlib import ExitStack

import numpy as np

S, D, P = 512, 1024, 128
KD = D // P
TB = S // P
HD = 64
CH = 64
TOPK = min(256, S // 4)
LRU_T = 12
LRU_G = 3
A_PAIRS, B_PAIRS, F_PAIRS = 4, 4, 8
PAIR_B0 = A_PAIRS
PAIR_F0 = A_PAIRS + B_PAIRS
PAIRS = A_PAIRS + B_PAIRS + F_PAIRS
EPS = 1e-6
BIG = 1e30
NOT_ADMITTED, TAKEN = -1e38, -3e38
EXT = 5 * P
RAW, RING = 2, 3

VEC = {}
_at = 0
for _name, _n in (("gain1", KD), ("final1", KD), ("gain2", KD), ("gain3", KD), ("final2", KD),
                  ("bma", KD), ("bmb", KD), ("conv_w", 4 * LRU_T), ("conv_b", LRU_T),
                  ("ba", LRU_T), ("bx", LRU_T), ("ap", LRU_T)):
    VEC[_name] = _at
    _at += _n
NVEC = _at
CON = {"ident": 0, "rot_b": 128, "rot_i": 256, "tri": 384, "half": 512, "upto": 640}
NCON = 640 + S


def slots_of_heads(first_pair, last_pair):
    out = {}
    for p in range(first_pair, last_pair):
        nxt, even, odd = p + 1, [], []
        if nxt < last_pair:
            even.append(("q", nxt))
            if nxt < PAIR_B0 or nxt >= PAIR_F0:
                even.append(("k", nxt))
            else:
                odd.append(("q_rot", nxt))
        odd.append(("g", p))
        out[2 * p], out[2 * p + 1] = even, odd
    return out


def make_plan():
    accs, units, widths = [], [], []

    def unit(name, width=KD * P):
        units.append(name)
        widths.append(width)
        return len(units) - 1

    def acc(name, blocks):
        accs.append((name, blocks))

    def whole(name):
        u = unit(name)
        acc(name, [(u, k) for k in range(KD)])

    def fill(names):
        for name in names:
            if name[0] == "q_rot":
                acc(name, [])
            else:
                whole(name)

    acc(("ssq", 0), [])
    for j in range(KD // 2):
        unit(("va", j))
    acc(("va", 0), [(units.index(("va", j)), i) for j in range(KD // 2) for i in range(2)])
    u = unit(("vbiw", 0), KD * 72)
    acc(("vbiw", 0), [(u, k) for k in range(KD)])
    for name in (("ik", 0), ("iq", 0), ("iq", 1), ("kb", 0)):
        whole(name)
        acc((name[0] + "_rot", name[1]), [])
    for t in range(KD):
        whole(("za", t))
    whole(("q", 0))
    whole(("k", 0))
    first = slots_of_heads(0, PAIR_B0 + B_PAIRS)
    for n in range(2 * PAIR_F0):
        fill(first[n])
    whole(("zb", 0))
    whole(("zb", 1))
    for t in range(KD):
        if t >= 2:
            whole(("zb", t))
        u = unit(("branch", t))
        acc(("pa", t), [(u, k) for k in range(4)])
        acc(("pb", t), [(u, 4 + k) for k in range(4)])
    for t in range(KD):
        whole(("wout", t))
    acc(("ssq", 1), [])
    acc(("ssq", 2), [])
    for g in range(LRU_T // LRU_G):
        w = unit(("wax", g), 2 * LRU_G * P)

        def ri(j):
            acc(("r", LRU_G * g + j), [(w, 2 * j)])
            acc(("i", LRU_G * g + j), [(w, 2 * j + 1)])

        whole(("xb", LRU_G * g))
        whole(("xb", LRU_G * g + 1))
        ri(0)
        whole(("xb", LRU_G * g + 2))
        ri(1)
        whole(("gl", LRU_G * g))
        ri(2)
        whole(("gl", LRU_G * g + 1))
        whole(("gl", LRU_G * g + 2))
    lo = [unit(("lout", j)) for j in range(LRU_T)]
    for t in range(KD):
        acc(("lo", t), [(lo[(LRU_T * t + k) // KD], (LRU_T * t + k) % KD) for k in range(LRU_T)])
    acc(("ssq", 3), [])
    u = unit(("f", 0), KD * 16)
    acc(("f", 0), [(u, k) for k in range(KD)])
    for half in range(2):
        if half == 1:
            acc(("cum", 0), [])
        for j in range(KD // 2):
            unit(("vf%d" % half, j))
        acc(("vf", half), [(units.index(("vf%d" % half, j)), i)
                           for j in range(KD // 2) for i in range(2)])
    whole(("q", PAIR_F0))
    whole(("k", PAIR_F0))
    second = slots_of_heads(PAIR_F0, PAIRS)
    for n in range(2 * PAIR_F0, 2 * PAIRS):
        fill(second[n])
    for t in range(KD):
        whole(("fo", t))
    acc(("ssq", 4), [])

    last_use = {}
    for a, (_, blocks) in enumerate(accs):
        for i, (u, _) in enumerate(blocks):
            last_use[u] = (a, i)
    steps, acc_done, unit_free = 0, {}, {}
    for a, (name, blocks) in enumerate(accs):
        for i, (u, _) in enumerate(blocks):
            ends = i == len(blocks) - 1
            if last_use[u] == (a, i) or ends:
                steps += 1
                if last_use[u] == (a, i):
                    unit_free[u] = steps
        if not blocks:
            steps += 1
        acc_done[name] = steps
    bank_user = [name for name, _ in accs if name[0] not in ("va", "vf")]
    number = {name: i for i, name in enumerate(bank_user)}
    return dict(accs=accs, blocks=dict(accs), units=units, widths=widths, last_use=last_use,
                order={name: a for a, (name, _) in enumerate(accs)},
                acc_done=acc_done, unit_free=unit_free, number=number)


PLAN = make_plan()


def build_program(nc, xT, vecs, rel_ext, b_f, consts, rope, wstream, outT):
    import concourse.bass as bass
    from concourse import mybir

    f32, f32r, bf16 = mybir.dt.float32, mybir.dt.float32r, mybir.dt.bfloat16
    ALU = mybir.AluOpType
    ACT = mybir.ActivationFunctionType
    AX = mybir.AxisListType.X

    units, widths, blocks_of = PLAN["units"], PLAN["widths"], PLAN["blocks"]
    acc_done, unit_free, number = PLAN["acc_done"], PLAN["unit_free"], PLAN["number"]
    NU = len(units)
    slot, before, ring_order = {}, {}, []
    for u, name in enumerate(units):
        if name[0] == "wax":
            slot[u] = None
            if name[1] > 0:
                before[u] = units.index(("wax", name[1] - 1))
        else:
            slot[u] = len(ring_order) % RING
            if len(ring_order) >= RING:
                before[u] = ring_order[-RING]
            ring_order.append(u)

    BIAS_W = P * TB
    rows_dram = nc.dram_tensor("ext_bias_rows", (8, P, EXT), f32, kind="Internal").ap()
    res_dram = nc.dram_tensor("res_spill", (P, KD, S), f32, kind="Internal").ap()

    OFF = [0, P, 3 * P, 6 * P]
    NP = 10 * P
    S_PARTS = [(3,), (0, 2), (1,)]
    S_BANK = [0, 1, 0]
    S_COL = {3: 0, 0: 0, 2: P, 1: 0}
    M_COL = {3: 0, 0: 1, 2: 2, 1: 3}
    T_PARTS = [(0,), (1, 3), (2,)]
    T_BANK = [0, 1, 0]
    T_OFF = {0: 0, 1: 4 * P, 3: 7 * P, 2: 8 * P}
    WK = [0, 0, 2 * P, 5 * P, 9 * P]

    ctx = ExitStack()
    with ctx:
        def sb(name, shape, dt):
            return ctx.enter_context(nc.sbuf_tensor(name, shape, dt))

        def sem(name):
            return ctx.enter_context(nc.semaphore(name))

        XH = sb("xn_hi", [P, KD, S], f32r)
        XL = sb("xn_lo", [P, KD, S], f32r)
        wraw = sb("w_raw", [P, RAW, KD * P], f32)
        whi = sb("w_hi", [P, RING, KD * P], f32r)
        wlo = sb("w_lo", [P, RING, KD * P], f32r)
        prob = sb("prob", [P, 2, NP], f32)
        PTH = sb("probT_hi", [P, NP], f32r)
        PTL = sb("probT_lo", [P, NP], f32r)
        tmp = sb("tmp", [P, 4, S], f32)
        sq = sb("sq", [P, 2, S], f32)
        rstd = sb("rstd", [P, 2, S], f32)
        sg = sb("gate", [P, 2, S], f32)
        yt = sb("y_f32", [P, 2, S], f32)
        vec = sb("vec", [P, NVEC], f32)
        hvec = sb("half_vec", [P, NVEC], f32)
        g12 = sb("gain12", [P, KD], f32)
        ident = sb("ident", [P, P], f32)
        ones = sb("ones", [P, P], f32)
        rotb = sb("rot_b", [P, P], f32r)
        roti = sb("rot_i", [P, P], f32r)
        idbig = sb("id_big", [P, P], bf16)
        tri = sb("tri", [P, P], bf16)
        upto = sb("upto", [P, S], f32)
        mx = sb("row_max", [P, 2, 4], f32)
        nmx = sb("row_negmax", [P, 2, 4], f32)
        rs = sb("row_sum", [P, 2, 4], f32)
        rcp = sb("row_rcp", [P, 2, 4], f32)
        iw = sb("iw", [P, TB, 8], f32)
        m8 = sb("max8", [P, 3, 8], f32)
        bfb = sb("b_f", [P, 16], f32)
        sp = sb("softplus", [P, 6, 64], f32)
        nsp4 = sb("nsp4", [P, LRU_T], f32)

        def zone(first_kib, spec):
            with ExitStack() as z:
                if first_kib:
                    z.enter_context(nc.sbuf_tensor(f"below_{spec[0][0]}", [P, first_kib * 256], f32))
                return [z.enter_context(nc.sbuf_tensor(*x)) for x in spec]

        QH, QL, KH, KL, VBH, VBL, KBH, KBL, bias, wk, MB, ROPE = zone(0, [
            ("q_hi", [P, 2, S], f32r), ("q_lo", [P, 2, S], f32r),
            ("k_hi", [P, 2, S], f32r), ("k_lo", [P, 2, S], f32r),
            ("vb_hi", [P, TB, P], f32r), ("vb_lo", [P, TB, P], f32r),
            ("kb_hi", [P, S], f32r), ("kb_lo", [P, S], f32r),
            ("bias", [P, 2, S], f32), ("index_score", [P, WK[4]], f32),
            ("top_mask", [P, NP], bf16), ("rope", [P, 4, S], f32)])
        VH, VL = zone(43, [("va_hi", [P, TB, S], f32r), ("va_lo", [P, TB, S], f32r)])
        YAH, YAL = zone(59, [("ya_hi", [P, 4, S], f32r), ("ya_lo", [P, 4, S], f32r)])
        GA, = zone(75, [("gate_a", [P, KD, S], f32)])
        XT, = zone(59, [("x_in", [P, KD, S], f32)])
        YBH, YBL = zone(43, [("yb_hi", [P, 4, S], f32r), ("yb_lo", [P, 4, S], f32r)])
        MGH, MGL = zone(0, [("merged_hi", [P, KD, S], f32r), ("merged_lo", [P, KD, S], f32r)])
        RES, = zone(75, [("res", [P, KD, S], f32)])
        YLH, YLL = zone(0, [("yl_hi", [P, LRU_T, S], f32r), ("yl_lo", [P, LRU_T, S], f32r)])
        LA, LX, LV, WAXH, WAXL = zone(48, [
            ("decay", [P, LRU_G, S], f32), ("gated_x", [P, LRU_G, S], f32),
            ("mult", [P, LRU_G, S], f32),
            ("wax_hi", [P, 2 * LRU_G * P], f32r), ("wax_lo", [P, 2 * LRU_G * P], f32r)])
        VFH, VFL, YFH, YFL, CQ, CK = zone(16, [
            ("vf_hi", [P, TB, 2 * S], f32r), ("vf_lo", [P, TB, 2 * S], f32r),
            ("yf_hi", [P, KD, S], f32r), ("yf_lo", [P, KD, S], f32r),
            ("cum_q", [P, 4, S], bf16), ("cum_k", [P, 4, S], bf16)])
        RES2, = zone(16, [("res_back", [P, KD, S], f32)])
        GB = tmp[:, 2:4, :]

        pj = [ctx.enter_context(nc.psum_tensor(f"acc{i}", [P, S], f32)) for i in range(2)]
        sbank = [ctx.enter_context(nc.psum_tensor(f"scores{i}", [P, S], f32)) for i in range(2)]
        tbank = [ctx.enter_context(nc.psum_tensor(f"probT{i}", [P, S], f32)) for i in range(2)]
        obank = [ctx.enter_context(nc.psum_tensor(f"out{i}", [P, S], f32)) for i in range(2)]
        tok = sbank + tbank

        x_loaded = [sem(f"x_loaded{i}") for i in range(4)]
        w_loaded = [sem(f"w_loaded{i}") for i in range(RAW)]
        const_loaded = sem("const_loaded")
        vec_loaded = sem("vec_loaded")
        ext_written = sem("ext_written")
        bias_loaded = [sem(f"bias_loaded{i}") for i in range(2)]
        res_loaded = [sem(f"res_loaded{t}") for t in range(KD)]
        res_spilled = sem("res_spilled")
        res_back = sem("res_back_loaded")
        cum_moved = sem("cum_moved")
        out_stored = sem("out_stored")
        w_hi = sem("w_hi_ready")
        xn_hi = sem("xn_hi_ready")
        acc_act = sem("acc_act_read")
        v_hi = sem("v_hi_ready")
        rope_hi = sem("rope_hi_ready")
        index_relu = sem("index_relu_ready")
        exp_done = sem("exp_done")
        pt_hi = sem("probT_hi_ready")
        y_hi = sem("y_hi_ready")
        sq_ready = sem("square_ready")
        root_ready = sem("root_ready")
        mg_hi = sem("merged_hi_ready")
        xc_hi = sem("conv_hi_ready")
        decay_ready = sem("decay_ready")
        mult_ready = sem("mult_ready")
        ls_exp = sem("logsig_exp_ready")
        act_own = sem("act_own")
        ones_ready = sem("ones_ready")
        consts_ready = sem("consts_ready")
        w_lo = sem("w_lo_ready")
        xn_f32 = sem("xn_f32_ready")
        xn_lo = sem("xn_lo_ready")
        v_lo = sem("v_lo_ready")
        rope_sum = sem("rope_sum_ready")
        rope_lo = sem("rope_lo_ready")
        index_sum = sem("index_sum_ready")
        mx_ready = sem("row_max_ready")
        prob_ready = sem("prob_ready")
        pt_lo = sem("probT_lo_ready")
        o_taken = sem("out_taken")
        y_lo = sem("y_lo_ready")
        sq_used = sem("square_used")
        var_ready = sem("var_ready")
        rstd2_ready = sem("rstd2_ready")
        mg_sum = sem("merged_sum_ready")
        mg_lo = sem("merged_lo_ready")
        xc_ready = sem("conv_ready")
        xc_lo = sem("conv_lo_ready")
        la_ready = sem("log_decay_ready")
        mult_sq = sem("mult_squared_ready")
        ls_arg = sem("logsig_arg_ready")
        ls_ready = sem("logsig_ready")
        cum_split = sem("cum_split_ready")
        yl_f32 = sem("recurrence_y_ready")
        out_ready = sem("out_ready")
        dve_own = sem("dve_own")
        acc_free = [sem(f"acc_free{i}") for i in range(2)]
        gemm_steps = sem("gemm_steps")
        index_done = sem("index_scores_done")
        s_done = sem("scores_done")
        t_done = sem("transpose_done")
        o_done = sem("out_done")
        bias_ready = sem("bias_ready")
        cum_ones = sem("cum_ones_ready")

        block = ctx.enter_context(nc.Block())

        def bank_of(name):
            return pj[number[name] % 2]

        def freed(name):
            return acc_free[number[name] % 2], number[name] // 2 + 1

        def cparts(negative, j):
            at = (3 * negative + j) * S // 2
            return prob[0:16, :, :].rearrange("h a b -> h (a b)")[:, at:at + S // 2].bitcast(bf16)

        @block.sync
        def _(sp):
            for i in range(4):
                sp.dma_start(XT[:, 2 * i:2 * i + 2, :], xT[:, 2 * i:2 * i + 2, :]).then_inc(x_loaded[i], 16)
            for u in range(NU):
                if u >= RAW:
                    sp.wait_ge(w_lo, u - RAW + 1)
                sp.dma_start(wraw[:, u % RAW, 0:widths[u]], wstream[u, :, 0:widths[u]])\
                  .then_inc(w_loaded[u % RAW], 16)
                if u == RAW - 1:
                    for dst, src in ((wk[:, 0:NCON], consts), (ROPE[:, :, :], rope),
                                     (bfb[:, :], b_f.to_broadcast([P, 16]))):
                        sp.dma_start(dst, src).then_inc(const_loaded, 16)

        @block.gpsimd
        def _(pool):
            pool.dma_start(rows_dram, bass.AP(rel_ext.tensor, 0, [[EXT, 8], [0, P], [1, EXT]])).then_inc(ext_written, 16)
            pool.wait_ge(ext_written, 16)
            for h in range(2 * A_PAIRS):
                if h >= 2:
                    pool.wait_ge(mx_ready, 3 * (h - 1))
                pool.dma_start(bias[:, h % 2, :], bass.AP(rows_dram.tensor, P * EXT * h + P - 1, [[EXT - 1, P], [1, S]]))\
                    .then_inc(bias_loaded[h % 2], 16)
                pool.wait_ge(bias_loaded[h % 2], 16 * (h // 2 + 1))
                pool.memset(bias[0:CH, h % 2, S - CH:S], -BIG).then_inc(bias_ready, 1)
            for t in range(KD):
                pool.wait_ge(mg_sum, t + 1)
                pool.dma_start(RES[:, t, :], xT[:, t, :]).then_inc(res_loaded[t], 16)
            for t in range(KD):
                pool.wait_ge(*freed(("lo", t)))
                pool.dma_start(res_dram[:, t, :], RES[:, t, :]).then_inc(res_spilled, 16)
            pool.wait_ge(xn_lo, 3 * KD)
            pool.wait_ge(res_spilled, 16 * KD)
            pool.memset(CQ[:, :, :], 1.0).then_inc(cum_ones, 1)
            pool.memset(CK[:, :, :], 1.0).then_inc(cum_ones, 1)
            pool.wait_ge(cum_ones, 2)
            pool.wait_ge(cum_split, 1)
            for g in range(4):
                for j in range(3):
                    pool.dma_start(CQ[32 * g + 3 + j:32 * g + 4 + j, :, :], cparts(0, j)[4 * g:4 * g + 4, :])\
                        .then_inc(cum_moved, 16)
                    pool.dma_start(CK[32 * g + j:32 * g + 1 + j, :, :], cparts(1, j)[4 * g:4 * g + 4, :])\
                        .then_inc(cum_moved, 16)
            pool.wait_ge(o_done, 2 * PAIRS)
            pool.dma_start(RES2[:, :, :], res_dram).then_inc(res_back, 16)
            pool.wait_ge(res_back, 16)
            for t in range(KD):
                pool.wait_ge(out_ready, t + 1)
                pool.dma_start(outT[:, t, :], RES2[:, t, :]).then_inc(out_stored, 16)
            pool.wait_ge(out_stored, 16 * KD)

        @block.tensor
        def _(pe):
            mm = pe.matmul

            def three(out, ah, al, bh, bl, start, stop):
                mm(out, ah, bh, start=start, stop=False)
                mm(out, ah, bl, start=False, stop=False)
                return mm(out, al, bh, start=False, stop=stop)

            def open_bank(name):
                n = number[name]
                if n >= 2:
                    pe.wait_ge(acc_free[n % 2], n // 2)

            def weights(u, b):
                if slot[u] is None:
                    return WAXH[:, b * P:b * P + P], WAXL[:, b * P:b * P + P]
                return whi[:, slot[u], b * P:b * P + P], wlo[:, slot[u], b * P:b * P + P]

            def close(name, i, last):
                u = blocks_of[name][i][0]
                if PLAN["last_use"][u] == (PLAN["order"][name], i) or i == len(blocks_of[name]) - 1:
                    last.then_inc(gemm_steps, 1)

            def gemm(name, rhs_hi, rhs_lo, first=0, end=None, ready=None):
                blocks = blocks_of[name]
                end = len(blocks) if end is None else end
                if first == 0:
                    open_bank(name)
                for i in range(first, end):
                    u, b = blocks[i]
                    if i == 0 or blocks[i - 1][0] != u:
                        pe.wait_ge(w_lo, u + 1)
                    if ready is not None:
                        pe.wait_ge(ready[0], ready[1] + i + 1)
                    wh, wl = weights(u, b)
                    last = three(bank_of(name)[:, :], wh, wl, rhs_hi[:, i, :], rhs_lo[:, i, :],
                                 i == 0, i == len(blocks) - 1)
                    close(name, i, last)

            def values(name, width=S):
                blocks = blocks_of[name]
                for i in range(KD):
                    u, half = blocks[i]
                    if half == 0:
                        pe.wait_ge(w_lo, u + 1)
                    if name[0] == "va":
                        pe.wait_ge(xn_lo, i + 1)
                    for t in range(TB):
                        if name == ("vf", 1) and i == 0:
                            pe.wait_ge(v_lo, TB + t + 1)
                        ts = slice(t * P, t * P + P)
                        ws = slice(half * S, half * S + S)
                        o = tok[t][:, :]
                        mm(o, XH[:, i, ts], whi[:, slot[u], ws], start=i == 0, stop=False)
                        mm(o, XH[:, i, ts], wlo[:, slot[u], ws], start=False, stop=False)
                        last = mm(o, XL[:, i, ts], whi[:, slot[u], ws], start=False, stop=i == KD - 1)
                    close(name, i, last)

            def small_values(name, n, xbase=None):
                open_bank(name)
                (u, _), = set((u, 0) for u, _ in blocks_of[name])
                pe.wait_ge(w_lo, u + 1)
                if xbase is not None:
                    pe.wait_ge(xn_lo, xbase + KD)
                for t in range(TB):
                    ts = slice(t * P, t * P + P)
                    o = bank_of(name)[:, t * n:t * n + n]
                    for k in range(KD):
                        wh, wl = (w[:, slot[u], k * n:k * n + n] for w in (whi, wlo))
                        mm(o, XH[:, k, ts], wh, start=k == 0, stop=False)
                        mm(o, XH[:, k, ts], wl, start=False, stop=False)
                        last = mm(o, XL[:, k, ts], wh, start=False, stop=k == KD - 1)
                last.then_inc(gemm_steps, 1)

            def rotate(name, rot, src):
                open_bank(name)
                pe.wait_ge(*freed(src))
                mm(bank_of(name)[:, :], rot[:, :], KH[:, 0, :], start=True, stop=False)
                mm(bank_of(name)[:, :], rot[:, :], KL[:, 0, :], start=False, stop=True).then_inc(gemm_steps, 1)

            def sum_squares(name, src, count):
                open_bank(name)
                pe.wait_ge(sq_used, count)
                mm(bank_of(name)[:, :], ones[:, :], src, start=True, stop=True).then_inc(gemm_steps, 1)

            def scores(n, part):
                pair, r0 = n // 2, HD * (n % 2)
                rows = slice(r0, r0 + HD)
                if part == 0 and n % 2 == 0:
                    if pair == 0:
                        pe.wait_ge(index_sum, 24)
                    if PAIR_B0 <= pair < PAIR_F0:
                        pe.wait_ge(rope_lo, 4 + pair - PAIR_B0 + 1)
                    else:
                        pe.wait_ge(*freed(("q", pair)))
                        pe.wait_ge(*freed(("k", pair)))
                    if pair == PAIR_B0:
                        pe.wait_ge(consts_ready, 2)
                    if pair == PAIR_F0:
                        pe.wait_ge(cum_moved, 24 * 16)
                        pe.wait_ge(v_lo, 3 * TB)
                if n > 0 or part == 2:
                    prior = 3 * n + {0: 0, 1: -1, 2: 1}[part]
                    pe.wait_ge(mx_ready if (prior - 1) // 3 < 2 * A_PAIRS else exp_done, prior)
                for qb in S_PARTS[part]:
                    w = P * (qb + 1)
                    o = sbank[S_BANK[part]][:, S_COL[qb]:S_COL[qb] + w]
                    qs = slice(qb * P, qb * P + P)
                    qh, ql = QH[rows, pair % 2, qs], QL[rows, pair % 2, qs]
                    if PAIR_B0 <= pair < PAIR_F0:
                        kh, kl = KBH[rows, 0:w], KBL[rows, 0:w]
                    else:
                        kh, kl = KH[rows, pair % 2, 0:w], KL[rows, pair % 2, 0:w]
                    last = three(o, qh, ql, kh, kl, True, pair < PAIR_B0)
                    if PAIR_B0 <= pair < PAIR_F0:
                        last = mm(o, idbig[:, :], MB[:, OFF[qb]:OFF[qb] + w], start=False, stop=True)
                    elif pair >= PAIR_F0:
                        h = n - 2 * PAIR_F0
                        g = slice(32 * (h // 4), 32 * (h // 4) + 6)
                        mm(o, CQ[g, h % 4, qs], CK[g, h % 4, 0:w], start=False, stop=False)
                        last = mm(o[:, w - P:w], idbig[:, :], tri[:, :], start=False, stop=True)
                last.then_inc(s_done, 1)

            def transposes(n, part):
                if part == 0:
                    pe.wait_ge(prob_ready, n + 1)
                if n > 0 or part == 2:
                    pe.wait_ge(pt_lo, 3 * n + {0: 0, 1: -1, 2: 1}[part])
                col = 0
                for kb in T_PARTS[part]:
                    for qb in range(kb, TB):
                        last = pe.transpose(tbank[T_BANK[part]][:, col:col + P],
                                            prob[:, n % 2, OFF[qb] + kb * P:OFF[qb] + kb * P + P],
                                            ident[:, :])
                        col += P
                last.then_inc(t_done, 1)

            def outputs(n):
                pair = n // 2
                if n >= 2:
                    pe.wait_ge(o_taken, n - 1)
                for part in range(3):
                    pe.wait_ge(pt_lo, 3 * n + part + 1)
                    for kb in T_PARTS[part]:
                        w = S - kb * P
                        if pair < PAIR_B0:
                            vh, vl = (v[:, kb, P * pair:P * pair + P] for v in (VH, VL))
                        elif pair < PAIR_F0:
                            vh, vl = VBH[:, kb, :], VBL[:, kb, :]
                        else:
                            c = P * (pair - PAIR_F0)
                            vh, vl = VFH[:, kb, c:c + P], VFL[:, kb, c:c + P]
                        ps = slice(T_OFF[kb], T_OFF[kb] + w)
                        last = three(obank[n % 2][:, kb * P:S], vh, vl, PTH[:, ps], PTL[:, ps],
                                     kb == 0, kb == 2)
                last.then_inc(o_done, 1)

            def attention(n0, n1, fills, tail):
                for n in range(n0, n1 + 1):
                    names = fills[n] if n < n1 else tail
                    lead = names[0] if names and names[0][0] != "q_rot" else None
                    for part, (k0, k1) in enumerate(((0, 2), (2, 5), (5, 8))):
                        if n > n0:
                            transposes(n - 1, part)
                        if n < n1:
                            scores(n, part)
                        if lead:
                            gemm(lead, XH, XL, k0, k1)
                    for name in names[1 if lead else 0:]:
                        if name[0] == "q_rot":
                            rotate(name, rotb, ("q", name[1]))
                        else:
                            gemm(name, XH, XL)
                    if n > n0:
                        outputs(n - 1)

            pe.wait_ge(ones_ready, 1)
            sum_squares(("ssq", 0), sq[:, 0, :], KD - 1)
            values(("va", 0))
            small_values(("vbiw", 0), 72)
            pe.wait_ge(consts_ready, 1)
            for name in (("ik", 0), ("iq", 0), ("iq", 1), ("kb", 0)):
                gemm(name, XH, XL)
                rotate((name[0] + "_rot", name[1]), rotb if name[0] == "kb" else roti, name)
            pe.wait_ge(rope_lo, 3)
            pe.wait_ge(v_lo, TB)
            for m in range(24):
                qb, h = m // 8 + 1, m % 8
                rows = slice(32 * (h % 4), 32 * (h % 4) + 32)
                if m >= 4:
                    pe.wait_ge(index_relu, m - 3)
                w = P * (qb + 1)
                qs = slice(qb * P, qb * P + P)
                three(tok[m % 4][:, 0:w], QH[rows, h // 4, qs], QL[rows, h // 4, qs],
                      KH[rows, 1, 0:w], KL[rows, 1, 0:w], True, True).then_inc(index_done, 1)
            for t in range(KD):
                gemm(("za", t), XH, XL)
            gemm(("q", 0), XH, XL)
            gemm(("k", 0), XH, XL)
            attention(0, 2 * PAIR_F0, slots_of_heads(0, PAIR_F0), [("zb", 0), ("zb", 1)])
            for t in range(KD):
                if t >= 2:
                    gemm(("zb", t), XH, XL)
                for name, yh, yl, base in ((("pa", t), YAH, YAL, 0), (("pb", t), YBH, YBL, 4)):
                    if t == 0:
                        pe.wait_ge(y_lo, base + 4)
                    gemm(name, yh, yl)
            for t in range(KD):
                gemm(("wout", t), MGH, MGL, ready=(mg_lo, 0) if t == 0 else None)
            sum_squares(("ssq", 1), sq[:, 0, :], 3 * (KD - 1))
            sum_squares(("ssq", 2), sq[:, 1, :], 3 * (KD - 1))

            def gate_inputs(c):
                pe.wait_ge(xc_lo, c + 1)
                for name in (("r", c), ("i", c)):
                    open_bank(name)
                    (u, b), = blocks_of[name]
                    pe.wait_ge(w_lo, u + 1)
                    wh, wl = weights(u, b)
                    cs = slice((c % 2) * S, (c % 2) * S + S)
                    last = three(bank_of(name)[:, :], wh, wl, PTH[:, cs], PTL[:, cs], True, True)
                    close(name, 0, last)

            for g in range(LRU_T // LRU_G):
                c = LRU_G * g
                gemm(("xb", c), XH, XL, ready=(xn_lo, KD) if g == 0 else None)
                gemm(("xb", c + 1), XH, XL)
                gate_inputs(c)
                gemm(("xb", c + 2), XH, XL)
                gate_inputs(c + 1)
                gemm(("gl", c), XH, XL)
                gate_inputs(c + 2)
                gemm(("gl", c + 1), XH, XL)
                gemm(("gl", c + 2), XH, XL)
            for t in range(KD):
                gemm(("lo", t), YLH, YLL, ready=(y_lo, 8) if t == 0 else None)
            sum_squares(("ssq", 3), sq[:, 0, :], 4 * (KD - 1))

            small_values(("f", 0), 16, 2 * KD)
            values(("vf", 0))
            open_bank(("cum", 0))
            pe.wait_ge(ls_ready, 2)
            for kb in range(TB):
                last = mm(bank_of(("cum", 0))[0:16, kb * P:S], sp[:, 5, kb * 16:kb * 16 + 16],
                          upto[:, 0:S - kb * P], start=kb == 0, stop=kb == TB - 1)
            last.then_inc(gemm_steps, 1)
            values(("vf", 1))
            gemm(("q", PAIR_F0), XH, XL)
            gemm(("k", PAIR_F0), XH, XL)
            attention(2 * PAIR_F0, 2 * PAIRS, slots_of_heads(PAIR_F0, PAIRS), [])
            for t in range(KD):
                gemm(("fo", t), YFH, YFL, ready=(y_lo, 8 + LRU_T) if t == 0 else None)
            sum_squares(("ssq", 4), sq[:, 0, :], 5 * (KD - 1))

        act_kinds = ("vbiw", "ik", "iq", "kb", "q", "k", "g", "gl")
        act_order = [name for name, _ in PLAN["accs"] if name[0] in act_kinds]
        act_read = {name: i + 1 for i, name in enumerate(act_order)}
        rope_order = [name for name, _ in PLAN["accs"] if name[0].endswith("_rot")]
        rope_number = {(name[0][:-4], name[1]): i for i, name in enumerate(rope_order)}

        def rope_parts(name):
            kind, i = name
            if kind == "ik":
                return KH[:, 1, :], KL[:, 1, :]
            if kind == "kb":
                return KBH[:, :], KBL[:, :]
            return QH[:, i % 2, :], QL[:, i % 2, :]

        def vcol(tensor, name, i):
            return tensor[:, VEC[name] + i:VEC[name] + i + 1]

        def values_of(name):
            if name[0] == "va":
                return VH, VL, slice(0, S)
            return VFH, VFL, slice(name[1] * S, name[1] * S + S)

        def gated(n):
            pair = n // 2
            rows = slice(HD * (n % 2), HD * (n % 2) + HD)
            if pair < PAIR_B0:
                return rows, YAH[:, pair, :], YAL[:, pair, :]
            if pair < PAIR_F0:
                return rows, YBH[:, pair - PAIR_B0, :], YBL[:, pair - PAIR_B0, :]
            return rows, YFH[:, pair - PAIR_F0, :], YFL[:, pair - PAIR_F0, :]

        class Refill:

            def __init__(self, split):
                self.next, self.split = 0, split

            def need(self, name):
                for u, _ in blocks_of[name]:
                    self.upto(u)

            def upto(self, u):
                while self.next <= u:
                    self.split(self.next)
                    self.next += 1

            def after(self, name):
                while self.next < NU and unit_free.get(before.get(self.next), 0) <= acc_done[name]:
                    self.split(self.next)
                    self.next += 1

        @block.scalar
        def _(act):
            act.dma_start(vec[:, :], vecs).then_inc(vec_loaded, 16)
            A = act.activation

            def split(u):
                act.wait_ge(w_loaded[u % RAW], 16 * (u // RAW + 1))
                if u in before:
                    act.wait_ge(gemm_steps, unit_free[before[u]])
                dst = WAXH[:, :] if slot[u] is None else whi[:, slot[u], 0:widths[u]]
                A(dst, wraw[:, u % RAW, 0:widths[u]], ACT.Copy).then_inc(w_hi, 1)

            refill = Refill(split)

            def evacuate(name):
                kind, i = name
                refill.need(name)
                act.wait_ge(gemm_steps, acc_done[name])
                if kind not in ("va", "vf"):
                    ps = bank_of(name)
                if kind in ("va", "vf"):
                    vh, _, cols = values_of(name)
                    for t in range(TB):
                        A(vh[:, t, cols], tok[t][:, :], ACT.Copy).then_inc(v_hi, 1)
                elif kind == "vbiw":
                    src = ps[:, 0:72 * TB].rearrange("p (t n) -> p t n", n=72)[:, :, 0:HD]
                    A(VBH[:, :, 0:HD], src, ACT.Copy)
                    A(VBH[:, :, HD:P], src, ACT.Copy).then_inc(acc_act, 1)
                elif name in rope_number:
                    A(KH[:, 0, :], ps[:, :], ACT.Copy).then_inc(acc_act, 1)
                elif kind in ("q", "k"):
                    A((QH if kind == "q" else KH)[:, i % 2, :], ps[:, :], ACT.Copy,
                      scale=HD ** -0.5 if kind == "q" else 1.0).then_inc(acc_act, 1)
                elif kind in ("g", "gl"):
                    if kind == "g" and i >= 2:
                        act.wait_ge(o_taken, 2 * i - 2)
                    if kind == "gl" and i >= 2:
                        act.wait_ge(yl_f32, i - 1)
                    A(sg[:, i % 2, :], ps[:, :], ACT.Tanh, scale=0.5).then_inc(acc_act, 1)
                elif kind == "za":
                    A(GA[:, i, :], ps[:, :], ACT.Tanh, scale=0.5, bias=vcol(hvec, "bma", i))\
                        .then_inc(freed(name)[0], 1)
                elif kind == "zb":
                    if i == 0:
                        act.wait_ge(rope_lo, 8)
                    if i >= 2:
                        act.wait_ge(mg_sum, i - 1)
                    A(GB[:, i % 2, :], ps[:, :], ACT.Tanh, scale=0.5, bias=vcol(hvec, "bmb", i))\
                        .then_inc(freed(name)[0], 1)
                elif kind == "xb":
                    if i >= 2:
                        act.wait_ge(xc_ready, i - 1)
                    A(prob[:, i % 2, 3:3 + S], ps[:, :], ACT.Copy).then_inc(freed(name)[0], 1)
                elif kind in ("r", "i"):
                    if kind == "r" and i >= 1:
                        act.wait_ge(mult_sq, i)
                    A(tmp[:, 0 if kind == "r" else 1, :], ps[:, :], ACT.Tanh, scale=0.5,
                      bias=vcol(hvec, "ba" if kind == "r" else "bx", i)).then_inc(freed(name)[0], 1)
                refill.after(name)

            def rotated(name):
                r = rope_number[name]
                act.wait_ge(rope_sum, r + 1)
                A(rope_parts(name)[0], tmp[:, 2, :], ACT.Copy,
                  scale=HD ** -0.5 if name[0] == "q" else 1.0).then_inc(rope_hi, 1)

            def exps(n, part):
                act.wait_ge(mx_ready, 3 * n + part + 1)
                for qb in S_PARTS[part]:
                    w = P * (qb + 1)
                    p = prob[:, n % 2, OFF[qb]:OFF[qb] + w]
                    c = M_COL[qb]
                    src = p if n < 2 * A_PAIRS else sbank[S_BANK[part]][:, S_COL[qb]:S_COL[qb] + w]
                    last = A(p, src, ACT.Exp, bias=nmx[:, n % 2, c:c + 1],
                             accum_out=rs[:, n % 2, c:c + 1])
                last.then_inc(exp_done, 1)

            def transposed(n, part):
                act.wait_ge(t_done, 3 * n + part + 1)
                w = sum(S - kb * P for kb in T_PARTS[part])
                c = T_OFF[T_PARTS[part][0]]
                A(PTH[:, c:c + w], tbank[T_BANK[part]][:, 0:w], ACT.Copy).then_inc(pt_hi, 1)

            def y_parts(n):
                if n % 2 == 1:
                    act.wait_ge(o_taken, n + 1)
                    A(gated(n)[1], yt[:, (n // 2) % 2, :], ACT.Copy).then_inc(y_hi, 1)

            def attention(n0, n1, fills, tail):
                for n in range(n0, n1 + 1):
                    names = fills[n] if n < n1 else tail
                    if names and names[0][0] != "q_rot":
                        refill.need(names[0])
                    for part in range(3):
                        if n > n0:
                            transposed(n - 1, part)
                        if n < n1:
                            exps(n, part)
                        if part == 0 and n >= n0 + 2:
                            y_parts(n - 2)
                    for name in names:
                        if name[0] == "q_rot":
                            rotated(("q", name[1]))
                            refill.after(name)
                        else:
                            evacuate(name)
                y_parts(n1 - 1)

            squares = [0]

            def square(src, t, scale=1.0, into=None):
                if t == 0:
                    A(sq[:, into or 0, :], src, ACT.Square, scale=scale).then_inc(sq_ready, 1)
                else:
                    k = squares[0]
                    A(yt[:, k % 2, :], src, ACT.Square, scale=scale).then_inc(sq_ready, 1)
                    squares[0] += 1

            def normalised(r):
                for t in range(KD):
                    act.wait_ge(xn_f32, KD * r + t + 1)
                    A(XH[:, t, :], tmp[:, 2 + t % 2, :], ACT.Copy).then_inc(xn_hi, 1)

            for t in range(KD):
                if t % 2 == 0:
                    act.wait_ge(x_loaded[t // 2], 16)
                if t >= 3:
                    act.wait_ge(sq_used, t - 2)
                square(XT[:, t, :], t)
            refill.upto(RAW - 1)
            act.wait_ge(var_ready, 1)
            A(rstd[:, 0, :], tmp[:, 3, :], ACT.Sqrt).then_inc(root_ready, 1)
            normalised(0)
            evacuate(("va", 0))
            evacuate(("vbiw", 0))
            for name in (("ik", 0), ("iq", 0), ("iq", 1), ("kb", 0)):
                evacuate(name)
                rotated(name)
            for m in range(24):
                act.wait_ge(index_done, m + 1)
                if m >= 2:
                    act.wait_ge(index_sum, m - 1)
                w = P * (m // 8 + 2)
                A(prob[:, m % 2, 0:w], tok[m % 4][:, 0:w], ACT.Relu).then_inc(index_relu, 1)
            act.wait_ge(consts_ready, 1)
            for t in range(KD):
                evacuate(("za", t))
            evacuate(("q", 0))
            evacuate(("k", 0))
            act.wait_ge(ls_arg, 1)
            A(sp[:, 1, 0:LRU_T], sp[:, 1, 0:LRU_T], ACT.Exp).then_inc(ls_exp, 1)
            attention(0, 2 * PAIR_F0, slots_of_heads(0, PAIR_F0), [("zb", 0), ("zb", 1)])

            def merged(t):
                act.wait_ge(mg_sum, t + 1)
                A(MGH[:, t, :], yt[:, t % 2, :], ACT.Copy, scale=0.5).then_inc(mg_hi, 1)

            for t in range(KD):
                if t >= 2:
                    evacuate(("zb", t))
                refill.need(("pb", t))
                merged(t)
                refill.after(("pb", t))

            def residual_squares(kind, used, finals=False):
                for t in range(KD):
                    refill.need((kind, t))
                    act.wait_ge(*freed((kind, t)))
                    src = (RES if kind != "fo" else RES2)[:, t, :]
                    if finals:
                        if t > 1:
                            act.wait_ge(sq_used, used + 2 * (t - 1))
                        if t == 0:
                            A(sq[:, 0, :], src, ACT.Square).then_inc(sq_ready, 1)
                            A(sq[:, 1, :], src, ACT.Square, scale=vcol(vec, "final1", t)).then_inc(sq_ready, 1)
                        else:
                            A(yt[:, 0, :], src, ACT.Square).then_inc(sq_ready, 1)
                            A(yt[:, 1, :], src, ACT.Square, scale=vcol(vec, "final1", t)).then_inc(sq_ready, 1)
                    else:
                        if t >= 3:
                            act.wait_ge(sq_used, used + t - 2)
                        square(src, t)
                    refill.after((kind, t))

            residual_squares("wout", KD - 1, finals=True)
            act.wait_ge(var_ready, 2)
            A(rstd[:, :, :], tmp[:, 0:2, :], ACT.Sqrt).then_inc(root_ready, 1)
            normalised(1)

            def conv_parts(c):
                act.wait_ge(xc_ready, c + 1)
                A(PTH[:, (c % 2) * S:(c % 2) * S + S], prob[:, c % 2, 640:640 + S], ACT.Copy).then_inc(xc_hi, 1)

            def decays(c):
                j = c % LRU_G
                evacuate(("r", c))
                evacuate(("i", c))
                if c >= LRU_G:
                    act.wait_ge(yl_f32, c - LRU_G + 1)
                act.wait_ge(la_ready, c + 1)
                A(LA[:, j, :], tmp[:, 2, :], ACT.Exp)
                A(tmp[:, 3, :], tmp[:, 2, :], ACT.Exp, scale=2.0)
                A(sq[:, 0, :], tmp[:, 2, :], ACT.Tanh, scale=-1.0).then_inc(decay_ready, 1)

            def yl_parts(c):
                act.wait_ge(yl_f32, c + 1)
                A(YLH[:, c, :], yt[:, c % 2, :], ACT.Copy).then_inc(y_hi, 1)

            for g in range(LRU_T // LRU_G):
                c = LRU_G * g
                evacuate(("xb", c))
                conv_parts(c)
                evacuate(("xb", c + 1))
                conv_parts(c + 1)
                decays(c)
                evacuate(("xb", c + 2))
                conv_parts(c + 2)
                decays(c + 1)
                evacuate(("gl", c))
                decays(c + 2)
                act.wait_ge(mult_sq, c + LRU_G)
                A(LV[:, :, :], LV[:, :, :], ACT.Sqrt, scale=0.25).then_inc(mult_ready, 1)
                evacuate(("gl", c + 1))
                yl_parts(c)
                evacuate(("gl", c + 2))
                yl_parts(c + 1)
                yl_parts(c + 2)
            residual_squares("lo", 3 * (KD - 1))
            act.wait_ge(var_ready, 3)
            A(rstd[:, 0, :], tmp[:, 0, :], ACT.Sqrt).then_inc(root_ready, 1)
            normalised(2)

            refill.need(("f", 0))
            act.wait_ge(ls_arg, 2)
            A(sp[:, 1, :], sp[:, 1, :], ACT.Exp).then_inc(ls_exp, 1)
            refill.after(("f", 0))
            evacuate(("vf", 0))
            evacuate(("vf", 1))
            evacuate(("q", PAIR_F0))
            evacuate(("k", PAIR_F0))
            attention(2 * PAIR_F0, 2 * PAIRS, slots_of_heads(PAIR_F0, PAIRS), [])
            residual_squares("fo", 4 * (KD - 1))
            act.wait_ge(var_ready, 4)
            A(rstd[:, 0, :], tmp[:, 0, :], ACT.Sqrt).then_inc(root_ready, 1)

        @block.vector
        def _(dve):
            T = dve.tensor_tensor
            TS = dve.tensor_scalar
            STT = dve.scalar_tensor_tensor
            own = [0]

            def step(ins):
                own[0] += 1
                ins.then_inc(dve_own, 1)

            def settle():
                dve.wait_ge(dve_own, own[0])

            def split(u):
                dve.wait_ge(w_hi, u + 1)
                raw = wraw[:, u % RAW, 0:widths[u]]
                hi, lo = ((WAXH[:, :], WAXL[:, :]) if slot[u] is None else
                          (whi[:, slot[u], 0:widths[u]], wlo[:, slot[u], 0:widths[u]]))
                T(lo, raw, hi, ALU.subtract).then_inc(w_lo, 1)

            refill = Refill(split)

            def low(dst, src, hi, scale=1.0):
                if scale == 1.0:
                    return T(dst, src, hi, ALU.subtract)
                return STT(dst, src, scale, hi, ALU.mult, ALU.subtract)

            def evacuate(name):
                kind, i = name
                refill.need(name)
                if name in act_read:
                    dve.wait_ge(acc_act, act_read[name])
                elif kind not in ("va", "vf"):
                    dve.wait_ge(gemm_steps, acc_done[name])
                if kind in ("va", "vf"):
                    vh, vl, cols = values_of(name)
                    first = 0 if kind == "va" else TB * (1 + i)
                    for t in range(TB):
                        dve.wait_ge(v_hi, first + t + 1)
                        low(vl[:, t, cols], tok[t][:, :], vh[:, t, cols]).then_inc(v_lo, 1)
                    refill.after(name)
                    return
                ps, free = bank_of(name), freed(name)[0]
                if kind == "vbiw":
                    both = ps[:, 0:72 * TB].rearrange("p (t n) -> p t n", n=72)
                    low(VBL[:, :, 0:HD], both[:, :, 0:HD], VBH[:, :, 0:HD])
                    low(VBL[:, :, HD:P], both[:, :, 0:HD], VBH[:, :, HD:P])
                    TS(iw[:, :, :], both[:, :, HD:72], 8 ** -0.5 * 32 ** -0.5, None, ALU.mult).then_inc(free, 1)
                elif name in rope_number:
                    cos = ROPE[:, 2 if kind in ("ik", "iq") else 0, :]
                    low(KL[:, 0, :], ps[:, :], KH[:, 0, :])
                    T(tmp[:, 0, :], ps[:, :], cos, ALU.mult).then_inc(free, 1)
                elif kind in ("q", "k"):
                    hi, lo = (QH, QL) if kind == "q" else (KH, KL)
                    low(lo[:, i % 2, :], ps[:, :], hi[:, i % 2, :],
                        HD ** -0.5 if kind == "q" else 1.0).then_inc(free, 1)
                elif kind in ("g", "gl"):
                    STT(sg[:, i % 2, :], sg[:, i % 2, :], 1.0, ps[:, :], ALU.add, ALU.mult).then_inc(free, 1)
                refill.after(name)

            def rotated(name):
                rot = (name[0] + "_rot", name[1])
                sin = ROPE[:, 3 if name[0] in ("ik", "iq") else 1, :]
                dve.wait_ge(gemm_steps, acc_done[rot])
                T(tmp[:, 1, :], bank_of(rot)[:, :], sin, ALU.mult).then_inc(freed(rot)[0], 1)
                dve.wait_ge(*freed(rot))
                dve.wait_ge(*freed(name))
                r = rope_number[name]
                T(tmp[:, 2, :], tmp[:, 0, :], tmp[:, 1, :], ALU.add).then_inc(rope_sum, 1)
                dve.wait_ge(rope_sum, r + 1)
                dve.wait_ge(rope_hi, r + 1)
                hi, lo = rope_parts(name)
                low(lo, tmp[:, 2, :], hi, HD ** -0.5 if name[0] == "q" else 1.0).then_inc(rope_lo, 1)
                refill.after(rot)

            def row_max(n, part):
                dve.wait_ge(s_done, 3 * n + part + 1)
                if n < 2 * A_PAIRS and part == 0:
                    dve.wait_ge(bias_ready, n + 1)
                for qb in S_PARTS[part]:
                    w, c = P * (qb + 1), M_COL[qb]
                    src = sbank[S_BANK[part]][:, S_COL[qb]:S_COL[qb] + w]
                    m = mx[:, n % 2, c:c + 1]
                    if n < 2 * A_PAIRS:
                        step(dve.tensor_tensor_reduce(
                            out=prob[:, n % 2, OFF[qb]:OFF[qb] + w], in0=src,
                            in1=bias[:, n % 2, S - w:S], scale=1.0, scalar=-3e38,
                            op0=ALU.add, op1=ALU.max, accum_out=m))
                    else:
                        step(dve.tensor_reduce(m, src, AX, ALU.max))
                settle()
                c0, k = M_COL[S_PARTS[part][0]], len(S_PARTS[part])
                TS(nmx[:, n % 2, c0:c0 + k], mx[:, n % 2, c0:c0 + k], -1.0, None, ALU.mult)\
                    .then_inc(mx_ready, 1)

            def probabilities(n):
                dve.wait_ge(exp_done, 3 * n + 3)
                step(dve.reciprocal(rcp[:, n % 2, :], rs[:, n % 2, :]))
                settle()
                for qb in range(TB):
                    p = prob[:, n % 2, OFF[qb]:OFF[qb] + P * (qb + 1)]
                    c = M_COL[qb]
                    last = TS(p, p, rcp[:, n % 2, c:c + 1], None, ALU.mult)
                last.then_inc(prob_ready, 1)

            def transposed(n, part):
                dve.wait_ge(pt_hi, 3 * n + part + 1)
                w = sum(S - kb * P for kb in T_PARTS[part])
                c = T_OFF[T_PARTS[part][0]]
                low(PTL[:, c:c + w], tbank[T_BANK[part]][:, 0:w], PTH[:, c:c + w]).then_inc(pt_lo, 1)

            tiles_y = [0]

            def take_output(n):
                rows, hi, lo = gated(n)
                dve.wait_ge(o_done, n + 1)
                pair = n // 2
                dve.wait_ge(*freed(("g", pair)))
                STT(yt[rows, pair % 2, :], obank[n % 2][rows, :], 0.5, sg[rows, pair % 2, :],
                    ALU.mult, ALU.mult).then_inc(o_taken, 1)

            def y_parts(n):
                if n % 2 == 1:
                    _, hi, lo = gated(n)
                    tiles_y[0] += 1
                    dve.wait_ge(o_taken, n + 1)
                    dve.wait_ge(y_hi, tiles_y[0])
                    low(lo, yt[:, (n // 2) % 2, :], hi).then_inc(y_lo, 1)

            def attention(n0, n1, fills, tail, extra):
                for n in range(n0, n1 + 1):
                    names = fills[n] if n < n1 else tail
                    if names and names[0][0] != "q_rot":
                        refill.need(names[0])
                    for part in range(3):
                        if n < n1:
                            row_max(n, part)
                        if n > n0:
                            transposed(n - 1, part)
                        if part == 0 and n >= n0 + 2:
                            take_output(n - 2)
                        if part == 1 and n >= n0 + 2:
                            y_parts(n - 2)
                    if n < n1:
                        probabilities(n)
                    extra(n)
                    for name in names:
                        if name[0] == "q_rot":
                            rotated(("q", name[1]))
                        else:
                            evacuate(name)
                take_output(n1 - 1)
                y_parts(n1 - 1)

            def one_square(t, used, buf, total=0):
                dve.wait_ge(sq_used, used)
                T(sq[:, total, :], sq[:, total, :], yt[:, buf, :], ALU.add).then_inc(sq_used, 1)

            def normalise(r, src, gain, root):
                def full(t):
                    if t >= 2:
                        dve.wait_ge(xn_lo, KD * r + t - 1)
                    STT(tmp[:, 2 + t % 2, :], src[:, t, :], gain(t), root, ALU.mult, ALU.mult)\
                        .then_inc(xn_f32, 1)

                def part(t):
                    dve.wait_ge(xn_hi, KD * r + t + 1)
                    low(XL[:, t, :], tmp[:, 2 + t % 2, :], XH[:, t, :]).then_inc(xn_lo, 1)

                full(0)
                for t in range(1, KD):
                    full(t)
                    part(t - 1)
                part(KD - 1)

            def log_sigmoid(src, n, dst, count):
                u, s, s2, p = (sp[:, j, 0:n] for j in (1, 2, 3, 4))
                STT(u, src, -1.0, src, ALU.mult, ALU.min).then_inc(ls_arg, 1)
                dve.wait_ge(ls_exp, count)
                step(TS(s, u, 2.0, None, ALU.add))
                settle()
                step(dve.reciprocal(s, s))
                settle()
                step(T(s, s, u, ALU.mult))
                settle()
                step(T(s2, s, s, ALU.mult))
                settle()
                step(TS(p, s2, 1.0 / 17, None, ALU.mult))
                settle()
                for k in range(7, 0, -1):
                    step(STT(p, p, 1.0 / (2 * k + 1), s2, ALU.add, ALU.mult))
                    settle()
                step(STT(p, p, 1.0, s, ALU.add, ALU.mult))
                settle()
                step(TS(s, src, 0.0, None, ALU.min))
                settle()
                STT(dst, p, -2.0, s, ALU.mult, ALU.add).then_inc(ls_ready, 1)

            dve.memset(ones[:, :], 1.0).then_inc(ones_ready, 1)

            for t in range(1, KD):
                dve.wait_ge(sq_ready, t + 1)
                one_square(t, t - 1, (t - 1) % 2)

            def inverse_variance(name, dst):
                dve.wait_ge(gemm_steps, acc_done[name])
                TS(dst, bank_of(name)[:, :], 1.0 / D, EPS, ALU.mult, ALU.add).then_inc(freed(name)[0], 1)
                dve.wait_ge(*freed(name))
                return dve.reciprocal(dst, dst)

            inverse_variance(("ssq", 0), tmp[:, 3, :]).then_inc(var_ready, 1)
            refill.upto(RAW - 1)
            dve.wait_ge(vec_loaded, 16)
            dve.wait_ge(root_ready, 1)
            normalise(0, XT, lambda t: vcol(vec, "gain1", t), rstd[:, 0, :])

            dve.wait_ge(const_loaded, 48)
            con = lambda name, n=P: wk[:, CON[name]:CON[name] + n]
            step(dve.tensor_copy(ident[:, :], con("ident")))
            dve.tensor_copy(rotb[:, :], con("rot_b"))
            dve.tensor_copy(roti[:, :], con("rot_i"))
            dve.tensor_copy(tri[:, :], con("tri"))
            dve.tensor_copy(MB[:, 0:P], con("half"))
            dve.tensor_copy(upto[:, :], con("upto", S))
            settle()
            TS(idbig[:, :], ident[:, :], BIG, None, ALU.mult)
            step(T(g12[:, :], vec[:, VEC["final1"]:VEC["final1"] + KD],
                   vec[:, VEC["gain2"]:VEC["gain2"] + KD], ALU.mult))
            TS(hvec[:, :], vec[:, :], 0.5, None, ALU.mult).then_inc(consts_ready, 1)
            dve.wait_ge(consts_ready, 1)
            evacuate(("va", 0))
            evacuate(("vbiw", 0))
            for name in (("ik", 0), ("iq", 0), ("iq", 1), ("kb", 0)):
                evacuate(name)
                rotated(name)
            for m in range(24):
                j, h = m // 8 + 1, m % 8
                w = P * (j + 1)
                dve.wait_ge(index_relu, m + 1)
                src, dst = prob[:, m % 2, 0:w], wk[:, WK[j]:WK[j] + w]
                if h == 0:
                    TS(dst, src, iw[:, j, 0:1], None, ALU.mult).then_inc(index_sum, 1)
                else:
                    dve.wait_ge(index_sum, m)
                    STT(dst, src, iw[:, j, h:h + 1], dst, ALU.mult, ALU.add).then_inc(index_sum, 1)
            dve.wait_ge(index_sum, 24)
            for j in (1, 2, 3):
                step(dve.memset(wk[0:CH, WK[j + 1] - CH:WK[j + 1]], NOT_ADMITTED))

            def top_round():
                settle()
                for j in (1, 2, 3):
                    step(dve.max(m8[:, j - 1, :], wk[:, WK[j]:WK[j + 1]]))
                for j in (1, 2, 3):
                    dve.wait_ge(dve_own, own[0] - 2)
                    row = wk[:, WK[j]:WK[j + 1]]
                    step(dve.match_replace(out=row, in_to_replace=m8[:, j - 1, :], in_values=row,
                                           imm_value=TAKEN))

            rounds = TOPK // 8
            for t in range(KD):
                top_round()
                refill.need(("za", t))
                refill.after(("za", t))
            rounds -= KD
            evacuate(("q", 0))
            evacuate(("k", 0))
            left = [rounds]

            def select(n):
                for _ in range(2 if n < 2 else 1):
                    if left[0] > 0:
                        top_round()
                        left[0] -= 1
                        if left[0] == 0:
                            settle()
                            TS(MB[:, P:NP], wk[:, :], TAKEN, -1.0, ALU.is_equal, ALU.add)\
                                .then_inc(consts_ready, 1)

            log_sigmoid(vec[:, VEC["ap"]:VEC["ap"] + LRU_T], LRU_T, sp[:, 5, 0:LRU_T], 1)
            dve.wait_ge(ls_ready, 1)
            step(TS(nsp4[:, :], sp[:, 5, 0:LRU_T], 4.0, None, ALU.mult))
            attention(0, 2 * PAIR_F0, slots_of_heads(0, PAIR_F0), [("zb", 0), ("zb", 1)], select)

            for t in range(KD):
                if t >= 2:
                    refill.need(("zb", t))
                    refill.after(("zb", t))
                refill.need(("pb", t))
                for name, gate, m in ((("pa", t), GA[:, t, :], 0), (("pb", t), GB[:, t % 2, :], 1)):
                    dve.wait_ge(gemm_steps, acc_done[name])
                    if m == 1:
                        dve.wait_ge(*freed(("zb", t)))
                    else:
                        dve.wait_ge(*freed(("za", t)))
                    STT(tmp[:, m, :], gate, 1.0, bank_of(name)[:, :], ALU.add, ALU.mult)\
                        .then_inc(freed(name)[0], 1)
                dve.wait_ge(*freed(("pa", t)))
                dve.wait_ge(*freed(("pb", t)))
                T(yt[:, t % 2, :], tmp[:, 0, :], tmp[:, 1, :], ALU.add).then_inc(mg_sum, 1)
                dve.wait_ge(mg_sum, t + 1)
                dve.wait_ge(mg_hi, t + 1)
                low(MGL[:, t, :], yt[:, t % 2, :], MGH[:, t, :], 0.5).then_inc(mg_lo, 1)
                refill.after(("pb", t))

            def residual(kind, res, ready, used, buf, double=False):
                def squares(t):
                    if double:
                        dve.wait_ge(sq_ready, ready + 2 * t + 2)
                        if t > 0:
                            one_square(t, used + 2 * t - 2, 0, 0)
                            one_square(t, used + 2 * t - 1, 1, 1)
                    else:
                        dve.wait_ge(sq_ready, ready + t + 1)
                        if t > 0:
                            one_square(t, used + t - 1, (buf + t - 1) % 2)

                for t in range(KD):
                    name = (kind, t)
                    refill.need(name)
                    if kind == "wout":
                        dve.wait_ge(res_loaded[t], 16)
                    dve.wait_ge(gemm_steps, acc_done[name])
                    T(res[:, t, :], bank_of(name)[:, :], res[:, t, :], ALU.add).then_inc(freed(name)[0], 1)
                    if t > 0:
                        squares(t - 1)
                    refill.after(name)
                squares(KD - 1)

            residual("wout", RES, KD, KD - 1, 0, double=True)
            step(inverse_variance(("ssq", 1), tmp[:, 0, :]))
            settle()
            two = ("ssq", 2)
            dve.wait_ge(gemm_steps, acc_done[two])
            STT(tmp[:, 1, :], bank_of(two)[:, :], 1.0 / D, tmp[:, 0, :], ALU.mult, ALU.mult)\
                .then_inc(freed(two)[0], 1)
            dve.wait_ge(*freed(two))
            step(TS(tmp[:, 1, :], tmp[:, 1, :], EPS, None, ALU.add))
            settle()
            dve.reciprocal(tmp[:, 1, :], tmp[:, 1, :]).then_inc(var_ready, 1)
            dve.wait_ge(root_ready, 2)
            step(T(rstd[:, 1, :], rstd[:, 0, :], rstd[:, 1, :], ALU.mult))
            settle()
            normalise(1, RES, lambda t: g12[:, t:t + 1], rstd[:, 1, :])

            step(dve.memset(prob[:, :, 0:3], 0.0))
            settle()

            def convolve(c):
                xb, xc = prob[:, c % 2, :], prob[:, c % 2, 640:640 + S]
                refill.need(("xb", c))
                dve.wait_ge(*freed(("xb", c)))
                if c >= 2:
                    dve.wait_ge(mult_sq, c - 1)
                tap = lambda i: vcol(vec, "conv_w", 4 * c + i)
                step(TS(xc, xb[:, 3:3 + S], tap(3), vcol(vec, "conv_b", c), ALU.mult, ALU.add))
                for i in (2, 1):
                    settle()
                    step(STT(xc, xb[:, i:i + S], tap(i), xc, ALU.mult, ALU.add))
                settle()
                STT(xc, xb[:, 0:S], tap(0), xc, ALU.mult, ALU.add).then_inc(xc_ready, 1)
                refill.after(("xb", c))
                dve.wait_ge(xc_ready, c + 1)
                dve.wait_ge(xc_hi, c + 1)
                cs = slice((c % 2) * S, (c % 2) * S + S)
                low(PTL[:, cs], xc, PTH[:, cs]).then_inc(xc_lo, 1)

            def decays(c):
                j = c % LRU_G
                refill.need(("i", c))
                settle()
                dve.wait_ge(*freed(("r", c)))
                TS(tmp[:, 2, :], tmp[:, 0, :], 1.0, nsp4[:, c:c + 1], ALU.add, ALU.mult).then_inc(la_ready, 1)
                dve.wait_ge(*freed(("i", c)))
                STT(LX[:, j, :], tmp[:, 1, :], 1.0, prob[:, c % 2, 640:640 + S], ALU.add, ALU.mult)
                refill.after(("i", c))

            def squared_mult(c):
                dve.wait_ge(decay_ready, c + 1)
                STT(LV[:, c % LRU_G, :], tmp[:, 3, :], 1.0, sq[:, 0, :], ALU.add, ALU.mult).then_inc(mult_sq, 1)

            def residual_x1(t):
                STT(RES[:, t, :], RES[:, t, :], vcol(vec, "final1", t), rstd[:, 0, :], ALU.mult, ALU.mult)

            def scan(c):
                j = c % LRU_G
                dve.wait_ge(mult_ready, c // LRU_G + 1)
                step(T(LX[:, j, :], LX[:, j, :], LV[:, j, :], ALU.mult))
                settle()
                step(dve.tensor_tensor_scan(LV[:, j, :], LA[:, j, :], LX[:, j, :], 0.0, ALU.mult, ALU.add))
                settle()
                dve.wait_ge(*freed(("gl", c)))
                STT(yt[:, c % 2, :], sg[:, c % 2, :], 0.5, LV[:, j, :], ALU.mult, ALU.mult).then_inc(yl_f32, 1)

            def yl_parts(c):
                tiles_y[0] += 1
                dve.wait_ge(yl_f32, c + 1)
                dve.wait_ge(y_hi, tiles_y[0])
                low(YLL[:, c, :], yt[:, c % 2, :], YLH[:, c, :]).then_inc(y_lo, 1)

            for g in range(LRU_T // LRU_G):
                c = LRU_G * g
                convolve(c)
                convolve(c + 1)
                decays(c)
                squared_mult(c)
                convolve(c + 2)
                decays(c + 1)
                residual_x1(2 * g)
                squared_mult(c + 1)
                evacuate(("gl", c))
                decays(c + 2)
                residual_x1(2 * g + 1)
                squared_mult(c + 2)
                scan(c)
                evacuate(("gl", c + 1))
                yl_parts(c)
                scan(c + 1)
                evacuate(("gl", c + 2))
                yl_parts(c + 1)
                scan(c + 2)
                yl_parts(c + 2)
            residual("lo", RES, 3 * KD, 3 * (KD - 1), KD - 1)
            inverse_variance(("ssq", 3), tmp[:, 0, :]).then_inc(var_ready, 1)
            dve.wait_ge(root_ready, 3)
            normalise(2, RES, lambda t: vcol(vec, "gain3", t), rstd[:, 0, :])

            refill.need(("f", 0))
            dve.wait_ge(gemm_steps, acc_done[("f", 0)])
            for t in range(TB):
                last = T(sp[:, 0, t * 16:t * 16 + 16], bank_of(("f", 0))[:, t * 16:t * 16 + 16], bfb[:, :], ALU.add)
            last.then_inc(freed(("f", 0))[0], 1)
            dve.wait_ge(*freed(("f", 0)))
            log_sigmoid(sp[:, 0, :], 64, sp[:, 5, :], 2)
            refill.after(("f", 0))
            dve.wait_ge(res_spilled, 16 * KD)
            evacuate(("vf", 0))
            dve.wait_ge(gemm_steps, acc_done[("cum", 0)])
            rest = tmp[0:16, 0, :]
            dve.tensor_copy(rest, bank_of(("cum", 0))[0:16, :]).then_inc(freed(("cum", 0))[0], 1)
            dve.wait_ge(*freed(("cum", 0)))
            for j in range(3):
                step(dve.tensor_copy(cparts(0, j), rest))
                settle()
                if j < 2:
                    step(T(rest, rest, cparts(0, j), ALU.subtract))
                last = TS(cparts(1, j), cparts(0, j), -1.0, None, ALU.mult)
                settle()
            last.then_inc(cum_split, 1)
            evacuate(("vf", 1))
            evacuate(("q", PAIR_F0))
            evacuate(("k", PAIR_F0))
            attention(2 * PAIR_F0, 2 * PAIRS, slots_of_heads(PAIR_F0, PAIRS), [], lambda n: None)
            dve.wait_ge(res_back, 16)
            residual("fo", RES2, 4 * KD, 4 * (KD - 1), 2 * (KD - 1))
            inverse_variance(("ssq", 4), tmp[:, 0, :]).then_inc(var_ready, 1)
            dve.wait_ge(root_ready, 4)
            for t in range(KD):
                STT(RES2[:, t, :], RES2[:, t, :], vcol(vec, "final2", t), rstd[:, 0, :], ALU.mult, ALU.mult)\
                    .then_inc(out_ready, 1)


def constants():
    con = np.zeros((P, NCON), np.float32)
    con[:, 0:P] = np.eye(P)
    tables = np.zeros((P, 4, S), np.float32)
    for i, (head, rot) in enumerate(((HD, HD // 4), (32, 32 // 4))):
        half = rot // 2
        inv = (np.float32(500000.0) ** (-np.arange(half, dtype=np.float32) / np.float32(half))).astype(np.float32)
        ang = (np.arange(S, dtype=np.float32)[:, None] * inv[None, :]).astype(np.float32).astype(np.float64)
        tables[:, 2 * i] = 1.0
        for base in range(0, P, head):
            for j in range(half):
                a, b = base + j, base + half + j
                con[b, CON[("rot_b", "rot_i")[i]] + a] = -1.0
                con[a, CON[("rot_b", "rot_i")[i]] + b] = 1.0
                tables[a, 2 * i] = tables[b, 2 * i] = np.cos(ang[:, j])
                tables[a, 2 * i + 1] = tables[b, 2 * i + 1] = np.sin(ang[:, j])
    p = np.arange(P)[:, None]
    con[:, CON["tri"]:CON["tri"] + P] = np.where(np.arange(P)[None, :] > p, -1.0, 0.0)
    con[:, CON["half"]:CON["half"] + P] = np.where((np.arange(P)[None, :] >= CH) & (p < CH), -1.0, 0.0)
    con[:, CON["upto"]:CON["upto"] + S] = np.arange(S)[None, :] >= p
    return con, tables


def pack(w_in, w_a, w_b, w_out, lru_in, wa, wx, lru_out, fox_in, fox_out):
    stream = np.zeros((len(PLAN["units"]), P, KD * P), np.float32)

    def columns(w, c0, n, k0=0, k1=None):
        part = w[k0 * P:(w.shape[0] if k1 is None else k1 * P), c0:c0 + n]
        return part.reshape(-1, P, n).transpose(1, 0, 2).reshape(P, -1)

    lout = np.concatenate([columns(lru_out, t * P, P) for t in range(KD)], axis=1)
    for u, (kind, i) in enumerate(PLAN["units"]):
        if kind == "va":
            part = columns(w_in, 1024, S, 2 * i, 2 * i + 2)
        elif kind == "vbiw":
            part = np.concatenate([w_in[:, 2624:2688], w_in[:, 3488:3496]], axis=1)
            part = columns(part, 0, 72)
        elif kind == "ik":
            part = columns(np.concatenate([w_in[:, 3456:3488]] * 4, axis=1), 0, P)
        elif kind == "kb":
            part = columns(np.concatenate([w_in[:, 2560:2624]] * 2, axis=1), 0, P)
        elif kind == "iq":
            part = columns(w_in, 3200 + i * P, P)
        elif kind == "za":
            part = columns(w_in, 3496 + i * P, P)
        elif kind == "zb":
            part = columns(w_in, 4520 + i * P, P)
        elif kind in ("q", "k", "g") and i < PAIR_B0:
            part = columns(w_in, {"q": 0, "k": 512, "g": 1536}[kind] + i * P, P)
        elif kind in ("q", "g") and i < PAIR_F0:
            part = columns(w_in, {"q": 2048, "g": 2688}[kind] + (i - PAIR_B0) * P, P)
        elif kind in ("q", "k", "g"):
            part = columns(fox_in, {"q": 0, "k": 1024, "g": 3072}[kind] + (i - PAIR_F0) * P, P)
        elif kind == "branch":
            part = np.concatenate([columns(w_a, i * P, P), columns(w_b, i * P, P)], axis=1)
        elif kind == "wout":
            part = columns(w_out, i * P, P)
        elif kind == "wax":
            both = [w[LRU_G * i + j] for j in range(LRU_G) for w in (wa, wx)]
            part = np.concatenate(both, axis=1)
        elif kind == "xb":
            part = columns(lru_in, i * P, P)
        elif kind == "gl":
            part = columns(lru_in, LRU_T * P + i * P, P)
        elif kind == "lout":
            part = lout[:, i * KD * P:(i + 1) * KD * P]
        elif kind == "f":
            part = columns(fox_in, 4096, 16)
        elif kind in ("vf0", "vf1"):
            part = columns(fox_in, 2048 + S * int(kind[2]), S, 2 * i, 2 * i + 2)
        elif kind == "fo":
            part = columns(fox_out, i * P, P)
        stream[u, :, 0:part.shape[1]] = part
    return stream


def kernel(**inputs):
    import concourse.bacc as bacc
    from concourse import mybir
    from concourse.bass_utils import run_bass_kernel_spmd

    a = {k: np.asarray(v) for k, v in inputs.items()}
    tiles = lambda v: v.reshape(-1, P).T
    vecs = np.concatenate([
        tiles(a["norm_gain"][0]), tiles(a["final_norm_gain"]), tiles(a["norm_g_2"][0]),
        tiles(a["norm_g_2"][1]), tiles(a["final_g_2"]), tiles(a["b_merge"][0, 0]),
        tiles(a["b_merge"][0, 1]),
        a["lru_conv_w_2"][0].reshape(4, LRU_T, P).transpose(2, 1, 0).reshape(P, 4 * LRU_T),
        tiles(a["lru_conv_b_2"][0]), tiles(a["lru_ba_2"][0]), tiles(a["lru_bx_2"][0]),
        tiles(a["lru_a_param_2"][0])], axis=1)
    con, tables = constants()
    arrays = {
        "xT": a["x"][0].T.reshape(KD, P, S).transpose(1, 0, 2),
        "vecs": vecs,
        "rel_ext": np.concatenate([a["rel_bias"][0][:, -1:]] * (2 * P - 1)
                                  + [a["rel_bias"][0][:, ::-1][:, 0:3 * P + 1]], axis=1),
        "b_f": a["fox_b_f_2"],
        "consts": con,
        "rope_tables": tables,
        "wstream": pack(a["w_in"][0], a["w_branch_a"][0], a["w_branch_b"][0], a["w_out"][0],
                        a["lru_w_in_2"][0], a["lru_wa_2"][0], a["lru_wx_2"][0],
                        a["lru_w_out_2"][0], a["fox_w_in_2"][0], a["fox_w_out_2"][0]),
    }
    arrays = {k: np.ascontiguousarray(v) for k, v in arrays.items()}
    nc = bacc.Bacc("TRN2", target_bir_lowering=False, num_devices=1)
    args = [nc.dram_tensor("in_" + k, v.shape, mybir.dt.from_np(v.dtype), kind="ExternalInput").ap()
            for k, v in arrays.items()]
    out = nc.dram_tensor("outT", (P, KD, S), mybir.dt.float32, kind="ExternalOutput").ap()
    build_program(nc, *args, out)
    got = run_bass_kernel_spmd(nc, [{"in_" + k: v for k, v in arrays.items()}], core_ids=[0]).results[0]["outT"]
    return np.ascontiguousarray(got.transpose(2, 1, 0).reshape(1, S, D))
```

```python
from contextlib import ExitStack

import numpy as np

S, D, P = 512, 1024, 128
KD = D // P
TB = S // P
HD = 64
CH = 64
TOPK = min(256, S // 4)
LRU_T = 12
LRU_G = 3
A_PAIRS, B_PAIRS, F_PAIRS = 4, 4, 8
PAIR_B0 = A_PAIRS
PAIR_F0 = A_PAIRS + B_PAIRS
PAIRS = A_PAIRS + B_PAIRS + F_PAIRS
EPS = 1e-6
BIG = 1e30
NOT_ADMITTED, TAKEN = -1e38, -3e38
EXT = 5 * P
RAW, RING = 2, 4

VEC = {}
_at = 0
for _name, _n in (("gain1", KD), ("final1", KD), ("gain2", KD), ("gain3", KD), ("final2", KD),
                  ("conv_w", 4 * LRU_T), ("conv_b", LRU_T),
                  ("bma", KD), ("bmb", KD), ("ba", LRU_T), ("bx", LRU_T), ("ap", LRU_T)):
    VEC[_name] = _at
    _at += _n
NVEC = _at
HALVED = slice(VEC["bma"], VEC["ap"])
CON = {"ident": 0, "rot_b": 128, "rot_i": 256, "tri": 384, "half": 512, "upto": 640}
NCON = 640 + S


def slots_of_heads(first_pair, last_pair):
    out = {}
    for p in range(first_pair, last_pair):
        nxt, gate = p + 1, [("g", p)]
        if nxt == last_pair:
            even, odd = [], gate
        elif nxt == PAIR_B0:
            even, odd = [("q", nxt)] + gate, [("q_rot", nxt), ("kb", 0), ("kb_rot", 0)]
        elif PAIR_B0 < nxt < PAIR_F0:
            even, odd = [("q", nxt)], [("q_rot", nxt)] + gate
        else:
            even, odd = [("q", nxt), ("k", nxt)], gate
        out[2 * p], out[2 * p + 1] = even, odd
    return out


def make_plan():
    accs, units, widths = [], [], []

    def unit(name, width=KD * P):
        units.append(name)
        widths.append(width)
        return len(units) - 1

    def acc(name, blocks):
        accs.append((name, blocks))

    def whole(name):
        u = unit(name)
        acc(name, [(u, k) for k in range(KD)])

    def fill(names):
        for name in names:
            if name[0].endswith("_rot"):
                acc(name, [])
            else:
                whole(name)

    acc(("ssq", 0), [])
    for j in range(KD // 2):
        unit(("va", j))
    acc(("va", 0), [(units.index(("va", j)), i) for j in range(KD // 2) for i in range(2)])
    u = unit(("vbiw", 0), KD * 72)
    acc(("vbiw", 0), [(u, k) for k in range(KD)])
    for name in (("ik", 0), ("iq", 0), ("iq", 1)):
        whole(name)
        acc((name[0] + "_rot", name[1]), [])
    for t in range(KD):
        whole(("za", t))
    whole(("q", 0))
    whole(("k", 0))
    first = slots_of_heads(0, PAIR_B0 + B_PAIRS)
    for n in range(2 * PAIR_F0):
        fill(first[n])
    whole(("zb", 0))
    whole(("zb", 1))
    for t in range(KD):
        if t >= 2:
            whole(("zb", t))
        u = unit(("branch", t))
        acc(("pa", t), [(u, k) for k in range(4)])
        acc(("pb", t), [(u, 4 + k) for k in range(4)])
    for t in range(KD):
        whole(("wout", t))
    acc(("ssq", 1), [])
    whole(("xb", 0))
    for c in range(LRU_T):
        if c + 1 < LRU_T:
            whole(("xb", c + 1))
        w = unit(("wax", c), 2 * P)
        acc(("r", c), [(w, 0)])
        acc(("i", c), [(w, 1)])
        if c >= 1:
            whole(("gl", c - 1))
    whole(("gl", LRU_T - 1))
    lo = [unit(("lout", j)) for j in range(LRU_T)]
    for t in range(KD):
        acc(("lo", t), [(lo[(LRU_T * t + k) // KD], (LRU_T * t + k) % KD) for k in range(LRU_T)])
    acc(("ssq", 2), [])
    u = unit(("f", 0), KD * 16)
    acc(("f", 0), [(u, k) for k in range(KD)])
    for half in range(2):
        if half == 1:
            acc(("cum", 0), [])
        for j in range(KD // 2):
            unit(("vf%d" % half, j))
        acc(("vf", half), [(units.index(("vf%d" % half, j)), i)
                           for j in range(KD // 2) for i in range(2)])
    whole(("q", PAIR_F0))
    whole(("k", PAIR_F0))
    second = slots_of_heads(PAIR_F0, PAIRS)
    for n in range(2 * PAIR_F0, 2 * PAIRS):
        fill(second[n])
    for t in range(KD):
        whole(("fo", t))
    acc(("ssq", 3), [])

    last_use = {}
    for a, (_, blocks) in enumerate(accs):
        for i, (u, _) in enumerate(blocks):
            last_use[u] = (a, i)
    steps, acc_done, unit_free = 0, {}, {}
    for a, (name, blocks) in enumerate(accs):
        for i, (u, _) in enumerate(blocks):
            ends = i == len(blocks) - 1
            if last_use[u] == (a, i) or ends:
                steps += 1
                if last_use[u] == (a, i):
                    unit_free[u] = steps
        if not blocks:
            steps += 1
        acc_done[name] = steps
    bank, used, turn = {}, [0] * 8, {"two": 0, "six": 0}
    for name, _ in accs:
        if name[0] in ("va", "vf"):
            continue
        ring = "six" if name[0] in ("xb", "gl", "r", "i") else "two"
        b = 2 + turn[ring] % 6 if ring == "six" else turn[ring] % 2
        turn[ring] += 1
        bank[name] = (b, used[b])
        used[b] += 1
    return dict(accs=accs, blocks=dict(accs), units=units, widths=widths, last_use=last_use,
                order={name: a for a, (name, _) in enumerate(accs)},
                acc_done=acc_done, unit_free=unit_free, bank=bank)


PLAN = make_plan()


def build_program(nc, xT, vecs, rel_ext, b_f, consts, rope, wstream, outT):
    import concourse.bass as bass
    from concourse import mybir

    f32, f32r, bf16 = mybir.dt.float32, mybir.dt.float32r, mybir.dt.bfloat16
    ALU = mybir.AluOpType
    ACT = mybir.ActivationFunctionType
    AX = mybir.AxisListType.X

    units, widths, blocks_of = PLAN["units"], PLAN["widths"], PLAN["blocks"]
    acc_done, unit_free, bank_use = PLAN["acc_done"], PLAN["unit_free"], PLAN["bank"]
    NU = len(units)
    slot, before, ring_order = {}, {}, []
    for u, name in enumerate(units):
        if name[0] == "wax":
            slot[u] = None
            if name[1] >= LRU_G:
                before[u] = units.index(("wax", name[1] - LRU_G))
        else:
            slot[u] = len(ring_order) % RING
            if len(ring_order) >= RING:
                before[u] = ring_order[-RING]
            ring_order.append(u)

    BIAS_W = P * TB
    rows_dram = nc.dram_tensor("ext_bias_rows", (8, P, EXT), f32, kind="Internal").ap()
    res_dram = nc.dram_tensor("res_spill", (P, KD, S), f32, kind="Internal").ap()

    OFF = [0, P, 3 * P, 6 * P]
    NP = 10 * P
    S_PARTS = [(3,), (0, 2), (1,)]
    S_BANK = [0, 1, 0]
    S_COL = {3: 0, 0: 0, 2: P, 1: 0}
    M_COL = {3: 0, 0: 1, 2: 2, 1: 3}
    T_PARTS = [(0,), (1, 3), (2,)]
    T_BANK = [0, 1, 0]
    T_OFF = {0: 0, 1: 4 * P, 3: 7 * P, 2: 8 * P}
    WK = [0, 0, 2 * P, 5 * P, 9 * P]

    ctx = ExitStack()
    with ctx:
        def sb(name, shape, dt):
            return ctx.enter_context(nc.sbuf_tensor(name, shape, dt))

        def sem(name):
            return ctx.enter_context(nc.semaphore(name))

        XH = sb("xn_hi", [P, KD, S], f32r)
        XL = sb("xn_lo", [P, KD, S], f32r)
        wraw = sb("w_raw", [P, RAW, KD * P], f32)
        whi = sb("w_hi", [P, RING, KD * P], f32r)
        wlo = sb("w_lo", [P, RING, KD * P], f32r)
        prob = sb("prob", [P, 2, NP], f32)
        PTH = sb("probT_hi", [P, NP], f32r)
        PTL = sb("probT_lo", [P, NP], f32r)
        tmp = sb("tmp", [P, 4, S], f32)
        sq = prob[:, 1, 0:2 * S].rearrange("p (a b) -> p a b", a=2)
        diag = sb("diag", [P, S], f32)
        decay2 = sb("decay_squared", [P, S], f32)
        mean = sb("mean_square", [P, 2 * TB], f32)
        root = sb("row_factor", [P, 4, 2 * TB], f32)
        sg = sb("gate", [P, 2, S], f32)
        yt = sb("y_f32", [P, 2, S], f32)
        vec = sb("vec", [P, NVEC], f32)
        hvec = sb("half_vec", [P, HALVED.stop - HALVED.start], f32)
        g12 = sb("gain12", [P, KD], f32)
        ident = sb("ident", [P, P], f32)
        ones = sb("ones", [P, P], f32)
        rotb = sb("rot_b", [P, P], f32r)
        roti = sb("rot_i", [P, P], f32r)
        idbig = sb("id_big", [P, P], bf16)
        tri = sb("tri", [P, P], bf16)
        mx = sb("row_max", [P, 2, 4], f32)
        nmx = sb("row_negmax", [P, 2, 4], f32)
        rs = sb("row_sum", [P, 2, 4], f32)
        rcp = sb("row_rcp", [P, 2, 4], f32)
        iw = sb("iw", [P, TB, 8], f32)
        m8 = sb("max8", [P, 3, 8], f32)
        bfb = sb("b_f", [P, 16], f32)
        sp = sb("softplus", [P, 6, 64], f32)
        rate = sb("decay_rate", [P, 3, LRU_T], f32)

        def zone(first_kib, spec):
            with ExitStack() as z:
                if first_kib:
                    z.enter_context(nc.sbuf_tensor(f"below_{spec[0][0]}", [P, first_kib * 256], f32))
                return [z.enter_context(nc.sbuf_tensor(*x)) for x in spec]

        QH, QL, KH, KL, VBH, VBL, bias, wk, MB, ROPE = zone(0, [
            ("q_hi", [P, 2, S], f32r), ("q_lo", [P, 2, S], f32r),
            ("k_hi", [P, 2, S], f32r), ("k_lo", [P, 2, S], f32r),
            ("vb_hi", [P, TB, P], f32r), ("vb_lo", [P, TB, P], f32r),
            ("bias", [P, 2, S], f32), ("index_score", [P, WK[4]], f32),
            ("top_mask", [P, NP], bf16), ("rope", [P, 4, S], f32)])
        VH, VL = zone(39, [("va_hi", [P, TB, S], f32r), ("va_lo", [P, TB, S], f32r)])
        YAH, YAL = zone(55, [("ya_hi", [P, 4, S], f32r), ("ya_lo", [P, 4, S], f32r)])
        GA, = zone(72, [("gate_a", [P, KD, S], f32)])
        XT, = zone(55, [("x_in", [P, KD, S], f32)])
        YBH, YBL = zone(39, [("yb_hi", [P, 4, S], f32r), ("yb_lo", [P, 4, S], f32r)])
        MGH, MGL = zone(0, [("merged_hi", [P, KD, S], f32r), ("merged_lo", [P, KD, S], f32r)])
        RES, = zone(72, [("res", [P, KD, S], f32)])
        YLH, YLL = zone(0, [("yl_hi", [P, LRU_T, S], f32r), ("yl_lo", [P, LRU_T, S], f32r)])
        LA, LX, LV, WAXH, WAXL = zone(48, [
            ("decay", [P, LRU_G, S], f32), ("gated_x", [P, LRU_G, S], f32),
            ("mult", [P, LRU_G, S], f32),
            ("wax_hi", [P, LRU_G, 2 * P], f32r), ("wax_lo", [P, LRU_G, 2 * P], f32r)])
        VFH, VFL, YFH, YFL, CQ, CK, upto = zone(16, [
            ("vf_hi", [P, TB, 2 * S], f32r), ("vf_lo", [P, TB, 2 * S], f32r),
            ("yf_hi", [P, KD, S], f32r), ("yf_lo", [P, KD, S], f32r),
            ("cum_q", [P, 4, S], bf16), ("cum_k", [P, 4, S], bf16),
            ("upto", [P, S], f32)])
        RES2, = zone(16, [("res_back", [P, KD, S], f32)])
        GB = tmp[:, 2:4, :]

        pj = [ctx.enter_context(nc.psum_tensor(f"acc{i}", [P, S], f32)) for i in range(2)]
        sbank = [ctx.enter_context(nc.psum_tensor(f"scores{i}", [P, S], f32)) for i in range(2)]
        tbank = [ctx.enter_context(nc.psum_tensor(f"probT{i}", [P, S], f32)) for i in range(2)]
        obank = [ctx.enter_context(nc.psum_tensor(f"out{i}", [P, S], f32)) for i in range(2)]
        tok = sbank + tbank

        x_loaded = [sem(f"x_loaded{i}") for i in range(4)]
        w_loaded = [sem(f"w_loaded{i}") for i in range(RAW)]
        const_loaded = sem("const_loaded")
        vec_loaded = sem("vec_loaded")
        upto_loaded = sem("upto_loaded")
        ext_written = sem("ext_written")
        bias_loaded = [sem(f"bias_loaded{i}") for i in range(2)]
        res_loaded = [sem(f"res_loaded{t}") for t in range(KD)]
        res_spilled = sem("res_spilled")
        res_back = sem("res_back_loaded")
        cum_moved = sem("cum_moved")
        out_stored = sem("out_stored")
        w_hi = sem("w_hi_ready")
        xn_hi = sem("xn_hi_ready")
        acc_act = sem("acc_act_read")
        v_hi = sem("v_hi_ready")
        rope_hi = sem("rope_hi_ready")
        index_relu = sem("index_relu_ready")
        exp_done = sem("exp_done")
        pt_hi = sem("probT_hi_ready")
        y_hi = sem("y_hi_ready")
        sq_ready = sem("square_ready")
        root_ready = sem("root_ready")
        mg_hi = sem("merged_hi_ready")
        xc_hi = sem("conv_hi_ready")
        decay_ready = sem("decay_ready")
        mult_ready = sem("mult_ready")
        ls_exp = sem("logsig_exp_ready")
        act_own = sem("act_own")
        ones_ready = sem("ones_ready")
        consts_ready = sem("consts_ready")
        w_lo = sem("w_lo_ready")
        xn_f32 = sem("xn_f32_ready")
        xn_lo = sem("xn_lo_ready")
        v_lo = sem("v_lo_ready")
        rope_sum = sem("rope_sum_ready")
        rope_lo = sem("rope_lo_ready")
        index_sum = sem("index_sum_ready")
        mx_ready = sem("row_max_ready")
        prob_ready = sem("prob_ready")
        pt_lo = sem("probT_lo_ready")
        o_taken = sem("out_taken")
        y_lo = sem("y_lo_ready")
        sq_used = sem("square_used")
        var_ready = sem("var_ready")
        diag_ready = sem("diag_ready")
        mg_sum = sem("merged_sum_ready")
        mg_lo = sem("merged_lo_ready")
        xc_ready = sem("conv_ready")
        xc_lo = sem("conv_lo_ready")
        mult_sq = sem("mult_squared_ready")
        ls_arg = sem("logsig_arg_ready")
        ls_ready = sem("logsig_ready")
        cum_split = sem("cum_split_ready")
        yl_f32 = sem("recurrence_y_ready")
        out_ready = sem("out_ready")
        dve_own = sem("dve_own")
        acc_free = [sem(f"acc_free{i}") for i in range(8)]
        gemm_steps = sem("gemm_steps")
        index_done = sem("index_scores_done")
        s_done = sem("scores_done")
        t_done = sem("transpose_done")
        o_done = sem("out_done")
        factor_ready = sem("factor_ready")
        bias_ready = sem("bias_ready")
        cum_ones = sem("cum_ones_ready")

        block = ctx.enter_context(nc.Block())

        def bank_of(name):
            return (pj + sbank + tbank + obank)[bank_use[name][0]]

        def freed(name):
            b, use = bank_use[name]
            return acc_free[b], use + 1

        rope_order = [name for name, _ in PLAN["accs"] if name[0].endswith("_rot")]
        rope_number = {(name[0][:-4], name[1]): i for i, name in enumerate(rope_order)}

        def cparts(negative, j):
            at = (3 * negative + j) * S // 2
            return prob[0:16, :, :].rearrange("h a b -> h (a b)")[:, at:at + S // 2].bitcast(bf16)

        def squared_decay(c):
            return tmp[:, 3, :] if c % 2 == 0 else decay2[:, :]

        @block.sync
        def _(sp):
            for i in range(4):
                sp.dma_start(XT[:, 2 * i:2 * i + 2, :], xT[:, 2 * i:2 * i + 2, :]).then_inc(x_loaded[i], 16)
            sp.wait_ge(x_loaded[2], 16)
            for u in range(NU):
                if u >= RAW:
                    sp.wait_ge(w_lo, u - RAW + 1)
                sp.dma_start(wraw[:, u % RAW, 0:widths[u]], wstream[u, :, 0:widths[u]])\
                  .then_inc(w_loaded[u % RAW], 16)
                if u == RAW - 1:
                    for dst, src in ((wk[:, 0:CON["upto"]], consts[:, 0:CON["upto"]]), (ROPE[:, :, :], rope),
                                     (bfb[:, :], b_f.to_broadcast([P, 16]))):
                        sp.dma_start(dst, src).then_inc(const_loaded, 16)

        @block.gpsimd
        def _(pool):
            pool.dma_start(rows_dram, bass.AP(rel_ext.tensor, 0, [[EXT, 8], [0, P], [1, EXT]])).then_inc(ext_written, 16)
            pool.wait_ge(ext_written, 16)
            for h in range(2 * A_PAIRS):
                if h >= 2:
                    pool.wait_ge(mx_ready, 3 * (h - 1))
                pool.dma_start(bias[:, h % 2, :], bass.AP(rows_dram.tensor, P * EXT * h + P - 1, [[EXT - 1, P], [1, S]]))\
                    .then_inc(bias_loaded[h % 2], 16)
                pool.wait_ge(bias_loaded[h % 2], 16 * (h // 2 + 1))
                pool.memset(bias[0:CH, h % 2, S - CH:S], -BIG).then_inc(bias_ready, 1)
            for t in range(KD):
                pool.wait_ge(mg_sum, t + 1)
                pool.dma_start(RES[:, t, :], xT[:, t, :]).then_inc(res_loaded[t], 16)
            for t in range(KD):
                pool.wait_ge(*freed(("lo", t)))
                pool.dma_start(res_dram[:, t, :], RES[:, t, :]).then_inc(res_spilled, 16)
            pool.wait_ge(xn_lo, 3 * KD)
            pool.wait_ge(res_spilled, 16 * KD)
            pool.memset(CQ[:, :, :], 1.0).then_inc(cum_ones, 1)
            pool.memset(CK[:, :, :], 1.0).then_inc(cum_ones, 1)
            pool.dma_start(upto[:, :], consts[:, CON["upto"]:NCON]).then_inc(upto_loaded, 16)
            pool.wait_ge(cum_ones, 2)
            pool.wait_ge(cum_split, 1)
            for g in range(4):
                for j in range(3):
                    pool.dma_start(CQ[32 * g + 3 + j:32 * g + 4 + j, :, :], cparts(0, j)[4 * g:4 * g + 4, :])\
                        .then_inc(cum_moved, 16)
                    pool.dma_start(CK[32 * g + j:32 * g + 1 + j, :, :], cparts(1, j)[4 * g:4 * g + 4, :])\
                        .then_inc(cum_moved, 16)
            pool.wait_ge(o_done, 2 * PAIRS)
            pool.dma_start(RES2[:, :, :], res_dram).then_inc(res_back, 16)
            pool.wait_ge(res_back, 16)
            for t in range(KD):
                pool.wait_ge(out_ready, t + 1)
                pool.dma_start(outT[:, t, :], RES2[:, t, :]).then_inc(out_stored, 16)
            pool.wait_ge(out_stored, 16 * KD)

        @block.tensor
        def _(pe):
            mm = pe.matmul

            def three(out, ah, al, bh, bl, start, stop):
                mm(out, ah, bh, start=start, stop=False)
                mm(out, ah, bl, start=False, stop=False)
                return mm(out, al, bh, start=False, stop=stop)

            def open_bank(name):
                b, use = bank_use[name]
                if use >= 1:
                    pe.wait_ge(acc_free[b], use)

            def weights(u, b):
                if slot[u] is None:
                    c = units[u][1] % LRU_G
                    return WAXH[:, c, b * P:b * P + P], WAXL[:, c, b * P:b * P + P]
                return whi[:, slot[u], b * P:b * P + P], wlo[:, slot[u], b * P:b * P + P]

            def close(name, i, last):
                u = blocks_of[name][i][0]
                if PLAN["last_use"][u] == (PLAN["order"][name], i) or i == len(blocks_of[name]) - 1:
                    last.then_inc(gemm_steps, 1)

            def gemm(name, rhs_hi, rhs_lo, first=0, end=None, ready=None):
                blocks = blocks_of[name]
                end = len(blocks) if end is None else end
                if first == 0:
                    open_bank(name)
                for i in range(first, end):
                    u, b = blocks[i]
                    if i == 0 or blocks[i - 1][0] != u:
                        pe.wait_ge(w_lo, u + 1)
                    if ready is not None:
                        pe.wait_ge(ready[0], ready[1] + i + 1)
                    wh, wl = weights(u, b)
                    last = three(bank_of(name)[:, :], wh, wl, rhs_hi[:, i, :], rhs_lo[:, i, :],
                                 i == 0, i == len(blocks) - 1)
                    close(name, i, last)

            def values(name, width=S):
                blocks = blocks_of[name]
                for i in range(KD):
                    u, half = blocks[i]
                    if half == 0:
                        pe.wait_ge(w_lo, u + 1)
                    if name[0] == "va":
                        pe.wait_ge(xn_lo, i + 1)
                    for t in range(TB):
                        if name == ("vf", 1) and i == 0:
                            pe.wait_ge(v_lo, TB + t + 1)
                        ts = slice(t * P, t * P + P)
                        ws = slice(half * S, half * S + S)
                        o = tok[t][:, :]
                        mm(o, XH[:, i, ts], whi[:, slot[u], ws], start=i == 0, stop=False)
                        mm(o, XH[:, i, ts], wlo[:, slot[u], ws], start=False, stop=False)
                        last = mm(o, XL[:, i, ts], whi[:, slot[u], ws], start=False, stop=i == KD - 1)
                    close(name, i, last)

            def small_values(name, n, xbase=None):
                open_bank(name)
                (u, _), = set((u, 0) for u, _ in blocks_of[name])
                pe.wait_ge(w_lo, u + 1)
                if xbase is not None:
                    pe.wait_ge(xn_lo, xbase + KD)
                for t in range(TB):
                    ts = slice(t * P, t * P + P)
                    o = bank_of(name)[:, t * n:t * n + n]
                    for k in range(KD):
                        wh, wl = (w[:, slot[u], k * n:k * n + n] for w in (whi, wlo))
                        mm(o, XH[:, k, ts], wh, start=k == 0, stop=False)
                        mm(o, XH[:, k, ts], wl, start=False, stop=False)
                        last = mm(o, XL[:, k, ts], wh, start=False, stop=k == KD - 1)
                last.then_inc(gemm_steps, 1)

            def rotate(name):
                src = (name[0][:-4], name[1])
                rot = roti if src[0] in ("ik", "iq") else rotb
                open_bank(name)
                pe.wait_ge(*freed(src))
                mm(bank_of(name)[:, :], rot[:, :], KH[:, 0, :], start=True, stop=False)
                mm(bank_of(name)[:, :], rot[:, :], KL[:, 0, :], start=False, stop=True).then_inc(gemm_steps, 1)

            def sum_squares(name, count, sums=1):
                open_bank(name)
                pe.wait_ge(sq_used, count)
                for j in range(sums):
                    for t in range(TB):
                        o = TB * j + t
                        last = mm(bank_of(name)[:, o:o + 1], sq[:, j, t * P:t * P + P], ones[:, 0:1],
                                  start=True, stop=True)
                last.then_inc(gemm_steps, 1)

            def broadcast(n, dst):
                pe.wait_ge(diag_ready, n)
                for t in range(TB):
                    ts = slice(t * P, t * P + P)
                    last = mm(dst[:, ts], ones[:, :], diag[:, ts], start=True, stop=True)
                last.then_inc(factor_ready, 1)

            def scores(n, part):
                pair, r0 = n // 2, HD * (n % 2)
                rows = slice(r0, r0 + HD)
                if part == 0 and n % 2 == 0:
                    if pair == 0:
                        pe.wait_ge(index_sum, 24)
                    if PAIR_B0 <= pair < PAIR_F0:
                        last_turned = ("kb", 0) if pair == PAIR_B0 else ("q", pair)
                        pe.wait_ge(rope_lo, rope_number[last_turned] + 1)
                    else:
                        pe.wait_ge(*freed(("q", pair)))
                        pe.wait_ge(*freed(("k", pair)))
                    if pair == PAIR_B0:
                        pe.wait_ge(consts_ready, 3)
                    if pair == PAIR_F0:
                        pe.wait_ge(cum_moved, 24 * 16)
                        pe.wait_ge(v_lo, 3 * TB)
                if n > 0 or part == 2:
                    prior = 3 * n + {0: 0, 1: -1, 2: 1}[part]
                    pe.wait_ge(mx_ready if (prior - 1) // 3 < 2 * A_PAIRS else exp_done, prior)
                for qb in S_PARTS[part]:
                    w = P * (qb + 1)
                    o = sbank[S_BANK[part]][:, S_COL[qb]:S_COL[qb] + w]
                    qs = slice(qb * P, qb * P + P)
                    qh, ql = QH[rows, pair % 2, qs], QL[rows, pair % 2, qs]
                    if PAIR_B0 <= pair < PAIR_F0:
                        kh, kl = KH[rows, 1, 0:w], KL[rows, 1, 0:w]
                    else:
                        kh, kl = KH[rows, pair % 2, 0:w], KL[rows, pair % 2, 0:w]
                    last = three(o, qh, ql, kh, kl, True, pair < PAIR_B0)
                    if PAIR_B0 <= pair < PAIR_F0:
                        last = mm(o, idbig[:, :], MB[:, OFF[qb]:OFF[qb] + w], start=False, stop=True)
                    elif pair >= PAIR_F0:
                        h = n - 2 * PAIR_F0
                        g = slice(32 * (h // 4), 32 * (h // 4) + 6)
                        mm(o, CQ[g, h % 4, qs], CK[g, h % 4, 0:w], start=False, stop=False)
                        last = mm(o[:, w - P:w], idbig[:, :], tri[:, :], start=False, stop=True)
                last.then_inc(s_done, 1)

            def transposes(n, part):
                if part == 0:
                    pe.wait_ge(prob_ready, n + 1)
                if n > 0 or part == 2:
                    pe.wait_ge(pt_lo, 3 * n + {0: 0, 1: -1, 2: 1}[part])
                col = 0
                for kb in T_PARTS[part]:
                    for qb in range(kb, TB):
                        last = pe.transpose(tbank[T_BANK[part]][:, col:col + P],
                                            prob[:, n % 2, OFF[qb] + kb * P:OFF[qb] + kb * P + P],
                                            ident[:, :])
                        col += P
                last.then_inc(t_done, 1)

            def outputs(n):
                pair = n // 2
                if n >= 2:
                    pe.wait_ge(o_taken, n - 1)
                for part in range(3):
                    pe.wait_ge(pt_lo, 3 * n + part + 1)
                    for kb in T_PARTS[part]:
                        w = S - kb * P
                        if pair < PAIR_B0:
                            vh, vl = (v[:, kb, P * pair:P * pair + P] for v in (VH, VL))
                        elif pair < PAIR_F0:
                            vh, vl = VBH[:, kb, :], VBL[:, kb, :]
                        else:
                            c = P * (pair - PAIR_F0)
                            vh, vl = VFH[:, kb, c:c + P], VFL[:, kb, c:c + P]
                        ps = slice(T_OFF[kb], T_OFF[kb] + w)
                        last = three(obank[n % 2][:, kb * P:S], vh, vl, PTH[:, ps], PTL[:, ps],
                                     kb == 0, kb == 2)
                last.then_inc(o_done, 1)

            def attention(n0, n1, fills, tail):
                for n in range(n0, n1 + 1):
                    names = list(fills[n] if n < n1 else tail)
                    if names and names[0][0].endswith("_rot"):
                        rotate(names.pop(0))
                    lead = names.pop(0) if names else None
                    for part, (k0, k1) in enumerate(((0, 2), (2, 5), (5, 8))):
                        if n > n0:
                            transposes(n - 1, part)
                        if n < n1:
                            scores(n, part)
                        if lead:
                            gemm(lead, XH, XL, k0, k1)
                    for name in names:
                        if name[0].endswith("_rot"):
                            rotate(name)
                        else:
                            gemm(name, XH, XL)
                    if n > n0:
                        outputs(n - 1)

            pe.wait_ge(ones_ready, 1)
            sum_squares(("ssq", 0), KD - 1)
            broadcast(1, obank[1])
            values(("va", 0))
            small_values(("vbiw", 0), 72)
            pe.wait_ge(consts_ready, 1)
            for name in (("ik", 0), ("iq", 0), ("iq", 1)):
                gemm(name, XH, XL)
                rotate((name[0] + "_rot", name[1]))
            pe.wait_ge(rope_lo, 3)
            pe.wait_ge(v_lo, TB)
            for m in range(24):
                qb, h = m // 8 + 1, m % 8
                rows = slice(32 * (h % 4), 32 * (h % 4) + 32)
                if m >= 4:
                    pe.wait_ge(index_relu, m - 3)
                w = P * (qb + 1)
                qs = slice(qb * P, qb * P + P)
                three(tok[m % 4][:, 0:w], QH[rows, h // 4, qs], QL[rows, h // 4, qs],
                      KH[rows, 1, 0:w], KL[rows, 1, 0:w], True, True).then_inc(index_done, 1)
            for t in range(KD):
                gemm(("za", t), XH, XL)
            gemm(("q", 0), XH, XL)
            gemm(("k", 0), XH, XL)
            attention(0, 2 * PAIR_F0, slots_of_heads(0, PAIR_F0), [("zb", 0), ("zb", 1)])
            for t in range(KD):
                if t >= 2:
                    gemm(("zb", t), XH, XL)
                for name, yh, yl, base in ((("pa", t), YAH, YAL, 0), (("pb", t), YBH, YBL, 4)):
                    if t == 0:
                        pe.wait_ge(y_lo, base + 4)
                    gemm(name, yh, yl)
            for t in range(KD):
                gemm(("wout", t), MGH, MGL, ready=(mg_lo, 0) if t == 0 else None)
            sum_squares(("ssq", 1), 3 * (KD - 1), 2)
            broadcast(2, obank[1])

            def gate_inputs(c):
                pe.wait_ge(xc_lo, c + 1)
                for name in (("r", c), ("i", c)):
                    open_bank(name)
                    (u, b), = blocks_of[name]
                    pe.wait_ge(w_lo, u + 1)
                    wh, wl = weights(u, b)
                    cs = slice((c % 2) * S, (c % 2) * S + S)
                    last = three(bank_of(name)[:, :], wh, wl, PTH[:, cs], PTL[:, cs], True, True)
                    close(name, 0, last)

            gemm(("xb", 0), XH, XL, ready=(xn_lo, KD))
            for c in range(LRU_T):
                if c + 1 < LRU_T:
                    gemm(("xb", c + 1), XH, XL)
                gate_inputs(c)
                if c >= 1:
                    gemm(("gl", c - 1), XH, XL)
            gemm(("gl", LRU_T - 1), XH, XL)
            pe.wait_ge(*freed(("gl", LRU_T - 2)))
            broadcast(3, obank[0])
            for t in range(KD):
                gemm(("lo", t), YLH, YLL, ready=(y_lo, 8) if t == 0 else None)
            sum_squares(("ssq", 2), 4 * (KD - 1))
            broadcast(4, obank[1])

            small_values(("f", 0), 16, 2 * KD)
            values(("vf", 0))
            open_bank(("cum", 0))
            pe.wait_ge(ls_ready, 2)
            pe.wait_ge(upto_loaded, 16)
            for kb in range(TB):
                last = mm(bank_of(("cum", 0))[0:16, kb * P:S], sp[:, 5, kb * 16:kb * 16 + 16],
                          upto[:, 0:S - kb * P], start=kb == 0, stop=kb == TB - 1)
            last.then_inc(gemm_steps, 1)
            values(("vf", 1))
            gemm(("q", PAIR_F0), XH, XL)
            gemm(("k", PAIR_F0), XH, XL)
            attention(2 * PAIR_F0, 2 * PAIRS, slots_of_heads(PAIR_F0, PAIRS), [])
            for t in range(KD):
                gemm(("fo", t), YFH, YFL, ready=(y_lo, 8 + LRU_T) if t == 0 else None)
            sum_squares(("ssq", 3), 5 * (KD - 1))
            broadcast(5, obank[1])

        act_kinds = ("vbiw", "ik", "iq", "kb", "q", "k", "g", "gl")
        act_order = [name for name, _ in PLAN["accs"] if name[0] in act_kinds]
        act_read = {name: i + 1 for i, name in enumerate(act_order)}

        def rope_parts(name):
            kind, i = name
            if kind == "ik":
                return KH[:, 1, :], KL[:, 1, :]
            if kind == "kb":
                return KH[:, 1, :], KL[:, 1, :]
            return QH[:, i % 2, :], QL[:, i % 2, :]

        def vcol(tensor, name, i):
            return tensor[:, VEC[name] + i:VEC[name] + i + 1]

        def halved(name, i):
            c = VEC[name] - HALVED.start + i
            return hvec[:, c:c + 1]

        def values_of(name):
            if name[0] == "va":
                return VH, VL, slice(0, S)
            return VFH, VFL, slice(name[1] * S, name[1] * S + S)

        def gated(n):
            pair = n // 2
            rows = slice(HD * (n % 2), HD * (n % 2) + HD)
            if pair < PAIR_B0:
                return rows, YAH[:, pair, :], YAL[:, pair, :]
            if pair < PAIR_F0:
                return rows, YBH[:, pair - PAIR_B0, :], YBL[:, pair - PAIR_B0, :]
            return rows, YFH[:, pair - PAIR_F0, :], YFL[:, pair - PAIR_F0, :]

        class Refill:

            def __init__(self, split):
                self.next, self.split = 0, split

            def need(self, name):
                for u, _ in blocks_of[name]:
                    self.upto(u)

            def upto(self, u):
                while self.next <= u:
                    self.split(self.next)
                    self.next += 1

            def after(self, name):
                while self.next < NU and unit_free.get(before.get(self.next), 0) <= acc_done[name]:
                    self.split(self.next)
                    self.next += 1

        @block.scalar
        def _(act):
            act.dma_start(vec[:, :], vecs).then_inc(vec_loaded, 16)
            act.dma_start(ident[:, :], consts[:, 0:P]).then_inc(vec_loaded, 16)
            A = act.activation

            def split(u):
                act.wait_ge(w_loaded[u % RAW], 16 * (u // RAW + 1))
                if u in before:
                    act.wait_ge(gemm_steps, unit_free[before[u]])
                dst = WAXH[:, units[u][1] % LRU_G, :] if slot[u] is None else whi[:, slot[u], 0:widths[u]]
                A(dst, wraw[:, u % RAW, 0:widths[u]], ACT.Copy).then_inc(w_hi, 1)

            refill = Refill(split)

            def evacuate(name):
                kind, i = name
                refill.need(name)
                act.wait_ge(gemm_steps, acc_done[name])
                if kind not in ("va", "vf"):
                    ps = bank_of(name)
                if kind in ("va", "vf"):
                    vh, _, cols = values_of(name)
                    for t in range(TB):
                        A(vh[:, t, cols], tok[t][:, :], ACT.Copy).then_inc(v_hi, 1)
                elif kind == "vbiw":
                    src = ps[:, 0:72 * TB].rearrange("p (t n) -> p t n", n=72)[:, :, 0:HD]
                    A(VBH[:, :, 0:HD], src, ACT.Copy)
                    A(VBH[:, :, HD:P], src, ACT.Copy).then_inc(acc_act, 1)
                elif name in rope_number:
                    A(KH[:, 0, :], ps[:, :], ACT.Copy).then_inc(acc_act, 1)
                elif kind in ("q", "k"):
                    A((QH if kind == "q" else KH)[:, i % 2, :], ps[:, :], ACT.Copy,
                      scale=HD ** -0.5 if kind == "q" else 1.0).then_inc(acc_act, 1)
                elif kind in ("g", "gl"):
                    if kind == "g" and i >= 2:
                        act.wait_ge(o_taken, 2 * i - 2)
                    if kind == "gl" and i >= 2:
                        act.wait_ge(yl_f32, i - 1)
                    A(sg[:, i % 2, :], ps[:, :], ACT.Tanh, scale=0.5).then_inc(acc_act, 1)
                elif kind == "za":
                    A(GA[:, i, :], ps[:, :], ACT.Tanh, scale=0.5, bias=halved("bma", i))\
                        .then_inc(freed(name)[0], 1)
                elif kind == "zb":
                    if i == 0:
                        act.wait_ge(rope_lo, 8)
                    if i >= 2:
                        act.wait_ge(mg_sum, i - 1)
                    A(GB[:, i % 2, :], ps[:, :], ACT.Tanh, scale=0.5, bias=halved("bmb", i))\
                        .then_inc(freed(name)[0], 1)
                elif kind == "xb":
                    if i >= 2:
                        act.wait_ge(xc_ready, i - 1)
                        act.wait_ge(mult_sq, i - 1)
                        act.wait_ge(xc_hi, i - 1)
                    A(prob[:, i % 2, 3:3 + S], ps[:, :], ACT.Copy)
                    A(prob[:, i % 2, 640:640 + S], ps[:, :], ACT.Identity, scale=vcol(vec, "conv_w", 4 * i + 3),
                      bias=vcol(vec, "conv_b", i)).then_inc(freed(name)[0], 1)
                elif kind == "r":
                    if i >= 1:
                        act.wait_ge(decay_ready, i)
                    A(tmp[:, 0, :], ps[:, :], ACT.Tanh, scale=0.5, bias=halved("ba", i))\
                        .then_inc(freed(name)[0], 1)
                elif kind == "i":
                    if i >= 2:
                        act.wait_ge(mult_sq, i - 1)
                    A(tmp[:, 1 + i % 2, :], ps[:, :], ACT.Tanh, scale=0.5, bias=halved("bx", i))\
                        .then_inc(freed(name)[0], 1)
                if kind != "r" and kind != "i":
                    refill.after(name)

            def rotated(name):
                r = rope_number[name]
                act.wait_ge(rope_sum, r + 1)
                A(rope_parts(name)[0], tmp[:, 2, :], ACT.Copy,
                  scale=HD ** -0.5 if name[0] == "q" else 1.0).then_inc(rope_hi, 1)

            def exps(n, part):
                act.wait_ge(mx_ready, 3 * n + part + 1)
                for qb in S_PARTS[part]:
                    w = P * (qb + 1)
                    p = prob[:, n % 2, OFF[qb]:OFF[qb] + w]
                    c = M_COL[qb]
                    src = p if n < 2 * A_PAIRS else sbank[S_BANK[part]][:, S_COL[qb]:S_COL[qb] + w]
                    last = A(p, src, ACT.Exp, bias=nmx[:, n % 2, c:c + 1],
                             accum_out=rs[:, n % 2, c:c + 1])
                last.then_inc(exp_done, 1)

            def transposed(n, part):
                act.wait_ge(t_done, 3 * n + part + 1)
                w = sum(S - kb * P for kb in T_PARTS[part])
                c = T_OFF[T_PARTS[part][0]]
                A(PTH[:, c:c + w], tbank[T_BANK[part]][:, 0:w], ACT.Copy).then_inc(pt_hi, 1)

            def y_parts(n):
                if n % 2 == 1:
                    act.wait_ge(o_taken, n + 1)
                    A(gated(n)[1], yt[:, (n // 2) % 2, :], ACT.Copy).then_inc(y_hi, 1)

            def attention(n0, n1, fills, tail):
                for n in range(n0, n1 + 1):
                    names = list(fills[n] if n < n1 else tail)
                    turned = names.pop(0) if names and names[0][0].endswith("_rot") else None
                    if names:
                        refill.need(names[0])
                    for part in range(3):
                        if n > n0:
                            transposed(n - 1, part)
                        if n < n1:
                            exps(n, part)
                        if part == 0 and n >= n0 + 2:
                            y_parts(n - 2)
                        if part == 0 and turned:
                            rotated((turned[0][:-4], turned[1]))
                    for name in names:
                        if name[0].endswith("_rot"):
                            rotated((name[0][:-4], name[1]))
                        else:
                            evacuate(name)
                y_parts(n1 - 1)

            squares = [0]

            def square(src, t, scale=1.0, into=None):
                if t == 0:
                    A(sq[:, into or 0, :], src, ACT.Square, scale=scale).then_inc(sq_ready, 1)
                else:
                    k = squares[0]
                    A(yt[:, k % 2, :], src, ACT.Square, scale=scale).then_inc(sq_ready, 1)
                    squares[0] += 1

            def normalised(r):
                for t in range(KD):
                    act.wait_ge(xn_f32, KD * r + t + 1)
                    A(XH[:, t, :], tmp[:, 2 + t % 2, :], ACT.Copy).then_inc(xn_hi, 1)

            def roots(norm, n):
                A(root[:, norm, 0:n], mean[:, 0:n], ACT.Sqrt).then_inc(root_ready, 1)

            for t in range(KD):
                if t % 2 == 0:
                    act.wait_ge(x_loaded[t // 2], 16)
                if t >= 3:
                    act.wait_ge(sq_used, t - 2)
                square(XT[:, t, :], t)
            refill.upto(RAW - 1)
            act.wait_ge(var_ready, 1)
            roots(0, TB)
            normalised(0)
            evacuate(("va", 0))
            evacuate(("vbiw", 0))
            for name in (("ik", 0), ("iq", 0), ("iq", 1)):
                evacuate(name)
                rotated(name)
            for m in range(24):
                act.wait_ge(index_done, m + 1)
                if m >= 2:
                    act.wait_ge(index_sum, m - 1)
                w = P * (m // 8 + 2)
                A(prob[:, m % 2, 0:w], tok[m % 4][:, 0:w], ACT.Relu).then_inc(index_relu, 1)
            act.wait_ge(consts_ready, 1)
            for t in range(KD):
                evacuate(("za", t))
            evacuate(("q", 0))
            evacuate(("k", 0))
            act.wait_ge(ls_arg, 1)
            A(sp[:, 1, 0:LRU_T], sp[:, 1, 0:LRU_T], ACT.Exp).then_inc(ls_exp, 1)
            attention(0, 2 * PAIR_F0, slots_of_heads(0, PAIR_F0), [("zb", 0), ("zb", 1)])

            def merged(t):
                act.wait_ge(mg_sum, t + 1)
                A(MGH[:, t, :], yt[:, t % 2, :], ACT.Copy, scale=0.5).then_inc(mg_hi, 1)

            for t in range(KD):
                if t >= 2:
                    evacuate(("zb", t))
                refill.need(("pb", t))
                merged(t)
                refill.after(("pb", t))

            def residual_squares(kind, used, finals=False):
                for t in range(KD):
                    refill.need((kind, t))
                    act.wait_ge(*freed((kind, t)))
                    src = (RES if kind != "fo" else RES2)[:, t, :]
                    if finals:
                        if t > 1:
                            act.wait_ge(sq_used, used + 2 * (t - 1))
                        if t == 0:
                            A(sq[:, 0, :], src, ACT.Square).then_inc(sq_ready, 1)
                            A(sq[:, 1, :], src, ACT.Square, scale=vcol(vec, "final1", t)).then_inc(sq_ready, 1)
                        else:
                            A(yt[:, 0, :], src, ACT.Square).then_inc(sq_ready, 1)
                            A(yt[:, 1, :], src, ACT.Square, scale=vcol(vec, "final1", t)).then_inc(sq_ready, 1)
                    else:
                        if t >= 3:
                            act.wait_ge(sq_used, used + t - 2)
                        square(src, t)
                    refill.after((kind, t))

            residual_squares("wout", KD - 1, finals=True)
            act.wait_ge(var_ready, 2)
            roots(1, 2 * TB)
            normalised(1)

            def conv_parts(c):
                act.wait_ge(xc_ready, c + 1)
                A(PTH[:, (c % 2) * S:(c % 2) * S + S], prob[:, c % 2, 640:640 + S], ACT.Copy).then_inc(xc_hi, 1)

            def decays(c):
                j = c % LRU_G
                evacuate(("r", c))
                evacuate(("i", c))
                if c >= LRU_G:
                    act.wait_ge(yl_f32, c - LRU_G + 1)
                act.wait_ge(*freed(("r", c)))
                for dst, func, k in ((LA[:, j, :], ACT.Exp, 0), (squared_decay(c), ACT.Exp, 1),
                                     (LV[:, j, :], ACT.Tanh, 2)):
                    last = A(dst, tmp[:, 0, :], func, scale=rate[:, k, c:c + 1], bias=rate[:, k, c:c + 1])
                last.then_inc(decay_ready, 1)

            def yl_parts(c):
                act.wait_ge(yl_f32, c + 1)
                A(YLH[:, c, :], yt[:, c % 2, :], ACT.Copy).then_inc(y_hi, 1)

            evacuate(("xb", 0))
            conv_parts(0)
            for c in range(LRU_T):
                if c + 1 < LRU_T:
                    evacuate(("xb", c + 1))
                decays(c)
                if c % LRU_G == LRU_G - 1:
                    act.wait_ge(mult_sq, c + 1)
                    A(LV[:, :, :], LV[:, :, :], ACT.Sqrt, scale=0.25).then_inc(mult_ready, 1)
                if c + 1 < LRU_T:
                    conv_parts(c + 1)
                refill.after(("i", c))
                if c >= 1:
                    evacuate(("gl", c - 1))
                if c % LRU_G == LRU_G - 1:
                    yl_parts(c - 2)
                    yl_parts(c - 1)
                elif c % LRU_G == 0 and c > 0:
                    yl_parts(c - 1)
            evacuate(("gl", LRU_T - 1))
            yl_parts(LRU_T - 1)
            residual_squares("lo", 3 * (KD - 1))
            act.wait_ge(var_ready, 3)
            roots(2, TB)
            normalised(2)

            refill.need(("f", 0))
            act.wait_ge(ls_arg, 2)
            A(sp[:, 1, :], sp[:, 1, :], ACT.Exp).then_inc(ls_exp, 1)
            refill.after(("f", 0))
            evacuate(("vf", 0))
            evacuate(("vf", 1))
            evacuate(("q", PAIR_F0))
            evacuate(("k", PAIR_F0))
            attention(2 * PAIR_F0, 2 * PAIRS, slots_of_heads(PAIR_F0, PAIRS), [])
            residual_squares("fo", 4 * (KD - 1))
            act.wait_ge(var_ready, 4)
            roots(3, TB)

        @block.vector
        def _(dve):
            T = dve.tensor_tensor
            TS = dve.tensor_scalar
            STT = dve.scalar_tensor_tensor
            own = [0]

            def step(ins):
                own[0] += 1
                ins.then_inc(dve_own, 1)

            def settle():
                dve.wait_ge(dve_own, own[0])

            def split(u):
                dve.wait_ge(w_hi, u + 1)
                raw = wraw[:, u % RAW, 0:widths[u]]
                c = units[u][1] % LRU_G
                hi, lo = ((WAXH[:, c, :], WAXL[:, c, :]) if slot[u] is None else
                          (whi[:, slot[u], 0:widths[u]], wlo[:, slot[u], 0:widths[u]]))
                T(lo, raw, hi, ALU.subtract).then_inc(w_lo, 1)

            refill = Refill(split)

            def low(dst, src, hi, scale=1.0):
                if scale == 1.0:
                    return T(dst, src, hi, ALU.subtract)
                return STT(dst, src, scale, hi, ALU.mult, ALU.subtract)

            def evacuate(name):
                kind, i = name
                refill.need(name)
                if name in act_read:
                    dve.wait_ge(acc_act, act_read[name])
                elif kind not in ("va", "vf"):
                    dve.wait_ge(gemm_steps, acc_done[name])
                if kind in ("va", "vf"):
                    vh, vl, cols = values_of(name)
                    first = 0 if kind == "va" else TB * (1 + i)
                    for t in range(TB):
                        dve.wait_ge(v_hi, first + t + 1)
                        low(vl[:, t, cols], tok[t][:, :], vh[:, t, cols]).then_inc(v_lo, 1)
                    refill.after(name)
                    return
                ps, free = bank_of(name), freed(name)[0]
                if kind == "vbiw":
                    both = ps[:, 0:72 * TB].rearrange("p (t n) -> p t n", n=72)
                    low(VBL[:, :, 0:HD], both[:, :, 0:HD], VBH[:, :, 0:HD])
                    low(VBL[:, :, HD:P], both[:, :, 0:HD], VBH[:, :, HD:P])
                    TS(iw[:, :, :], both[:, :, HD:72], 8 ** -0.5 * 32 ** -0.5, None, ALU.mult).then_inc(free, 1)
                elif name in rope_number:
                    cos = ROPE[:, 2 if kind in ("ik", "iq") else 0, :]
                    low(KL[:, 0, :], ps[:, :], KH[:, 0, :])
                    T(tmp[:, 0, :], ps[:, :], cos, ALU.mult).then_inc(free, 1)
                elif kind in ("q", "k"):
                    hi, lo = (QH, QL) if kind == "q" else (KH, KL)
                    low(lo[:, i % 2, :], ps[:, :], hi[:, i % 2, :],
                        HD ** -0.5 if kind == "q" else 1.0).then_inc(free, 1)
                elif kind in ("g", "gl"):
                    STT(sg[:, i % 2, :], sg[:, i % 2, :], 1.0, ps[:, :], ALU.add, ALU.mult).then_inc(free, 1)
                refill.after(name)

            def rotated(name):
                rot = (name[0] + "_rot", name[1])
                sin = ROPE[:, 3 if name[0] in ("ik", "iq") else 1, :]
                dve.wait_ge(gemm_steps, acc_done[rot])
                T(tmp[:, 1, :], bank_of(rot)[:, :], sin, ALU.mult).then_inc(freed(rot)[0], 1)
                dve.wait_ge(*freed(rot))
                dve.wait_ge(*freed(name))
                r = rope_number[name]
                T(tmp[:, 2, :], tmp[:, 0, :], tmp[:, 1, :], ALU.add).then_inc(rope_sum, 1)
                dve.wait_ge(rope_sum, r + 1)
                dve.wait_ge(rope_hi, r + 1)
                hi, lo = rope_parts(name)
                low(lo, tmp[:, 2, :], hi, HD ** -0.5 if name[0] == "q" else 1.0).then_inc(rope_lo, 1)
                refill.after(rot)

            def row_max(n, part):
                dve.wait_ge(s_done, 3 * n + part + 1)
                if n < 2 * A_PAIRS and part == 0:
                    dve.wait_ge(bias_ready, n + 1)
                for qb in S_PARTS[part]:
                    w, c = P * (qb + 1), M_COL[qb]
                    src = sbank[S_BANK[part]][:, S_COL[qb]:S_COL[qb] + w]
                    m = mx[:, n % 2, c:c + 1]
                    if n < 2 * A_PAIRS:
                        step(dve.tensor_tensor_reduce(
                            out=prob[:, n % 2, OFF[qb]:OFF[qb] + w], in0=src,
                            in1=bias[:, n % 2, S - w:S], scale=1.0, scalar=-3e38,
                            op0=ALU.add, op1=ALU.max, accum_out=m))
                    else:
                        step(dve.tensor_reduce(m, src, AX, ALU.max))
                settle()
                c0, k = M_COL[S_PARTS[part][0]], len(S_PARTS[part])
                TS(nmx[:, n % 2, c0:c0 + k], mx[:, n % 2, c0:c0 + k], -1.0, None, ALU.mult)\
                    .then_inc(mx_ready, 1)

            def probabilities(n):
                dve.wait_ge(exp_done, 3 * n + 3)
                step(dve.reciprocal(rcp[:, n % 2, :], rs[:, n % 2, :]))
                settle()
                for qb in range(TB):
                    p = prob[:, n % 2, OFF[qb]:OFF[qb] + P * (qb + 1)]
                    c = M_COL[qb]
                    last = TS(p, p, rcp[:, n % 2, c:c + 1], None, ALU.mult)
                last.then_inc(prob_ready, 1)

            def transposed(n, part):
                dve.wait_ge(pt_hi, 3 * n + part + 1)
                w = sum(S - kb * P for kb in T_PARTS[part])
                c = T_OFF[T_PARTS[part][0]]
                low(PTL[:, c:c + w], tbank[T_BANK[part]][:, 0:w], PTH[:, c:c + w]).then_inc(pt_lo, 1)

            tiles_y = [0]

            def take_output(n):
                rows, hi, lo = gated(n)
                dve.wait_ge(o_done, n + 1)
                pair = n // 2
                dve.wait_ge(*freed(("g", pair)))
                STT(yt[rows, pair % 2, :], obank[n % 2][rows, :], 0.5, sg[rows, pair % 2, :],
                    ALU.mult, ALU.mult).then_inc(o_taken, 1)

            def y_parts(n):
                if n % 2 == 1:
                    _, hi, lo = gated(n)
                    tiles_y[0] += 1
                    dve.wait_ge(o_taken, n + 1)
                    dve.wait_ge(y_hi, tiles_y[0])
                    low(lo, yt[:, (n // 2) % 2, :], hi).then_inc(y_lo, 1)

            def attention(n0, n1, fills, tail, extra):
                for n in range(n0, n1 + 1):
                    names = list(fills[n] if n < n1 else tail)
                    turned = names.pop(0) if names and names[0][0].endswith("_rot") else None
                    if names:
                        refill.need(names[0])
                    for part in range(3):
                        if n < n1:
                            row_max(n, part)
                        if n > n0:
                            transposed(n - 1, part)
                        if part == 0 and n >= n0 + 2:
                            take_output(n - 2)
                        if part == 1 and n >= n0 + 2:
                            y_parts(n - 2)
                        if part == 0 and turned:
                            rotated((turned[0][:-4], turned[1]))
                    if n < n1:
                        probabilities(n)
                    extra(n)
                    for name in names:
                        if name[0].endswith("_rot"):
                            rotated((name[0][:-4], name[1]))
                        else:
                            evacuate(name)
                take_output(n1 - 1)
                y_parts(n1 - 1)

            def one_square(t, used, buf, total=0):
                dve.wait_ge(sq_used, used)
                T(sq[:, total, :], sq[:, total, :], yt[:, buf, :], ALU.add).then_inc(sq_used, 1)

            def normalise(r, src, gain, root):
                def full(t):
                    if t >= 2:
                        dve.wait_ge(xn_lo, KD * r + t - 1)
                    STT(tmp[:, 2 + t % 2, :], src[:, t, :], gain(t), root, ALU.mult, ALU.mult)\
                        .then_inc(xn_f32, 1)

                def part(t):
                    dve.wait_ge(xn_hi, KD * r + t + 1)
                    low(XL[:, t, :], tmp[:, 2 + t % 2, :], XH[:, t, :]).then_inc(xn_lo, 1)

                full(0)
                for t in range(1, KD):
                    full(t)
                    part(t - 1)
                part(KD - 1)

            def log_sigmoid(src, n, dst, count):
                u, s, s2, p = (sp[:, j, 0:n] for j in (1, 2, 3, 4))
                STT(u, src, -1.0, src, ALU.mult, ALU.min).then_inc(ls_arg, 1)
                dve.wait_ge(ls_exp, count)
                step(TS(s, u, 2.0, None, ALU.add))
                settle()
                step(dve.reciprocal(s, s))
                settle()
                step(T(s, s, u, ALU.mult))
                settle()
                step(T(s2, s, s, ALU.mult))
                settle()
                step(TS(p, s2, 1.0 / 17, None, ALU.mult))
                settle()
                for k in range(7, 0, -1):
                    step(STT(p, p, 1.0 / (2 * k + 1), s2, ALU.add, ALU.mult))
                    settle()
                step(STT(p, p, 1.0, s, ALU.add, ALU.mult))
                settle()
                step(TS(s, src, 0.0, None, ALU.min))
                settle()
                STT(dst, p, -2.0, s, ALU.mult, ALU.add).then_inc(ls_ready, 1)

            dve.memset(ones[:, :], 1.0).then_inc(ones_ready, 1)

            for t in range(1, KD):
                dve.wait_ge(sq_ready, t + 1)
                one_square(t, t - 1, (t - 1) % 2)

            def row_factors(norm, name):
                dve.wait_ge(gemm_steps, acc_done[name])
                TS(mean[:, 0:TB], bank_of(name)[:, 0:TB], 1.0 / D, EPS, ALU.mult, ALU.add)\
                    .then_inc(freed(name)[0], 1)
                dve.wait_ge(*freed(name))
                dve.reciprocal(mean[:, 0:TB], mean[:, 0:TB]).then_inc(var_ready, 1)
                dve.wait_ge(root_ready, norm + 1)
                diagonals(root[:, norm, 0:TB])

            def diagonals(factors):
                for t in range(TB):
                    last = TS(diag[:, t * P:t * P + P], ident[:, :], factors[:, t:t + 1], None, ALU.mult)
                last.then_inc(diag_ready, 1)

            dve.wait_ge(vec_loaded, 32)
            row_factors(0, ("ssq", 0))
            refill.upto(RAW - 1)
            dve.wait_ge(factor_ready, 1)
            normalise(0, XT, lambda t: vcol(vec, "gain1", t), obank[1][:, :])

            dve.wait_ge(const_loaded, 48)
            con = lambda name, n=P: wk[:, CON[name]:CON[name] + n]
            dve.tensor_copy(rotb[:, :], con("rot_b"))
            dve.tensor_copy(roti[:, :], con("rot_i"))
            dve.tensor_copy(tri[:, :], con("tri"))
            dve.tensor_copy(MB[:, 0:P], con("half"))
            TS(idbig[:, :], ident[:, :], BIG, None, ALU.mult)
            step(T(g12[:, :], vec[:, VEC["final1"]:VEC["final1"] + KD],
                   vec[:, VEC["gain2"]:VEC["gain2"] + KD], ALU.mult))
            TS(hvec[:, :], vec[:, HALVED], 0.5, None, ALU.mult).then_inc(consts_ready, 1)
            dve.wait_ge(consts_ready, 1)
            evacuate(("va", 0))
            evacuate(("vbiw", 0))
            for name in (("ik", 0), ("iq", 0), ("iq", 1)):
                evacuate(name)
                rotated(name)
            for m in range(24):
                j, h = m // 8 + 1, m % 8
                w = P * (j + 1)
                dve.wait_ge(index_relu, m + 1)
                src, dst = prob[:, m % 2, 0:w], wk[:, WK[j]:WK[j] + w]
                if h == 0:
                    TS(dst, src, iw[:, j, 0:1], None, ALU.mult).then_inc(index_sum, 1)
                else:
                    dve.wait_ge(index_sum, m)
                    STT(dst, src, iw[:, j, h:h + 1], dst, ALU.mult, ALU.add).then_inc(index_sum, 1)
            dve.wait_ge(index_sum, 24)
            for j in (1, 2, 3):
                step(dve.memset(wk[0:CH, WK[j + 1] - CH:WK[j + 1]], NOT_ADMITTED))

            def top_round():
                settle()
                for j in (1, 2, 3):
                    step(dve.max(m8[:, j - 1, :], wk[:, WK[j]:WK[j + 1]]))
                for j in (1, 2, 3):
                    dve.wait_ge(dve_own, own[0] - 2)
                    row = wk[:, WK[j]:WK[j + 1]]
                    step(dve.match_replace(out=row, in_to_replace=m8[:, j - 1, :], in_values=row,
                                           imm_value=TAKEN))

            rounds = TOPK // 8
            for t in range(KD):
                top_round()
                refill.need(("za", t))
                refill.after(("za", t))
            rounds -= KD
            evacuate(("q", 0))
            evacuate(("k", 0))
            left = [rounds]

            def select(n):
                for _ in range(2 if n < 2 else 1):
                    if left[0] > 0:
                        top_round()
                        left[0] -= 1
                        if left[0] == 0:
                            settle()
                            TS(MB[:, P:NP], wk[:, :], TAKEN, -1.0, ALU.is_equal, ALU.add)\
                                .then_inc(consts_ready, 1)

            log_sigmoid(vec[:, VEC["ap"]:VEC["ap"] + LRU_T], LRU_T, sp[:, 5, 0:LRU_T], 1)
            dve.wait_ge(ls_ready, 1)
            for j, factor in enumerate((4.0, 8.0, -4.0)):
                last = TS(rate[:, j, :], sp[:, 5, 0:LRU_T], factor, None, ALU.mult)
            last.then_inc(consts_ready, 1)
            attention(0, 2 * PAIR_F0, slots_of_heads(0, PAIR_F0), [("zb", 0), ("zb", 1)], select)

            for t in range(KD):
                if t >= 2:
                    refill.need(("zb", t))
                    refill.after(("zb", t))
                refill.need(("pb", t))
                for name, gate, m in ((("pa", t), GA[:, t, :], 0), (("pb", t), GB[:, t % 2, :], 1)):
                    dve.wait_ge(gemm_steps, acc_done[name])
                    if m == 1:
                        dve.wait_ge(*freed(("zb", t)))
                    else:
                        dve.wait_ge(*freed(("za", t)))
                    STT(tmp[:, m, :], gate, 1.0, bank_of(name)[:, :], ALU.add, ALU.mult)\
                        .then_inc(freed(name)[0], 1)
                dve.wait_ge(*freed(("pa", t)))
                dve.wait_ge(*freed(("pb", t)))
                T(yt[:, t % 2, :], tmp[:, 0, :], tmp[:, 1, :], ALU.add).then_inc(mg_sum, 1)
                dve.wait_ge(mg_sum, t + 1)
                dve.wait_ge(mg_hi, t + 1)
                low(MGL[:, t, :], yt[:, t % 2, :], MGH[:, t, :], 0.5).then_inc(mg_lo, 1)
                refill.after(("pb", t))

            def residual(kind, res, ready, used, buf, double=False):
                def squares(t):
                    if double:
                        if t > 0:
                            dve.wait_ge(sq_ready, ready + 2 * t + 1)
                            one_square(t, used + 2 * t - 2, 0, 0)
                            dve.wait_ge(sq_ready, ready + 2 * t + 2)
                            one_square(t, used + 2 * t - 1, 1, 1)
                    else:
                        dve.wait_ge(sq_ready, ready + t + 1)
                        if t > 0:
                            one_square(t, used + t - 1, (buf + t - 1) % 2)

                for t in range(KD):
                    name = (kind, t)
                    refill.need(name)
                    if kind == "wout":
                        dve.wait_ge(res_loaded[t], 16)
                    elif kind == "lo":
                        step(STT(res[:, t, :], res[:, t, :], vcol(vec, "final1", t), obank[0][:, :],
                                 ALU.mult, ALU.mult))
                        settle()
                    dve.wait_ge(gemm_steps, acc_done[name])
                    T(res[:, t, :], bank_of(name)[:, :], res[:, t, :], ALU.add).then_inc(freed(name)[0], 1)
                    squares(t)
                    refill.after(name)

            residual("wout", RES, KD, KD - 1, 0, double=True)
            one = ("ssq", 1)
            dve.wait_ge(gemm_steps, acc_done[one])
            step(TS(mean[:, 0:TB], bank_of(one)[:, 0:TB], 1.0 / D, EPS, ALU.mult, ALU.add))
            settle()
            step(TS(mean[:, TB:2 * TB], mean[:, 0:TB], EPS, None, ALU.mult))
            settle()
            STT(mean[:, TB:2 * TB], bank_of(one)[:, TB:2 * TB], 1.0 / D, mean[:, TB:2 * TB],
                ALU.mult, ALU.add).then_inc(freed(one)[0], 1)
            dve.wait_ge(*freed(one))
            dve.reciprocal(mean[:, :], mean[:, :]).then_inc(var_ready, 1)
            dve.wait_ge(root_ready, 2)
            diagonals(root[:, 1, TB:2 * TB])
            dve.wait_ge(factor_ready, 2)
            normalise(1, RES, lambda t: g12[:, t:t + 1], obank[1][:, :])

            step(dve.memset(prob[:, :, 0:3], 0.0))
            settle()

            def convolve(c):
                xb, xc = prob[:, c % 2, :], prob[:, c % 2, 640:640 + S]
                refill.need(("xb", c))
                dve.wait_ge(*freed(("xb", c)))
                if c >= 2:
                    dve.wait_ge(mult_sq, c - 1)
                tap = lambda i: vcol(vec, "conv_w", 4 * c + i)
                for i in (2, 1):
                    step(STT(xc, xb[:, i:i + S], tap(i), xc, ALU.mult, ALU.add))
                    settle()
                STT(xc, xb[:, 0:S], tap(0), xc, ALU.mult, ALU.add).then_inc(xc_ready, 1)
                refill.after(("xb", c))

            def conv_part(c):
                xc = prob[:, c % 2, 640:640 + S]
                dve.wait_ge(xc_ready, c + 1)
                dve.wait_ge(xc_hi, c + 1)
                cs = slice((c % 2) * S, (c % 2) * S + S)
                low(PTL[:, cs], xc, PTH[:, cs]).then_inc(xc_lo, 1)

            def decays(c):
                j = c % LRU_G
                refill.need(("i", c))
                settle()
                dve.wait_ge(*freed(("i", c)))
                STT(LX[:, j, :], tmp[:, 1 + c % 2, :], 1.0, prob[:, c % 2, 640:640 + S], ALU.add, ALU.mult)

            def squared_mult(c):
                dve.wait_ge(decay_ready, c + 1)
                lv = LV[:, c % LRU_G, :]
                STT(lv, squared_decay(c), 1.0, lv, ALU.add, ALU.mult).then_inc(mult_sq, 1)

            def scan(c):
                j = c % LRU_G
                dve.wait_ge(mult_ready, c // LRU_G + 1)
                step(T(LX[:, j, :], LX[:, j, :], LV[:, j, :], ALU.mult))
                settle()
                step(dve.tensor_tensor_scan(LV[:, j, :], LA[:, j, :], LX[:, j, :], 0.0, ALU.mult, ALU.add))
                settle()
                dve.wait_ge(*freed(("gl", c)))
                STT(yt[:, c % 2, :], sg[:, c % 2, :], 0.5, LV[:, j, :], ALU.mult, ALU.mult).then_inc(yl_f32, 1)

            def yl_parts(c):
                tiles_y[0] += 1
                dve.wait_ge(yl_f32, c + 1)
                dve.wait_ge(y_hi, tiles_y[0])
                low(YLL[:, c, :], yt[:, c % 2, :], YLH[:, c, :]).then_inc(y_lo, 1)

            convolve(0)
            conv_part(0)
            for c in range(LRU_T):
                if c + 1 < LRU_T:
                    convolve(c + 1)
                decays(c)
                squared_mult(c)
                if c + 1 < LRU_T:
                    conv_part(c + 1)
                refill.after(("i", c))
                if c % LRU_G == LRU_G - 1:
                    scan(c - 2)
                if c >= 1:
                    evacuate(("gl", c - 1))
                if c % LRU_G == LRU_G - 1:
                    scan(c - 1)
                    yl_parts(c - 2)
                    yl_parts(c - 1)
                elif c % LRU_G == 0 and c > 0:
                    scan(c - 1)
                    yl_parts(c - 1)
                if c == 1:
                    diagonals(root[:, 1, 0:TB])
            evacuate(("gl", LRU_T - 1))
            scan(LRU_T - 1)
            yl_parts(LRU_T - 1)
            dve.wait_ge(factor_ready, 3)
            residual("lo", RES, 3 * KD, 3 * (KD - 1), KD - 1)
            row_factors(2, ("ssq", 2))
            dve.wait_ge(factor_ready, 4)
            normalise(2, RES, lambda t: vcol(vec, "gain3", t), obank[1][:, :])

            refill.need(("f", 0))
            dve.wait_ge(gemm_steps, acc_done[("f", 0)])
            for t in range(TB):
                last = T(sp[:, 0, t * 16:t * 16 + 16], bank_of(("f", 0))[:, t * 16:t * 16 + 16], bfb[:, :], ALU.add)
            last.then_inc(freed(("f", 0))[0], 1)
            dve.wait_ge(*freed(("f", 0)))
            log_sigmoid(sp[:, 0, :], 64, sp[:, 5, :], 2)
            refill.after(("f", 0))
            dve.wait_ge(res_spilled, 16 * KD)
            evacuate(("vf", 0))
            dve.wait_ge(gemm_steps, acc_done[("cum", 0)])
            rest = tmp[0:16, 0, :]
            dve.tensor_copy(rest, bank_of(("cum", 0))[0:16, :]).then_inc(freed(("cum", 0))[0], 1)
            dve.wait_ge(*freed(("cum", 0)))
            for j in range(3):
                step(dve.tensor_copy(cparts(0, j), rest))
                settle()
                if j < 2:
                    step(T(rest, rest, cparts(0, j), ALU.subtract))
                last = TS(cparts(1, j), cparts(0, j), -1.0, None, ALU.mult)
                settle()
            last.then_inc(cum_split, 1)
            evacuate(("vf", 1))
            evacuate(("q", PAIR_F0))
            evacuate(("k", PAIR_F0))
            attention(2 * PAIR_F0, 2 * PAIRS, slots_of_heads(PAIR_F0, PAIRS), [], lambda n: None)
            dve.wait_ge(res_back, 16)
            residual("fo", RES2, 4 * KD, 4 * (KD - 1), 2 * (KD - 1))
            row_factors(3, ("ssq", 3))
            dve.wait_ge(factor_ready, 5)
            for t in range(KD):
                STT(RES2[:, t, :], RES2[:, t, :], vcol(vec, "final2", t), obank[1][:, :], ALU.mult, ALU.mult)\
                    .then_inc(out_ready, 1)


def constants():
    con = np.zeros((P, NCON), np.float32)
    con[:, 0:P] = np.eye(P)
    tables = np.zeros((P, 4, S), np.float32)
    for i, (head, rot) in enumerate(((HD, HD // 4), (32, 32 // 4))):
        half = rot // 2
        inv = (np.float32(500000.0) ** (-np.arange(half, dtype=np.float32) / np.float32(half))).astype(np.float32)
        ang = (np.arange(S, dtype=np.float32)[:, None] * inv[None, :]).astype(np.float32).astype(np.float64)
        tables[:, 2 * i] = 1.0
        for base in range(0, P, head):
            for j in range(half):
                a, b = base + j, base + half + j
                con[b, CON[("rot_b", "rot_i")[i]] + a] = -1.0
                con[a, CON[("rot_b", "rot_i")[i]] + b] = 1.0
                tables[a, 2 * i] = tables[b, 2 * i] = np.cos(ang[:, j])
                tables[a, 2 * i + 1] = tables[b, 2 * i + 1] = np.sin(ang[:, j])
    p = np.arange(P)[:, None]
    con[:, CON["tri"]:CON["tri"] + P] = np.where(np.arange(P)[None, :] > p, -1.0, 0.0)
    con[:, CON["half"]:CON["half"] + P] = np.where((np.arange(P)[None, :] >= CH) & (p < CH), -1.0, 0.0)
    con[:, CON["upto"]:CON["upto"] + S] = np.arange(S)[None, :] >= p
    return con, tables


def pack(w_in, w_a, w_b, w_out, lru_in, wa, wx, lru_out, fox_in, fox_out):
    stream = np.zeros((len(PLAN["units"]), P, KD * P), np.float32)

    def columns(w, c0, n, k0=0, k1=None):
        part = w[k0 * P:(w.shape[0] if k1 is None else k1 * P), c0:c0 + n]
        return part.reshape(-1, P, n).transpose(1, 0, 2).reshape(P, -1)

    lout = np.concatenate([columns(lru_out, t * P, P) for t in range(KD)], axis=1)
    for u, (kind, i) in enumerate(PLAN["units"]):
        if kind == "va":
            part = columns(w_in, 1024, S, 2 * i, 2 * i + 2)
        elif kind == "vbiw":
            part = np.concatenate([w_in[:, 2624:2688], w_in[:, 3488:3496]], axis=1)
            part = columns(part, 0, 72)
        elif kind == "ik":
            part = columns(np.concatenate([w_in[:, 3456:3488]] * 4, axis=1), 0, P)
        elif kind == "kb":
            part = columns(np.concatenate([w_in[:, 2560:2624]] * 2, axis=1), 0, P)
        elif kind == "iq":
            part = columns(w_in, 3200 + i * P, P)
        elif kind == "za":
            part = columns(w_in, 3496 + i * P, P)
        elif kind == "zb":
            part = columns(w_in, 4520 + i * P, P)
        elif kind in ("q", "k", "g") and i < PAIR_B0:
            part = columns(w_in, {"q": 0, "k": 512, "g": 1536}[kind] + i * P, P)
        elif kind in ("q", "g") and i < PAIR_F0:
            part = columns(w_in, {"q": 2048, "g": 2688}[kind] + (i - PAIR_B0) * P, P)
        elif kind in ("q", "k", "g"):
            part = columns(fox_in, {"q": 0, "k": 1024, "g": 3072}[kind] + (i - PAIR_F0) * P, P)
        elif kind == "branch":
            part = np.concatenate([columns(w_a, i * P, P), columns(w_b, i * P, P)], axis=1)
        elif kind == "wout":
            part = columns(w_out, i * P, P)
        elif kind == "wax":
            part = np.concatenate([wa[i], wx[i]], axis=1)
        elif kind == "xb":
            part = columns(lru_in, i * P, P)
        elif kind == "gl":
            part = columns(lru_in, LRU_T * P + i * P, P)
        elif kind == "lout":
            part = lout[:, i * KD * P:(i + 1) * KD * P]
        elif kind == "f":
            part = columns(fox_in, 4096, 16)
        elif kind in ("vf0", "vf1"):
            part = columns(fox_in, 2048 + S * int(kind[2]), S, 2 * i, 2 * i + 2)
        elif kind == "fo":
            part = columns(fox_out, i * P, P)
        stream[u, :, 0:part.shape[1]] = part
    return stream


def kernel(**inputs):
    import concourse.bacc as bacc
    from concourse import mybir
    from concourse.bass_utils import run_bass_kernel_spmd

    a = {k: np.asarray(v) for k, v in inputs.items()}
    tiles = lambda v: v.reshape(-1, P).T
    vecs = np.concatenate([
        tiles(a["norm_gain"][0]), tiles(a["final_norm_gain"]), tiles(a["norm_g_2"][0]),
        tiles(a["norm_g_2"][1]), tiles(a["final_g_2"]),
        a["lru_conv_w_2"][0].reshape(4, LRU_T, P).transpose(2, 1, 0).reshape(P, 4 * LRU_T),
        tiles(a["lru_conv_b_2"][0]), tiles(a["b_merge"][0, 0]), tiles(a["b_merge"][0, 1]),
        tiles(a["lru_ba_2"][0]), tiles(a["lru_bx_2"][0]),
        tiles(a["lru_a_param_2"][0])], axis=1)
    con, tables = constants()
    arrays = {
        "xT": a["x"][0].T.reshape(KD, P, S).transpose(1, 0, 2),
        "vecs": vecs,
        "rel_ext": np.concatenate([a["rel_bias"][0][:, -1:]] * (2 * P - 1)
                                  + [a["rel_bias"][0][:, ::-1][:, 0:3 * P + 1]], axis=1),
        "b_f": a["fox_b_f_2"],
        "consts": con,
        "rope_tables": tables,
        "wstream": pack(a["w_in"][0], a["w_branch_a"][0], a["w_branch_b"][0], a["w_out"][0],
                        a["lru_w_in_2"][0], a["lru_wa_2"][0], a["lru_wx_2"][0],
                        a["lru_w_out_2"][0], a["fox_w_in_2"][0], a["fox_w_out_2"][0]),
    }
    arrays = {k: np.ascontiguousarray(v) for k, v in arrays.items()}
    nc = bacc.Bacc("TRN2", target_bir_lowering=False, num_devices=1)
    args = [nc.dram_tensor("in_" + k, v.shape, mybir.dt.from_np(v.dtype), kind="ExternalInput").ap()
            for k, v in arrays.items()]
    out = nc.dram_tensor("outT", (P, KD, S), mybir.dt.float32, kind="ExternalOutput").ap()
    build_program(nc, *args, out)
    got = run_bass_kernel_spmd(nc, [{"in_" + k: v for k, v in arrays.items()}], core_ids=[0]).results[0]["outT"]
    return np.ascontiguousarray(got.transpose(2, 1, 0).reshape(1, S, D))
```

```python
from contextlib import ExitStack

import numpy as np

S, D, P = 512, 1024, 128
KD = D // P
TB = S // P
HD = 64
CH = 64
TOPK = min(256, S // 4)
LRU_T = 12
LRU_G = 3
A_PAIRS, B_PAIRS, F_PAIRS = 4, 4, 8
PAIR_B0 = A_PAIRS
PAIR_F0 = A_PAIRS + B_PAIRS
PAIRS = A_PAIRS + B_PAIRS + F_PAIRS
EPS = 1e-6
BIG = 1e30
NOT_ADMITTED, TAKEN = -1e38, -3e38
EXT = 5 * P
ADDS = KD - 2
RAW, RING = 2, 4

VEC = {}
_at = 0
for _name, _n in (("gain1", KD), ("final1", KD), ("gain2", KD), ("gain3", KD), ("final2", KD),
                  ("conv_w", 4 * LRU_T), ("conv_b", LRU_T),
                  ("bma", KD), ("bmb", KD), ("ba", LRU_T), ("bx", LRU_T), ("ap", LRU_T)):
    VEC[_name] = _at
    _at += _n
NVEC = _at
HALVED = slice(VEC["bma"], VEC["ap"])
CON = {"ident": 0, "rot_b": 128, "rot_i": 256, "tri": 384, "half": 512, "upto": 640}
NCON = 640 + S


OPENING = (("ik", 0), ("vbiw", 0), ("ik_rot", 0), ("vbiw_t", 0), ("iq", 0), ("za", 0), ("iq_rot", 0),
           ("iq", 1), ("za", 1), ("iq_rot", 1), ("za", 2))
OPENING_ZA = sum(name[0] == "za" for name in OPENING)


def slots_of_heads(first_pair, last_pair):
    out = {}
    for p in range(first_pair, last_pair):
        nxt, gate = p + 1, [("g", p)]
        if nxt == last_pair:
            even, odd = [], gate
        elif nxt == PAIR_B0:
            even, odd = [("q", nxt)] + gate, [("q_rot", nxt), ("kb", 0), ("kb_rot", 0)]
        elif PAIR_B0 < nxt < PAIR_F0:
            even, odd = [("q", nxt)], [("q_rot", nxt)] + gate
        else:
            even, odd = [("q", nxt)], [("k", nxt)] + gate
        out[2 * p], out[2 * p + 1] = even, odd
    return out


def begun_early(fills, n):
    if n % 2 == 0 and len([x for x in fills[n + 1] if x[0][-4:] != "_rot"]) > len(fills[n]):
        return fills[n + 1][0]
    return None


def make_plan():
    accs, units, widths = [], [], []

    def unit(name, width=KD * P):
        units.append(name)
        widths.append(width)
        return len(units) - 1

    def acc(name, blocks):
        accs.append((name, blocks))

    def whole(name):
        u = unit(name)
        acc(name, [(u, k) for k in range(KD)])

    def narrow(name, n):
        u = unit(name, KD * n)
        acc(name, [(u, k) for k in range(KD)])

    def fill(names):
        for name in names:
            if name[0].endswith("_rot"):
                acc(name, [])
            else:
                whole(name)

    for j in range(KD // 2):
        unit(("va", j))
    acc(("va", 0), [(units.index(("va", j)), i) for j in range(KD // 2) for i in range(2)])
    for name in OPENING:
        if name[0] == "vbiw":
            narrow(name, 72)
        elif name[0][-2:] == "_t" or name[0][-4:] == "_rot":
            acc(name, [])
        else:
            whole(name)
    for t in range(OPENING_ZA, KD):
        whole(("za", t))
    whole(("q", 0))
    whole(("k", 0))
    first = slots_of_heads(0, PAIR_B0 + B_PAIRS)
    for n in range(2 * PAIR_F0):
        fill(first[n])
    whole(("zb", 0))
    whole(("zb", 1))
    for t in range(KD):
        if t >= 2:
            whole(("zb", t))
        u = unit(("branch", t))
        acc(("pa", t), [(u, k) for k in range(4)])
        acc(("pb", t), [(u, 4 + k) for k in range(4)])
    for t in range(KD):
        whole(("wout", t))
    whole(("xb", 0))
    for c in range(LRU_T):
        if c + 1 < LRU_T:
            whole(("xb", c + 1))
        w = unit(("wax", c), 2 * P)
        acc(("r", c), [(w, 0)])
        acc(("i", c), [(w, 1)])
        if c >= 1:
            whole(("gl", c - 1))
    whole(("gl", LRU_T - 1))
    lo = [unit(("lout", j)) for j in range(LRU_T)]
    for t in range(KD):
        acc(("lo", t), [(lo[(LRU_T * t + k) // KD], (LRU_T * t + k) % KD) for k in range(LRU_T)])
    narrow(("f", 0), 16)
    acc(("f_t", 0), [])
    for half in range(2):
        if half == 1:
            acc(("cum", 0), [])
        for j in range(KD // 2):
            unit(("vf%d" % half, j))
        acc(("vf", half), [(units.index(("vf%d" % half, j)), i)
                           for j in range(KD // 2) for i in range(2)])
    whole(("q", PAIR_F0))
    whole(("k", PAIR_F0))
    second = slots_of_heads(PAIR_F0, PAIRS)
    for n in range(2 * PAIR_F0, 2 * PAIRS):
        fill(second[n])
    for t in range(KD):
        whole(("fo", t))

    last_use = {}
    for a, (_, blocks) in enumerate(accs):
        for i, (u, _) in enumerate(blocks):
            last_use[u] = (a, i)
    steps, acc_done, unit_free = 0, {}, {}
    for a, (name, blocks) in enumerate(accs):
        for i, (u, _) in enumerate(blocks):
            ends = i == len(blocks) - 1
            if last_use[u] == (a, i) or ends:
                steps += 1
                if last_use[u] == (a, i):
                    unit_free[u] = steps
        if not blocks:
            steps += 1
        acc_done[name] = steps
    bank, used, turn = {}, [0] * 8, {"two": 0, "six": 0}
    for name, _ in accs:
        if name[0] in ("va", "vf"):
            continue
        ring = "six" if name[0] in ("xb", "gl", "r", "i") else "two"
        b = 2 + turn[ring] % 6 if ring == "six" else turn[ring] % 2
        turn[ring] += 1
        bank[name] = (b, used[b])
        used[b] += 1
    return dict(accs=accs, blocks=dict(accs), units=units, widths=widths, last_use=last_use,
                order={name: a for a, (name, _) in enumerate(accs)},
                acc_done=acc_done, unit_free=unit_free, bank=bank)


PLAN = make_plan()


def build_program(nc, xT, vecs, rel_ext, b_f, consts, rope, wstream, outT):
    import concourse.bass as bass
    from concourse import mybir

    f32, f32r, bf16 = mybir.dt.float32, mybir.dt.float32r, mybir.dt.bfloat16
    ALU = mybir.AluOpType
    ACT = mybir.ActivationFunctionType
    AX = mybir.AxisListType.X

    units, widths, blocks_of = PLAN["units"], PLAN["widths"], PLAN["blocks"]
    acc_done, unit_free, bank_use = PLAN["acc_done"], PLAN["unit_free"], PLAN["bank"]
    NU = len(units)
    slot, before, ring_order = {}, {}, []
    for u, name in enumerate(units):
        if name[0] == "wax":
            slot[u] = None
            if name[1] >= LRU_G:
                before[u] = units.index(("wax", name[1] - LRU_G))
        else:
            slot[u] = len(ring_order) % RING
            if len(ring_order) >= RING:
                before[u] = ring_order[-RING]
            ring_order.append(u)

    rows_dram = nc.dram_tensor("ext_bias_rows", (8, P, EXT), f32, kind="Internal").ap()
    res_dram = nc.dram_tensor("res_spill", (P, KD, S), f32, kind="Internal").ap()

    OFF = [0, P, 3 * P, 6 * P]
    NP = 10 * P
    S_PARTS = [(3,), (0, 2), (1,)]
    S_BANK = [0, 1, 0]
    S_COL = {3: 0, 0: 0, 2: P, 1: 0}
    M_COL = {3: 0, 0: 1, 2: 2, 1: 3}
    T_PARTS = [(0,), (1, 3), (2,)]
    T_BANK = [0, 1, 0]
    T_OFF = {0: 0, 1: 4 * P, 3: 7 * P, 2: 8 * P}
    WK = [0, 0, 2 * P, 5 * P, 9 * P]

    ctx = ExitStack()
    with ctx:
        def sb(name, shape, dt):
            return ctx.enter_context(nc.sbuf_tensor(name, shape, dt))

        def sem(name):
            return ctx.enter_context(nc.semaphore(name))

        XH = sb("xn_hi", [P, KD, S], f32r)
        XL = sb("xn_lo", [P, KD, S], f32r)
        wraw = sb("w_raw", [P, RAW, KD * P], f32)
        whi = sb("w_hi", [P, RING, KD * P], f32r)
        wlo = sb("w_lo", [P, RING, KD * P], f32r)
        prob = sb("prob", [P, 2, NP], f32)
        PTH = sb("probT_hi", [P, NP], f32r)
        PTL = sb("probT_lo", [P, NP], f32r)
        tmp = sb("tmp", [P, 4, S], f32)
        sq = prob[:, 1, 0:2 * S].rearrange("p (a b) -> p a b", a=2)
        diag = sb("diag", [P, S], f32)
        decay2 = sb("decay_squared", [P, S], f32)
        mean = sb("mean_square", [P, 2 * TB], f32)
        root = sb("row_factor", [P, 4, 2 * TB], f32)
        sg = sb("gate", [P, 2, S], f32)
        yt = sb("y_f32", [P, 2, S], f32)
        vec = sb("vec", [P, NVEC], f32)
        hvec = sb("half_vec", [P, HALVED.stop - HALVED.start], f32)
        g12 = sb("gain12", [P, KD], f32)
        ident = sb("ident", [P, P], f32)
        ones = sb("ones", [P, P], f32)
        rotb = sb("rot_b", [P, P], f32r)
        roti = sb("rot_i", [P, P], f32r)
        idbig = sb("id_big", [P, P], bf16)
        tri = sb("tri", [P, P], bf16)
        mx = sb("row_max", [P, 2, 4], f32)
        nmx = sb("row_negmax", [P, 2, 4], f32)
        rs = sb("row_sum", [P, 2, 4], f32)
        rcp = sb("row_rcp", [P, 2, 4], f32)
        iw = sb("iw", [P, TB, 8], f32)
        m8 = sb("max8", [P, 3, 8], f32)
        flat = tmp[:, 3, :]
        bfb = sb("b_f", [P, 16], f32)
        sp = sb("softplus", [P, 6, 64], f32)
        rate = sb("decay_rate", [P, 3, LRU_T], f32)

        def zone(first_kib, spec):
            with ExitStack() as z:
                if first_kib:
                    z.enter_context(nc.sbuf_tensor(f"below_{spec[0][0]}", [P, first_kib * 256], f32))
                return [z.enter_context(nc.sbuf_tensor(*x)) for x in spec]

        QH, QL, KH, KL, VBH, VBL, bias, wk, MB, ROPE = zone(0, [
            ("q_hi", [P, 2, S], f32r), ("q_lo", [P, 2, S], f32r),
            ("k_hi", [P, 2, S], f32r), ("k_lo", [P, 2, S], f32r),
            ("vb_hi", [P, TB, P], f32r), ("vb_lo", [P, TB, P], f32r),
            ("bias", [P, 2, S], f32), ("index_score", [P, WK[4]], f32),
            ("top_mask", [P, NP], bf16), ("rope", [P, 4, S], f32)])
        VH, VL = zone(39, [("va_hi", [P, TB, S], f32r), ("va_lo", [P, TB, S], f32r)])
        YAH, YAL = zone(55, [("ya_hi", [P, 4, S], f32r), ("ya_lo", [P, 4, S], f32r)])
        GA, = zone(72, [("gate_a", [P, KD, S], f32)])
        XT, = zone(55, [("x_in", [P, KD, S], f32)])
        XUH, = zone(72, [("xu_hi", [P, KD, S], f32r)])
        XUL, = zone(0, [("xu_lo", [P, KD, S], f32r)])
        YBH, YBL = zone(39, [("yb_hi", [P, 4, S], f32r), ("yb_lo", [P, 4, S], f32r)])
        MGH, MGL = zone(0, [("merged_hi", [P, KD, S], f32r), ("merged_lo", [P, KD, S], f32r)])
        RES, = zone(72, [("res", [P, KD, S], f32)])
        YLH, YLL = zone(0, [("yl_hi", [P, LRU_T, S], f32r), ("yl_lo", [P, LRU_T, S], f32r)])
        LA, LX, LV, WAXH, WAXL = zone(48, [
            ("decay", [P, LRU_G, S], f32), ("gated_x", [P, LRU_G, S], f32),
            ("mult", [P, LRU_G, S], f32),
            ("wax_hi", [P, LRU_G, 2 * P], f32r), ("wax_lo", [P, LRU_G, 2 * P], f32r)])
        VFH, VFL, XNH, CQ, CK = zone(16, [
            ("vf_hi", [P, TB, 2 * S], f32r), ("vf_lo", [P, TB, 2 * S], f32r),
            ("xf_hi", [P, KD, S], f32r),
            ("cum_q", [P, 4, S], bf16), ("cum_k", [P, 4, S], bf16)])
        XNL, = zone(72, [("xf_lo", [P, KD, S], f32r)])
        YFH, YFL = XH, XL
        upto = decay2
        RES2, = zone(16, [("res_back", [P, KD, S], f32)])
        GB = tmp[:, 2:4, :]

        pj = [ctx.enter_context(nc.psum_tensor(f"acc{i}", [P, S], f32)) for i in range(2)]
        sbank = [ctx.enter_context(nc.psum_tensor(f"scores{i}", [P, S], f32)) for i in range(2)]
        tbank = [ctx.enter_context(nc.psum_tensor(f"probT{i}", [P, S], f32)) for i in range(2)]
        obank = [ctx.enter_context(nc.psum_tensor(f"out{i}", [P, S], f32)) for i in range(2)]
        tok = sbank + tbank

        x_loaded = [sem(f"x_loaded{i}") for i in range(4)]
        w_loaded = [sem(f"w_loaded{i}") for i in range(RAW)]
        const_loaded = sem("const_loaded")
        vec_loaded = sem("vec_loaded")
        upto_loaded = sem("upto_loaded")
        ext_written = sem("ext_written")
        bias_loaded = [sem(f"bias_loaded{i}") for i in range(2)]
        res_loaded = [sem(f"res_loaded{t}") for t in range(KD)]
        res_spilled = sem("res_spilled")
        res_back = sem("res_back_loaded")
        cum_moved = sem("cum_moved")
        out_stored = sem("out_stored")
        w_hi = sem("w_hi_ready")
        xn_hi = sem("xn_hi_ready")
        xu_hi = sem("xu_hi_ready")
        acc_act = sem("acc_act_read")
        v_hi = sem("v_hi_ready")
        rope_hi = sem("rope_hi_ready")
        index_relu = sem("index_relu_ready")
        exp_done = sem("exp_done")
        pt_hi = sem("probT_hi_ready")
        y_hi = sem("y_hi_ready")
        sq_ready = sem("square_ready")
        root_ready = sem("root_ready")
        mg_hi = sem("merged_hi_ready")
        xc_hi = sem("conv_hi_ready")
        decay_ready = sem("decay_ready")
        mult_ready = sem("mult_ready")
        ls_exp = sem("logsig_exp_ready")
        ones_ready = sem("ones_ready")
        consts_ready = sem("consts_ready")
        w_lo = sem("w_lo_ready")
        xn_f32 = sem("xn_f32_ready")
        xn_lo = sem("xn_lo_ready")
        xu_lo = sem("xu_lo_ready")
        v_lo = sem("v_lo_ready")
        rope_sum = sem("rope_sum_ready")
        rope_lo = sem("rope_lo_ready")
        index_sum = sem("index_sum_ready")
        mx_ready = sem("row_max_ready")
        prob_ready = sem("prob_ready")
        pt_lo = sem("probT_lo_ready")
        o_taken = sem("out_taken")
        y_lo = sem("y_lo_ready")
        sq_used = sem("square_used")
        var_ready = sem("var_ready")
        diag_ready = sem("diag_ready")
        mg_sum = sem("merged_sum_ready")
        mg_lo = sem("merged_lo_ready")
        xc_ready = sem("conv_ready")
        xc_lo = sem("conv_lo_ready")
        mult_sq = sem("mult_squared_ready")
        ls_arg = sem("logsig_arg_ready")
        ls_ready = sem("logsig_ready")
        cum_split = sem("cum_split_ready")
        yl_f32 = sem("recurrence_y_ready")
        out_ready = sem("out_ready")
        dve_own = sem("dve_own")
        acc_free = [sem(f"acc_free{i}") for i in range(8)]
        gemm_steps = sem("gemm_steps")
        ssq_done = sem("sum_of_squares_done")
        index_done = sem("index_scores_done")
        s_done = sem("scores_done")
        t_done = sem("transpose_done")
        o_done = sem("out_done")
        factor_ready = sem("factor_ready")
        bias_ready = sem("bias_ready")
        cum_ones = sem("cum_ones_ready")

        block = ctx.enter_context(nc.Block())

        def bank_of(name):
            return (pj + sbank + tbank + obank)[bank_use[name][0]]

        def freed(name):
            b, use = bank_use[name]
            return acc_free[b], use + 1

        rope_order = [name for name, _ in PLAN["accs"] if name[0].endswith("_rot")]
        rope_number = {(name[0][:-4], name[1]): i for i, name in enumerate(rope_order)}

        def cparts(negative, j):
            at = (3 * negative + j) * S // 2
            return prob[0:16, :, :].rearrange("h a b -> h (a b)")[:, at:at + S // 2].bitcast(bf16)

        def squared_decay(c):
            return tmp[:, 3, :] if c % 2 == 0 else decay2[:, :]

        @block.sync
        def _(sp):
            def x_tiles(i):
                sp.dma_start(XT[:, 2 * i:2 * i + 2, :], xT[:, 2 * i:2 * i + 2, :]).then_inc(x_loaded[i], 16)

            x_tiles(0)
            for u in range(NU):
                if u >= RAW:
                    sp.wait_ge(w_lo, u - RAW + 1)
                sp.dma_start(wraw[:, u % RAW, 0:widths[u]], wstream[u, :, 0:widths[u]])\
                  .then_inc(w_loaded[u % RAW], 16)
                if u == 0:
                    for i in range(1, 4):
                        x_tiles(i)
                if u == 3:
                    for dst, src in ((wk[:, 0:CON["upto"]], consts[:, 0:CON["upto"]]), (ROPE[:, :, :], rope),
                                     (bfb[:, :], b_f.to_broadcast([P, 16]))):
                        sp.dma_start(dst, src).then_inc(const_loaded, 16)
            for t in range(KD):
                sp.wait_ge(out_ready, t + 1)
                sp.dma_start(outT[:, t, :], RES2[:, t, :]).then_inc(out_stored, 16)
            sp.wait_ge(out_stored, 16 * KD)

        @block.gpsimd
        def _(pool):
            pool.wait_ge(w_lo, 4)
            pool.dma_start(rows_dram, bass.AP(rel_ext.tensor, 0, [[EXT, 8], [0, P], [1, EXT]]))\
                .then_inc(ext_written, 16)
            pool.wait_ge(ext_written, 16)
            for h in range(2 * A_PAIRS):
                if h >= 2:
                    pool.wait_ge(mx_ready, 3 * (h - 1))
                shifted = bass.AP(rows_dram.tensor, P * EXT * h + P - 1, [[EXT - 1, P], [1, S]])
                pool.dma_start(bias[:, h % 2, :], shifted).then_inc(bias_loaded[h % 2], 16)
                pool.wait_ge(bias_loaded[h % 2], 16 * (h // 2 + 1))
                pool.memset(bias[0:CH, h % 2, S - CH:S], -BIG).then_inc(bias_ready, 1)
            for t in range(KD):
                pool.wait_ge(mg_sum, t + 1)
                pool.dma_start(RES[:, t, :], xT[:, t, :]).then_inc(res_loaded[t], 16)
            for t in range(KD):
                pool.wait_ge(*freed(("lo", t)))
                pool.dma_start(res_dram[:, t, :], RES[:, t, :]).then_inc(res_spilled, 16)
            pool.memset(CQ[:, :, :], 1.0).then_inc(cum_ones, 1)
            pool.memset(CK[:, :, :], 1.0).then_inc(cum_ones, 1)
            pool.dma_start(upto[:, :], consts[:, CON["upto"]:NCON]).then_inc(upto_loaded, 16)
            pool.wait_ge(cum_ones, 2)
            pool.wait_ge(cum_split, 1)
            for j in range(3):
                for dst, row, negative in ((CQ, 3 + j, 0), (CK, j, 1)):
                    pool.dma_start(dst[row:P:32, :, :], cparts(negative, j)).then_inc(cum_moved, 16)
            pool.wait_ge(o_done, 2 * PAIRS)
            pool.dma_start(RES2[:, :, :], res_dram).then_inc(res_back, 16)
            pool.wait_ge(res_back, 16)

        @block.tensor
        def _(pe):
            mm = pe.matmul

            def three(out, ah, al, bh, bl, start, stop):
                mm(out, ah, bh, start=start, stop=False)
                mm(out, ah, bl, start=False, stop=False)
                return mm(out, al, bh, start=False, stop=stop)

            def open_bank(name):
                b, use = bank_use[name]
                if use >= 1:
                    pe.wait_ge(acc_free[b], use)

            def weights(u, b):
                if slot[u] is None:
                    c = units[u][1] % LRU_G
                    return WAXH[:, c, b * P:b * P + P], WAXL[:, c, b * P:b * P + P]
                return whi[:, slot[u], b * P:b * P + P], wlo[:, slot[u], b * P:b * P + P]

            def close(name, i, last):
                u = blocks_of[name][i][0]
                if PLAN["last_use"][u] == (PLAN["order"][name], i) or i == len(blocks_of[name]) - 1:
                    last.then_inc(gemm_steps, 1)

            def gemm(name, rhs_hi, rhs_lo, first=0, end=None, ready=None):
                blocks = blocks_of[name]
                end = len(blocks) if end is None else end
                if first == 0:
                    open_bank(name)
                for i in range(first, end):
                    u, b = blocks[i]
                    if i == 0 or blocks[i - 1][0] != u:
                        pe.wait_ge(w_lo, u + 1)
                    if ready is not None:
                        pe.wait_ge(ready[0], ready[1] + i + 1)
                    wh, wl = weights(u, b)
                    last = three(bank_of(name)[:, :], wh, wl, rhs_hi[:, i, :], rhs_lo[:, i, :],
                                 i == 0, i == len(blocks) - 1)
                    close(name, i, last)

            def values(name, xh, xl, first=0, end=KD):
                blocks = blocks_of[name]
                for i in range(first, end):
                    u, half = blocks[i]
                    if half == 0:
                        pe.wait_ge(w_lo, u + 1)
                    if name[0] == "va":
                        pe.wait_ge(xu_lo, i + 1)
                    for t in range(TB):
                        if name == ("vf", 1) and i == 0:
                            pe.wait_ge(v_lo, TB + t + 1)
                        ts = slice(t * P, t * P + P)
                        ws = slice(half * S, half * S + S)
                        o = tok[t][:, :]
                        mm(o, xh[:, i, ts], whi[:, slot[u], ws], start=i == 0, stop=False)
                        mm(o, xh[:, i, ts], wlo[:, slot[u], ws], start=False, stop=False)
                        last = mm(o, xl[:, i, ts], whi[:, slot[u], ws], start=False, stop=i == KD - 1)
                    close(name, i, last)

            def narrow(name, n, ready=None):
                open_bank(name)
                u = blocks_of[name][0][0]
                pe.wait_ge(w_lo, u + 1)
                if ready is not None:
                    pe.wait_ge(*ready)
                for k in range(KD):
                    wh, wl = (w[:, slot[u], k * n:k * n + n] for w in (whi, wlo))
                    last = three(bank_of(name)[0:n, :], wh, wl, XH[:, k, :], XL[:, k, :], k == 0, k == KD - 1)
                last.then_inc(gemm_steps, 1)

            def narrow_transposed(name, n, source):
                open_bank(name)
                pe.wait_ge(*freed(source))
                for t in range(TB):
                    last = pe.transpose(bank_of(name)[:, t * n:t * n + n], flat[0:n, t * P:t * P + P],
                                        ident[0:n, 0:n])
                last.then_inc(gemm_steps, 1)

            def rotate(name):
                src = (name[0][:-4], name[1])
                rot = roti if src[0] in ("ik", "iq") else rotb
                open_bank(name)
                pe.wait_ge(consts_ready, 1)
                pe.wait_ge(*freed(src))
                mm(bank_of(name)[:, :], rot[:, :], KH[:, 0, :], start=True, stop=False)
                mm(bank_of(name)[:, :], rot[:, :], KL[:, 0, :], start=False, stop=True).then_inc(gemm_steps, 1)

            def sum_squares(squares, adds, last_in, sums=1):
                pe.wait_ge(sq_used, adds)
                pe.wait_ge(sq_ready, squares)
                for j in range(sums):
                    for t in range(TB):
                        out, ts = obank[0][:, TB * j + t:TB * j + t + 1], slice(t * P, t * P + P)
                        mm(out, sq[:, j, ts], ones[:, 0:1], start=True, stop=False)
                        last = mm(out, yt[:, last_in + j, ts], ones[:, 0:1], start=False, stop=True)
                last.then_inc(ssq_done, 1)

            def broadcast(n, dst):
                pe.wait_ge(diag_ready, n)
                for t in range(TB):
                    ts = slice(t * P, t * P + P)
                    last = mm(dst[:, ts], ones[:, :], diag[:, ts], start=True, stop=True)
                last.then_inc(factor_ready, 1)

            def scores(n, part):
                pair, r0 = n // 2, HD * (n % 2)
                rows = slice(r0, r0 + HD)
                if part == 0 and n % 2 == 0:
                    if pair == 0:
                        pe.wait_ge(index_sum, 24)
                    if PAIR_B0 <= pair < PAIR_F0:
                        last_turned = ("kb", 0) if pair == PAIR_B0 else ("q", pair)
                        pe.wait_ge(rope_lo, rope_number[last_turned] + 1)
                    else:
                        pe.wait_ge(*freed(("q", pair)))
                        pe.wait_ge(*freed(("k", pair)))
                    if pair == PAIR_B0:
                        pe.wait_ge(consts_ready, 3)
                    if pair == PAIR_F0:
                        pe.wait_ge(cum_moved, 6 * 16)
                        pe.wait_ge(v_lo, 3 * TB)
                if n > 0 or part == 2:
                    prior = 3 * n + {0: 0, 1: -1, 2: 1}[part]
                    pe.wait_ge(mx_ready if (prior - 1) // 3 < 2 * A_PAIRS else exp_done, prior)
                for qb in S_PARTS[part]:
                    w = P * (qb + 1)
                    o = sbank[S_BANK[part]][:, S_COL[qb]:S_COL[qb] + w]
                    qs = slice(qb * P, qb * P + P)
                    qh, ql = QH[rows, pair % 2, qs], QL[rows, pair % 2, qs]
                    if PAIR_B0 <= pair < PAIR_F0:
                        kh, kl = KH[rows, 1, 0:w], KL[rows, 1, 0:w]
                    else:
                        kh, kl = KH[rows, pair % 2, 0:w], KL[rows, pair % 2, 0:w]
                    last = three(o, qh, ql, kh, kl, True, pair < PAIR_B0)
                    if PAIR_B0 <= pair < PAIR_F0:
                        last = mm(o, idbig[:, :], MB[:, OFF[qb]:OFF[qb] + w], start=False, stop=True)
                    elif pair >= PAIR_F0:
                        h = n - 2 * PAIR_F0
                        g = slice(32 * (h // 4), 32 * (h // 4) + 6)
                        mm(o, CQ[g, h % 4, qs], CK[g, h % 4, 0:w], start=False, stop=False)
                        last = mm(o[:, w - P:w], idbig[:, :], tri[:, :], start=False, stop=True)
                last.then_inc(s_done, 1)

            def transposes(n, part):
                if part == 0:
                    pe.wait_ge(prob_ready, n + 1)
                if n > 0 or part == 2:
                    pe.wait_ge(pt_lo, 3 * n + {0: 0, 1: -1, 2: 1}[part])
                col = 0
                for kb in T_PARTS[part]:
                    for qb in range(kb, TB):
                        last = pe.transpose(tbank[T_BANK[part]][:, col:col + P],
                                            prob[:, n % 2, OFF[qb] + kb * P:OFF[qb] + kb * P + P],
                                            ident[:, :])
                        col += P
                last.then_inc(t_done, 1)

            def outputs(n):
                pair = n // 2
                if n >= 2:
                    pe.wait_ge(o_taken, n - 1)
                for part in range(3):
                    pe.wait_ge(pt_lo, 3 * n + part + 1)
                    for kb in T_PARTS[part]:
                        w = S - kb * P
                        if pair < PAIR_B0:
                            vh, vl = (v[:, kb, P * pair:P * pair + P] for v in (VH, VL))
                        elif pair < PAIR_F0:
                            vh, vl = VBH[:, kb, :], VBL[:, kb, :]
                        else:
                            c = P * (pair - PAIR_F0)
                            vh, vl = VFH[:, kb, c:c + P], VFL[:, kb, c:c + P]
                        ps = slice(T_OFF[kb], T_OFF[kb] + w)
                        last = three(obank[n % 2][:, kb * P:S], vh, vl, PTH[:, ps], PTL[:, ps],
                                     kb == 0, kb == 2)
                last.then_inc(o_done, 1)

            def attention(n0, n1, fills, tail, xh, xl):
                for n in range(n0, n1 + 1):
                    names = list(fills[n] if n < n1 else tail)
                    if names and names[0][0].endswith("_rot"):
                        rotate(names.pop(0))
                    late = names.pop() if names and names[-1][0].endswith("_rot") else None
                    blocks = [(name, k) for name in names for k in range(KD)]
                    if n < n1:
                        if n % 2 == 0 and begun_early(fills, n):
                            blocks += [(begun_early(fills, n), k) for k in range(KD // 2)]
                        if n % 2 == 1 and begun_early(fills, n - 1):
                            blocks = blocks[KD // 2:]
                    for part, (b0, b1) in enumerate(((0, 2), (2, 5), (5, 8))):
                        if n > n0:
                            transposes(n - 1, part)
                        if n < n1:
                            scores(n, part)
                        for name, k in blocks[b0:b1]:
                            gemm(name, xh, xl, k, k + 1)
                    for name, k in blocks[8:]:
                        gemm(name, xh, xl, k, k + 1)
                    if n > n0:
                        outputs(n - 1)
                    if late:
                        rotate(late)

            pe.wait_ge(ones_ready, 1)
            values(("va", 0), XUH, XUL, 0, 4)
            sum_squares(KD, ADDS, 0)
            values(("va", 0), XUH, XUL, 4, 5)
            broadcast(1, obank[1])
            values(("va", 0), XUH, XUL, 5, KD)
            for name in OPENING:
                if name[0] == "vbiw":
                    narrow(name, 72)
                elif name[0] == "vbiw_t":
                    narrow_transposed(name, 72, ("vbiw", 0))
                elif name[0].endswith("_rot"):
                    rotate(name)
                else:
                    gemm(name, XH, XL, ready=(xn_lo, 0) if name[0] == "ik" else None)
            pe.wait_ge(rope_lo, 3)
            pe.wait_ge(v_lo, TB)
            for m in range(24):
                qb, h = m // 8 + 1, m % 8
                rows = slice(32 * (h % 4), 32 * (h % 4) + 32)
                if m >= 4:
                    pe.wait_ge(index_relu, m - 3)
                w = P * (qb + 1)
                qs = slice(qb * P, qb * P + P)
                three(tok[m % 4][:, 0:w], QH[rows, h // 4, qs], QL[rows, h // 4, qs],
                      KH[rows, 1, 0:w], KL[rows, 1, 0:w], True, True).then_inc(index_done, 1)
            for t in range(OPENING_ZA, KD):
                gemm(("za", t), XH, XL)
            gemm(("q", 0), XH, XL)
            gemm(("k", 0), XH, XL)
            attention(0, 2 * PAIR_F0, slots_of_heads(0, PAIR_F0), [("zb", 0), ("zb", 1)], XH, XL)
            for t in range(KD):
                if t >= 2:
                    gemm(("zb", t), XH, XL)
                for name, yh, yl, base in ((("pa", t), YAH, YAL, 0), (("pb", t), YBH, YBL, 4)):
                    if t == 0:
                        pe.wait_ge(y_lo, base + 4)
                    gemm(name, yh, yl)
            for t in range(KD):
                gemm(("wout", t), MGH, MGL, ready=(mg_lo, 0) if t == 0 else None)
            sum_squares(3 * KD, 3 * ADDS, 0, 2)
            broadcast(2, obank[1])

            def gate_inputs(c):
                pe.wait_ge(xc_lo, c + 1)
                for name in (("r", c), ("i", c)):
                    open_bank(name)
                    (u, b), = blocks_of[name]
                    pe.wait_ge(w_lo, u + 1)
                    wh, wl = weights(u, b)
                    cs = slice((c % 2) * S, (c % 2) * S + S)
                    last = three(bank_of(name)[:, :], wh, wl, PTH[:, cs], PTL[:, cs], True, True)
                    close(name, 0, last)

            gemm(("xb", 0), XH, XL, ready=(xn_lo, KD))
            for c in range(LRU_T):
                if c + 1 < LRU_T:
                    gemm(("xb", c + 1), XH, XL)
                gate_inputs(c)
                if c >= 1:
                    gemm(("gl", c - 1), XH, XL)
            gemm(("gl", LRU_T - 1), XH, XL)
            for t in range(KD):
                gemm(("lo", t), YLH, YLL, ready=(y_lo, 8) if t == 0 else None)
                if t == 0:
                    broadcast(3, obank[0])
            sum_squares(4 * KD, 4 * ADDS, 1)

            narrow(("f", 0), 16, (xu_lo, 2 * KD))
            broadcast(4, obank[1])
            values(("vf", 0), XH, XL, 0, 1)
            narrow_transposed(("f_t", 0), 16, ("f", 0))
            values(("vf", 0), XH, XL, 1, KD)
            open_bank(("cum", 0))
            pe.wait_ge(ls_ready, 2)
            pe.wait_ge(upto_loaded, 16)
            for kb in range(TB):
                last = mm(bank_of(("cum", 0))[0:16, kb * P:S], sp[:, 5, kb * 16:kb * 16 + 16],
                          upto[:, 0:S - kb * P], start=kb == 0, stop=kb == TB - 1)
            last.then_inc(gemm_steps, 1)
            values(("vf", 1), XH, XL)
            gemm(("q", PAIR_F0), XNH, XNL, ready=(xn_lo, 2 * KD))
            gemm(("k", PAIR_F0), XNH, XNL)
            attention(2 * PAIR_F0, 2 * PAIRS, slots_of_heads(PAIR_F0, PAIRS), [], XNH, XNL)
            for t in range(KD):
                gemm(("fo", t), YFH, YFL, ready=(y_lo, 8 + LRU_T) if t == 0 else None)
            sum_squares(5 * KD, 5 * ADDS, 0)
            broadcast(5, obank[1])

        act_kinds = ("vbiw_t", "ik", "iq", "kb", "q", "k", "g", "gl")
        act_order = [name for name, _ in PLAN["accs"] if name[0] in act_kinds]
        act_read = {name: i + 1 for i, name in enumerate(act_order)}

        def rope_parts(name):
            kind, i = name
            if kind == "ik":
                return KH[:, 1, :], KL[:, 1, :]
            if kind == "kb":
                return KH[:, 1, :], KL[:, 1, :]
            return QH[:, i % 2, :], QL[:, i % 2, :]

        def vcol(tensor, name, i):
            return tensor[:, VEC[name] + i:VEC[name] + i + 1]

        def halved(name, i):
            c = VEC[name] - HALVED.start + i
            return hvec[:, c:c + 1]

        def values_of(name):
            if name[0] == "va":
                return VH, VL, slice(0, S)
            return VFH, VFL, slice(name[1] * S, name[1] * S + S)

        def gated(n):
            pair = n // 2
            rows = slice(HD * (n % 2), HD * (n % 2) + HD)
            if pair < PAIR_B0:
                return rows, YAH[:, pair, :], YAL[:, pair, :]
            if pair < PAIR_F0:
                return rows, YBH[:, pair - PAIR_B0, :], YBL[:, pair - PAIR_B0, :]
            return rows, YFH[:, pair - PAIR_F0, :], YFL[:, pair - PAIR_F0, :]

        class Refill:

            def __init__(self, split):
                self.next, self.split = 0, split

            def need(self, name):
                for u, _ in blocks_of[name]:
                    self.upto(u)

            def upto(self, u):
                while self.next <= u:
                    self.split(self.next)
                    self.next += 1

            def freed_by(self, step):
                while self.next < NU and unit_free.get(before.get(self.next), 0) <= step:
                    self.split(self.next)
                    self.next += 1

            def after(self, name):
                self.freed_by(acc_done[name])

            def within(self, name):
                self.need(name)
                for u, _ in blocks_of[name][:-4]:
                    self.freed_by(unit_free[u])

        @block.scalar
        def _(act):
            act.dma_start(vec[:, :], vecs).then_inc(vec_loaded, 16)
            act.dma_start(ident[:, :], consts[:, 0:P]).then_inc(vec_loaded, 16)
            A = act.activation

            def split(u):
                act.wait_ge(w_loaded[u % RAW], 16 * (u // RAW + 1))
                if u in before:
                    act.wait_ge(gemm_steps, unit_free[before[u]])
                dst = WAXH[:, units[u][1] % LRU_G, :] if slot[u] is None else whi[:, slot[u], 0:widths[u]]
                A(dst, wraw[:, u % RAW, 0:widths[u]], ACT.Copy).then_inc(w_hi, 1)

            refill = Refill(split)

            def evacuate(name):
                kind, i = name
                if kind in ("va", "vf"):
                    refill.within(name)
                refill.need(name)
                act.wait_ge(gemm_steps, acc_done[name])
                if kind not in ("va", "vf"):
                    ps = bank_of(name)
                if kind in ("va", "vf"):
                    vh, _, cols = values_of(name)
                    for t in range(TB):
                        A(vh[:, t, cols], tok[t][:, :], ACT.Identity, scale=root[:, 0 if kind == "va" else 2, t:t + 1])\
                            .then_inc(v_hi, 1)
                elif kind in ("vbiw", "f"):
                    n = widths[blocks_of[name][0][0]] // KD
                    A(flat[0:n, :], ps[0:n, :], ACT.Copy).then_inc(freed(name)[0], 1)
                elif kind == "vbiw_t":
                    src = ps[:, 0:72 * TB].rearrange("p (t n) -> p t n", n=72)[:, :, 0:HD]
                    A(VBH[:, :, 0:HD], src, ACT.Copy)
                    A(VBH[:, :, HD:P], src, ACT.Copy).then_inc(acc_act, 1)
                elif name in rope_number:
                    A(KH[:, 0, :], ps[:, :], ACT.Copy).then_inc(acc_act, 1)
                elif kind in ("q", "k"):
                    A((QH if kind == "q" else KH)[:, i % 2, :], ps[:, :], ACT.Copy,
                      scale=HD ** -0.5 if kind == "q" else 1.0).then_inc(acc_act, 1)
                elif kind in ("g", "gl"):
                    if kind == "g" and i >= 2:
                        act.wait_ge(o_taken, 2 * i - 2)
                    if kind == "gl" and i >= 2:
                        act.wait_ge(yl_f32, i - 1)
                    A(sg[:, i % 2, :], ps[:, :], ACT.Tanh, scale=0.5).then_inc(acc_act, 1)
                elif kind == "za":
                    A(GA[:, i, :], ps[:, :], ACT.Tanh, scale=0.5, bias=halved("bma", i))\
                        .then_inc(freed(name)[0], 1)
                elif kind == "zb":
                    if i == 0:
                        act.wait_ge(rope_lo, len(rope_order))
                    if i >= 2:
                        act.wait_ge(mg_sum, i - 1)
                    A(GB[:, i % 2, :], ps[:, :], ACT.Tanh, scale=0.5, bias=halved("bmb", i))\
                        .then_inc(freed(name)[0], 1)
                elif kind == "xb":
                    if i >= 2:
                        act.wait_ge(xc_ready, i - 1)
                        act.wait_ge(mult_sq, i - 1)
                        act.wait_ge(xc_hi, i - 1)
                    A(prob[:, i % 2, 3:3 + S], ps[:, :], ACT.Copy)
                    A(prob[:, i % 2, 640:640 + S], ps[:, :], ACT.Identity, scale=vcol(vec, "conv_w", 4 * i + 3),
                      bias=vcol(vec, "conv_b", i)).then_inc(freed(name)[0], 1)
                elif kind == "r":
                    if i >= 1:
                        act.wait_ge(decay_ready, i)
                    A(tmp[:, 0, :], ps[:, :], ACT.Tanh, scale=0.5, bias=halved("ba", i))\
                        .then_inc(freed(name)[0], 1)
                elif kind == "i":
                    if i >= 2:
                        act.wait_ge(mult_sq, i - 1)
                    A(tmp[:, 1 + i % 2, :], ps[:, :], ACT.Tanh, scale=0.5, bias=halved("bx", i))\
                        .then_inc(freed(name)[0], 1)
                if kind not in ("xb", "r", "i", "ik", "vbiw"):
                    refill.after(name)

            def rotated(name):
                r = rope_number[name]
                act.wait_ge(rope_sum, r + 1)
                A(rope_parts(name)[0], tmp[:, 2, :], ACT.Copy,
                  scale=HD ** -0.5 if name[0] == "q" else 1.0).then_inc(rope_hi, 1)
                refill.after((name[0] + "_rot", name[1]))

            def exps(n, part):
                act.wait_ge(mx_ready, 3 * n + part + 1)
                for qb in S_PARTS[part]:
                    w = P * (qb + 1)
                    p = prob[:, n % 2, OFF[qb]:OFF[qb] + w]
                    c = M_COL[qb]
                    src = p if n < 2 * A_PAIRS else sbank[S_BANK[part]][:, S_COL[qb]:S_COL[qb] + w]
                    last = A(p, src, ACT.Exp, bias=nmx[:, n % 2, c:c + 1],
                             accum_out=rs[:, n % 2, c:c + 1])
                last.then_inc(exp_done, 1)

            def transposed(n, part):
                act.wait_ge(t_done, 3 * n + part + 1)
                w = sum(S - kb * P for kb in T_PARTS[part])
                c = T_OFF[T_PARTS[part][0]]
                A(PTH[:, c:c + w], tbank[T_BANK[part]][:, 0:w], ACT.Copy).then_inc(pt_hi, 1)

            def y_parts(n):
                if n % 2 == 1:
                    act.wait_ge(o_taken, n + 1)
                    A(gated(n)[1], yt[:, (n // 2) % 2, :], ACT.Copy).then_inc(y_hi, 1)

            def attention(n0, n1, fills, tail):
                for n in range(n0, n1 + 1):
                    names = list(fills[n] if n < n1 else tail)
                    turned = names.pop(0) if names and names[0][0].endswith("_rot") else None
                    if names:
                        refill.need(names[0])
                    for part in range(3):
                        if n > n0:
                            transposed(n - 1, part)
                        if n < n1:
                            exps(n, part)
                        if part == 0 and n >= n0 + 2:
                            y_parts(n - 2)
                        if part == 0 and turned:
                            rotated((turned[0][:-4], turned[1]))
                    for name in names:
                        if name[0].endswith("_rot"):
                            rotated((name[0][:-4], name[1]))
                        else:
                            evacuate(name)
                    if n < n1 and begun_early(fills, n):
                        refill.need(begun_early(fills, n))
                y_parts(n1 - 1)

            squares = [0]

            def square(src, t, scale=1.0, into=None):
                if t == 0:
                    A(sq[:, into or 0, :], src, ACT.Square, scale=scale).then_inc(sq_ready, 1)
                else:
                    k = squares[0]
                    A(yt[:, k % 2, :], src, ACT.Square, scale=scale).then_inc(sq_ready, 1)
                    squares[0] += 1

            def scaled(src, t, gain, xh):
                A(xh[:, t, :], src[:, t, :], ACT.Identity, scale=vcol(vec, gain, t)).then_inc(xu_hi, 1)

            def normalised(r, xh=XH, middle=lambda: None):
                for t in range(KD):
                    if t == KD // 2:
                        middle()
                    act.wait_ge(xn_f32, KD * r + t + 1)
                    A(xh[:, t, :], tmp[:, 2 + t % 2, :], ACT.Copy).then_inc(xn_hi, 1)

            def roots(norm, n):
                A(root[:, norm, 0:n], mean[:, 0:n], ACT.Sqrt).then_inc(root_ready, 1)

            for t in range(KD):
                if t % 2 == 0:
                    act.wait_ge(x_loaded[t // 2], 16)
                if t >= 3:
                    act.wait_ge(sq_used, t - 2)
                square(XT[:, t, :], t)
                if t == 0:
                    act.wait_ge(vec_loaded, 32)
                scaled(XT, t, "gain1", XUH)
                if t % 2 == 1:
                    refill.upto(t // 2 - (t == KD - 1))
            act.wait_ge(var_ready, 1)
            roots(0, TB)
            refill.upto(3)
            normalised(0, middle=lambda: refill.upto(4))
            evacuate(("va", 0))
            act.wait_ge(consts_ready, 1)
            for name in OPENING:
                if name[0].endswith("_rot"):
                    rotated((name[0][:-4], name[1]))
                else:
                    evacuate(name)
            for m in range(24):
                act.wait_ge(index_done, m + 1)
                if m >= 2:
                    act.wait_ge(index_sum, m - 1)
                w = P * (m // 8 + 2)
                A(prob[:, m % 2, 0:w], tok[m % 4][:, 0:w], ACT.Relu).then_inc(index_relu, 1)
            for t in range(OPENING_ZA, KD):
                evacuate(("za", t))
            evacuate(("q", 0))
            evacuate(("k", 0))
            act.wait_ge(ls_arg, 1)
            A(sp[:, 1, 0:LRU_T], sp[:, 1, 0:LRU_T], ACT.Exp).then_inc(ls_exp, 1)
            attention(0, 2 * PAIR_F0, slots_of_heads(0, PAIR_F0), [("zb", 0), ("zb", 1)])

            def merged(t):
                act.wait_ge(mg_sum, t + 1)
                A(MGH[:, t, :], yt[:, t % 2, :], ACT.Copy, scale=0.5).then_inc(mg_hi, 1)

            for t in range(KD):
                if t >= 2:
                    evacuate(("zb", t))
                refill.need(("pb", t))
                merged(t)
                refill.after(("pb", t))

            def residual_squares(kind, used, finals=False):
                for t in range(KD):
                    refill.need((kind, t))
                    act.wait_ge(*freed((kind, t)))
                    src = (RES if kind != "fo" else RES2)[:, t, :]
                    if finals:
                        if t > 1:
                            act.wait_ge(sq_used, used + 2 * (t - 1))
                        if t == 0:
                            A(sq[:, 0, :], src, ACT.Square).then_inc(sq_ready, 1)
                            A(sq[:, 1, :], src, ACT.Square, scale=vcol(vec, "final1", t)).then_inc(sq_ready, 1)
                        else:
                            A(yt[:, 0, :], src, ACT.Square).then_inc(sq_ready, 1)
                            A(yt[:, 1, :], src, ACT.Square, scale=vcol(vec, "final1", t)).then_inc(sq_ready, 1)
                    else:
                        if t >= 3:
                            act.wait_ge(sq_used, used + t - 2)
                        square(src, t)
                        if kind == "lo":
                            scaled(RES, t, "gain3", XH)
                    refill.after((kind, t))

            residual_squares("wout", ADDS, finals=True)
            act.wait_ge(var_ready, 2)
            roots(1, 2 * TB)
            normalised(1)

            def conv_parts(c):
                act.wait_ge(xc_ready, c + 1)
                A(PTH[:, (c % 2) * S:(c % 2) * S + S], prob[:, c % 2, 640:640 + S], ACT.Copy).then_inc(xc_hi, 1)

            def decays(c):
                j = c % LRU_G
                if c >= LRU_G:
                    act.wait_ge(yl_f32, c - LRU_G + 1)
                act.wait_ge(*freed(("r", c)))
                for dst, func, k in ((LA[:, j, :], ACT.Exp, 0), (squared_decay(c), ACT.Exp, 1),
                                     (LV[:, j, :], ACT.Tanh, 2)):
                    last = A(dst, tmp[:, 0, :], func, scale=rate[:, k, c:c + 1], bias=rate[:, k, c:c + 1])
                last.then_inc(decay_ready, 1)

            def yl_parts(c):
                act.wait_ge(yl_f32, c + 1)
                A(YLH[:, c, :], yt[:, c % 2, :], ACT.Copy).then_inc(y_hi, 1)

            evacuate(("xb", 0))
            conv_parts(0)
            refill.after(("xb", 0))
            for c in range(LRU_T):
                if c + 1 < LRU_T:
                    evacuate(("xb", c + 1))
                evacuate(("r", c))
                evacuate(("i", c))
                if c + 1 < LRU_T:
                    conv_parts(c + 1)
                    refill.after(("xb", c + 1))
                if c >= 3:
                    yl_parts(c - 3)
                decays(c)
                if c % LRU_G == LRU_G - 1:
                    act.wait_ge(mult_sq, c + 1)
                    A(LV[:, :, :], LV[:, :, :], ACT.Sqrt, scale=0.25).then_inc(mult_ready, 1)
                refill.after(("i", c))
                if c >= 1:
                    evacuate(("gl", c - 1))
            yl_parts(LRU_T - 3)
            yl_parts(LRU_T - 2)
            evacuate(("gl", LRU_T - 1))
            yl_parts(LRU_T - 1)
            residual_squares("lo", 3 * ADDS)
            act.wait_ge(var_ready, 3)
            roots(2, TB)

            evacuate(("f", 0))
            act.wait_ge(ls_arg, 2)
            A(sp[:, 1, :], sp[:, 1, :], ACT.Exp).then_inc(ls_exp, 1)
            normalised(2, XNH)
            evacuate(("vf", 0))
            evacuate(("vf", 1))
            evacuate(("q", PAIR_F0))
            evacuate(("k", PAIR_F0))
            attention(2 * PAIR_F0, 2 * PAIRS, slots_of_heads(PAIR_F0, PAIRS), [])
            residual_squares("fo", 4 * ADDS)
            act.wait_ge(var_ready, 4)
            roots(3, TB)

        @block.vector
        def _(dve):
            T = dve.tensor_tensor
            TS = dve.tensor_scalar
            STT = dve.scalar_tensor_tensor
            own = [0]

            def step(ins):
                own[0] += 1
                ins.then_inc(dve_own, 1)

            def settle():
                dve.wait_ge(dve_own, own[0])

            def split(u):
                dve.wait_ge(w_hi, u + 1)
                raw = wraw[:, u % RAW, 0:widths[u]]
                c = units[u][1] % LRU_G
                hi, lo = ((WAXH[:, c, :], WAXL[:, c, :]) if slot[u] is None else
                          (whi[:, slot[u], 0:widths[u]], wlo[:, slot[u], 0:widths[u]]))
                T(lo, raw, hi, ALU.subtract).then_inc(w_lo, 1)

            refill = Refill(split)

            def low(dst, src, hi, scale=1.0):
                if isinstance(scale, float) and scale == 1.0:
                    return T(dst, src, hi, ALU.subtract)
                return STT(dst, src, scale, hi, ALU.mult, ALU.subtract)

            def evacuate(name):
                kind, i = name
                if kind in ("va", "vf"):
                    refill.within(name)
                refill.need(name)
                if name in act_read:
                    dve.wait_ge(acc_act, act_read[name])
                elif kind in ("va", "vf"):
                    pass
                elif kind in ("vbiw", "f", "za"):
                    if kind != "vbiw":
                        refill.after(name)
                    return
                else:
                    dve.wait_ge(gemm_steps, acc_done[name])
                if kind in ("va", "vf"):
                    vh, vl, cols = values_of(name)
                    first = 0 if kind == "va" else TB * (1 + i)
                    for t in range(TB):
                        dve.wait_ge(v_hi, first + t + 1)
                        low(vl[:, t, cols], tok[t][:, :], vh[:, t, cols],
                            root[:, 0 if kind == "va" else 2, t:t + 1]).then_inc(v_lo, 1)
                    refill.after(name)
                    return
                ps, free = bank_of(name), freed(name)[0]
                if kind == "vbiw_t":
                    both = ps[:, 0:72 * TB].rearrange("p (t n) -> p t n", n=72)
                    low(VBL[:, :, 0:HD], both[:, :, 0:HD], VBH[:, :, 0:HD])
                    low(VBL[:, :, HD:P], both[:, :, 0:HD], VBH[:, :, HD:P])
                    TS(iw[:, :, :], both[:, :, HD:72], 8 ** -0.5 * 32 ** -0.5, None, ALU.mult).then_inc(free, 1)
                elif name in rope_number:
                    cos = ROPE[:, 2 if kind in ("ik", "iq") else 0, :]
                    low(KL[:, 0, :], ps[:, :], KH[:, 0, :])
                    T(tmp[:, 0, :], ps[:, :], cos, ALU.mult).then_inc(free, 1)
                elif kind in ("q", "k"):
                    hi, lo = (QH, QL) if kind == "q" else (KH, KL)
                    low(lo[:, i % 2, :], ps[:, :], hi[:, i % 2, :],
                        HD ** -0.5 if kind == "q" else 1.0).then_inc(free, 1)
                elif kind in ("g", "gl"):
                    STT(sg[:, i % 2, :], sg[:, i % 2, :], 1.0, ps[:, :], ALU.add, ALU.mult).then_inc(free, 1)
                if kind != "ik":
                    refill.after(name)

            def rotated(name):
                rot = (name[0] + "_rot", name[1])
                sin = ROPE[:, 3 if name[0] in ("ik", "iq") else 1, :]
                dve.wait_ge(gemm_steps, acc_done[rot])
                T(tmp[:, 1, :], bank_of(rot)[:, :], sin, ALU.mult).then_inc(freed(rot)[0], 1)
                dve.wait_ge(*freed(rot))
                dve.wait_ge(*freed(name))
                r = rope_number[name]
                T(tmp[:, 2, :], tmp[:, 0, :], tmp[:, 1, :], ALU.add).then_inc(rope_sum, 1)
                dve.wait_ge(rope_sum, r + 1)
                dve.wait_ge(rope_hi, r + 1)
                hi, lo = rope_parts(name)
                low(lo, tmp[:, 2, :], hi, HD ** -0.5 if name[0] == "q" else 1.0).then_inc(rope_lo, 1)
                refill.after(rot)

            def row_max(n, part):
                dve.wait_ge(s_done, 3 * n + part + 1)
                if n < 2 * A_PAIRS and part == 0:
                    dve.wait_ge(bias_ready, n + 1)
                for qb in S_PARTS[part]:
                    w, c = P * (qb + 1), M_COL[qb]
                    src = sbank[S_BANK[part]][:, S_COL[qb]:S_COL[qb] + w]
                    m = mx[:, n % 2, c:c + 1]
                    if n < 2 * A_PAIRS:
                        step(dve.tensor_tensor_reduce(
                            out=prob[:, n % 2, OFF[qb]:OFF[qb] + w], in0=src,
                            in1=bias[:, n % 2, S - w:S], scale=1.0, scalar=-3e38,
                            op0=ALU.add, op1=ALU.max, accum_out=m))
                    else:
                        step(dve.tensor_reduce(m, src, AX, ALU.max))
                settle()
                c0, k = M_COL[S_PARTS[part][0]], len(S_PARTS[part])
                TS(nmx[:, n % 2, c0:c0 + k], mx[:, n % 2, c0:c0 + k], -1.0, None, ALU.mult)\
                    .then_inc(mx_ready, 1)

            def probabilities(n):
                dve.wait_ge(exp_done, 3 * n + 3)
                step(dve.reciprocal(rcp[:, n % 2, :], rs[:, n % 2, :]))
                settle()
                for qb in range(TB):
                    p = prob[:, n % 2, OFF[qb]:OFF[qb] + P * (qb + 1)]
                    c = M_COL[qb]
                    last = TS(p, p, rcp[:, n % 2, c:c + 1], None, ALU.mult)
                last.then_inc(prob_ready, 1)

            def transposed(n, part):
                dve.wait_ge(pt_hi, 3 * n + part + 1)
                w = sum(S - kb * P for kb in T_PARTS[part])
                c = T_OFF[T_PARTS[part][0]]
                low(PTL[:, c:c + w], tbank[T_BANK[part]][:, 0:w], PTH[:, c:c + w]).then_inc(pt_lo, 1)

            tiles_y = [0]

            def take_output(n):
                rows, hi, lo = gated(n)
                dve.wait_ge(o_done, n + 1)
                pair = n // 2
                dve.wait_ge(*freed(("g", pair)))
                STT(yt[rows, pair % 2, :], obank[n % 2][rows, :], 0.5, sg[rows, pair % 2, :],
                    ALU.mult, ALU.mult).then_inc(o_taken, 1)

            def y_parts(n):
                if n % 2 == 1:
                    _, hi, lo = gated(n)
                    tiles_y[0] += 1
                    dve.wait_ge(o_taken, n + 1)
                    dve.wait_ge(y_hi, tiles_y[0])
                    low(lo, yt[:, (n // 2) % 2, :], hi).then_inc(y_lo, 1)

            def attention(n0, n1, fills, tail, extra):
                for n in range(n0, n1 + 1):
                    names = list(fills[n] if n < n1 else tail)
                    turned = names.pop(0) if names and names[0][0].endswith("_rot") else None
                    if names:
                        refill.need(names[0])
                    for part in range(3):
                        if n < n1:
                            row_max(n, part)
                        if n > n0:
                            transposed(n - 1, part)
                        if part == 0 and n >= n0 + 2:
                            take_output(n - 2)
                        if part == 1 and n >= n0 + 2:
                            y_parts(n - 2)
                        if part == 0 and turned:
                            rotated((turned[0][:-4], turned[1]))
                    if n < n1:
                        probabilities(n)
                    extra(n)
                    for name in names:
                        if name[0].endswith("_rot"):
                            rotated((name[0][:-4], name[1]))
                        else:
                            evacuate(name)
                    if n < n1 and begun_early(fills, n):
                        refill.need(begun_early(fills, n))
                take_output(n1 - 1)
                y_parts(n1 - 1)

            def one_square(t, used, buf, total=0):
                dve.wait_ge(sq_used, used)
                T(sq[:, total, :], sq[:, total, :], yt[:, buf, :], ALU.add).then_inc(sq_used, 1)

            def scaled(src, t, gain, xh, xl, count):
                dve.wait_ge(xu_hi, count)
                low(xl[:, t, :], src[:, t, :], xh[:, t, :], vcol(vec, gain, t)).then_inc(xu_lo, 1)

            def normalise(r, src, gain, root, xh=XH, xl=XL, middle=lambda: None):
                def full(t):
                    if t >= 2:
                        dve.wait_ge(xn_lo, KD * r + t - 1)
                    STT(tmp[:, 2 + t % 2, :], src[:, t, :], gain(t), root, ALU.mult, ALU.mult)\
                        .then_inc(xn_f32, 1)

                def part(t):
                    dve.wait_ge(xn_hi, KD * r + t + 1)
                    low(xl[:, t, :], tmp[:, 2 + t % 2, :], xh[:, t, :]).then_inc(xn_lo, 1)

                full(0)
                for t in range(1, KD):
                    full(t)
                    part(t - 1)
                    if t == KD // 2:
                        middle()
                part(KD - 1)

            def log_sigmoid(src, n, dst, count):
                u, s, s2, p = (sp[:, j, 0:n] for j in (1, 2, 3, 4))
                STT(u, src, -1.0, src, ALU.mult, ALU.min).then_inc(ls_arg, 1)
                dve.wait_ge(ls_exp, count)
                step(TS(s, u, 2.0, None, ALU.add))
                settle()
                step(dve.reciprocal(s, s))
                settle()
                step(T(s, s, u, ALU.mult))
                settle()
                step(T(s2, s, s, ALU.mult))
                settle()
                step(TS(p, s2, 1.0 / 17, None, ALU.mult))
                settle()
                for k in range(7, 0, -1):
                    step(STT(p, p, 1.0 / (2 * k + 1), s2, ALU.add, ALU.mult))
                    settle()
                step(STT(p, p, 1.0, s, ALU.add, ALU.mult))
                settle()
                step(TS(s, src, 0.0, None, ALU.min))
                settle()
                STT(dst, p, -2.0, s, ALU.mult, ALU.add).then_inc(ls_ready, 1)

            dve.memset(ones[:, :], 1.0).then_inc(ones_ready, 1)

            dve.wait_ge(vec_loaded, 32)
            for t in range(KD):
                dve.wait_ge(sq_ready, t + 1)
                if 0 < t < KD - 1:
                    one_square(t, t - 1, (t - 1) % 2)
                scaled(XT, t, "gain1", XUH, XUL, t + 1)
                if t % 2 == 1:
                    refill.upto(t // 2 - (t == KD - 1))

            def row_factors(norm):
                dve.wait_ge(ssq_done, norm + 1)
                step(TS(mean[:, 0:TB], obank[0][:, 0:TB], 1.0 / D, EPS, ALU.mult, ALU.add))
                settle()
                dve.reciprocal(mean[:, 0:TB], mean[:, 0:TB]).then_inc(var_ready, 1)
                dve.wait_ge(root_ready, norm + 1)
                diagonals(root[:, norm, 0:TB])

            def diagonals(factors):
                for t in range(TB):
                    last = TS(diag[:, t * P:t * P + P], ident[:, :], factors[:, t:t + 1], None, ALU.mult)
                last.then_inc(diag_ready, 1)

            row_factors(0)
            refill.upto(3)
            dve.wait_ge(factor_ready, 1)
            normalise(0, XT, lambda t: vcol(vec, "gain1", t), obank[1][:, :],
                      middle=lambda: refill.upto(4))

            dve.wait_ge(const_loaded, 48)
            con = lambda name, n=P: wk[:, CON[name]:CON[name] + n]
            dve.tensor_copy(rotb[:, :], con("rot_b"))
            dve.tensor_copy(roti[:, :], con("rot_i"))
            dve.tensor_copy(tri[:, :], con("tri"))
            dve.tensor_copy(MB[:, 0:P], con("half"))
            TS(idbig[:, :], ident[:, :], BIG, None, ALU.mult)
            step(T(g12[:, :], vec[:, VEC["final1"]:VEC["final1"] + KD],
                   vec[:, VEC["gain2"]:VEC["gain2"] + KD], ALU.mult))
            TS(hvec[:, :], vec[:, HALVED], 0.5, None, ALU.mult).then_inc(consts_ready, 1)
            dve.wait_ge(consts_ready, 1)
            evacuate(("va", 0))
            for name in OPENING:
                if name[0].endswith("_rot"):
                    rotated((name[0][:-4], name[1]))
                else:
                    evacuate(name)
            dve.wait_ge(*freed(("vbiw_t", 0)))
            for m in range(24):
                j, h = m // 8 + 1, m % 8
                w = P * (j + 1)
                dve.wait_ge(index_relu, m + 1)
                src, dst = prob[:, m % 2, 0:w], wk[:, WK[j]:WK[j] + w]
                if h == 0:
                    TS(dst, src, iw[:, j, 0:1], None, ALU.mult).then_inc(index_sum, 1)
                else:
                    dve.wait_ge(index_sum, m)
                    STT(dst, src, iw[:, j, h:h + 1], dst, ALU.mult, ALU.add).then_inc(index_sum, 1)
            dve.wait_ge(index_sum, 24)
            for j in (1, 2, 3):
                step(dve.memset(wk[0:CH, WK[j + 1] - CH:WK[j + 1]], NOT_ADMITTED))

            def top_round():
                settle()
                for j in (1, 2, 3):
                    step(dve.max(m8[:, j - 1, :], wk[:, WK[j]:WK[j + 1]]))
                for j in (1, 2, 3):
                    dve.wait_ge(dve_own, own[0] - 2)
                    row = wk[:, WK[j]:WK[j + 1]]
                    step(dve.match_replace(out=row, in_to_replace=m8[:, j - 1, :], in_values=row,
                                           imm_value=TAKEN))

            left = [TOPK // 8]
            for t in range(OPENING_ZA, KD):
                for _ in range(1 + (t % 2)):
                    top_round()
                    left[0] -= 1
                evacuate(("za", t))
            evacuate(("q", 0))
            evacuate(("k", 0))

            def select(n):
                for _ in range(2 if n < 2 else 1):
                    if left[0] > 0:
                        top_round()
                        left[0] -= 1
                        if left[0] == 0:
                            settle()
                            TS(MB[:, P:NP], wk[:, :], TAKEN, -1.0, ALU.is_equal, ALU.add)\
                                .then_inc(consts_ready, 1)

            log_sigmoid(vec[:, VEC["ap"]:VEC["ap"] + LRU_T], LRU_T, sp[:, 5, 0:LRU_T], 1)
            dve.wait_ge(ls_ready, 1)
            for j, factor in enumerate((4.0, 8.0, -4.0)):
                last = TS(rate[:, j, :], sp[:, 5, 0:LRU_T], factor, None, ALU.mult)
            last.then_inc(consts_ready, 1)
            attention(0, 2 * PAIR_F0, slots_of_heads(0, PAIR_F0), [("zb", 0), ("zb", 1)], select)

            for t in range(KD):
                if t >= 2:
                    refill.need(("zb", t))
                    refill.after(("zb", t))
                refill.need(("pb", t))
                for name, gate, m in ((("pa", t), GA[:, t, :], 0), (("pb", t), GB[:, t % 2, :], 1)):
                    dve.wait_ge(gemm_steps, acc_done[name])
                    if m == 1:
                        dve.wait_ge(*freed(("zb", t)))
                    else:
                        dve.wait_ge(*freed(("za", t)))
                    STT(tmp[:, m, :], gate, 1.0, bank_of(name)[:, :], ALU.add, ALU.mult)\
                        .then_inc(freed(name)[0], 1)
                dve.wait_ge(*freed(("pa", t)))
                dve.wait_ge(*freed(("pb", t)))
                T(yt[:, t % 2, :], tmp[:, 0, :], tmp[:, 1, :], ALU.add).then_inc(mg_sum, 1)
                dve.wait_ge(mg_sum, t + 1)
                dve.wait_ge(mg_hi, t + 1)
                low(MGL[:, t, :], yt[:, t % 2, :], MGH[:, t, :], 0.5).then_inc(mg_lo, 1)
                refill.after(("pb", t))

            def residual(kind, res, ready, used, buf, double=False):
                def squares(t):
                    if double:
                        if t > 0:
                            dve.wait_ge(sq_ready, ready + 2 * t + 1)
                            one_square(t, used + 2 * t - 2, 0, 0)
                            dve.wait_ge(sq_ready, ready + 2 * t + 2)
                            one_square(t, used + 2 * t - 1, 1, 1)
                    else:
                        dve.wait_ge(sq_ready, ready + t + 1)
                        if t > 0:
                            one_square(t, used + t - 1, (buf + t - 1) % 2)

                for t in range(KD):
                    name = (kind, t)
                    refill.need(name)
                    if kind == "wout":
                        dve.wait_ge(res_loaded[t], 16)
                    elif kind == "lo":
                        step(STT(res[:, t, :], res[:, t, :], vcol(vec, "final1", t), obank[0][:, :],
                                 ALU.mult, ALU.mult))
                        settle()
                    dve.wait_ge(gemm_steps, acc_done[name])
                    T(res[:, t, :], bank_of(name)[:, :], res[:, t, :], ALU.add).then_inc(freed(name)[0], 1)
                    if t < KD - 1:
                        squares(t)
                    if kind == "lo":
                        scaled(res, t, "gain3", XH, XL, KD + t + 1)
                    refill.after(name)

            residual("wout", RES, KD, ADDS, 0, double=True)
            dve.wait_ge(ssq_done, 2)
            step(TS(mean[:, 0:TB], obank[0][:, 0:TB], 1.0 / D, EPS, ALU.mult, ALU.add))
            settle()
            step(TS(mean[:, TB:2 * TB], mean[:, 0:TB], EPS, None, ALU.mult))
            settle()
            step(STT(mean[:, TB:2 * TB], obank[0][:, TB:2 * TB], 1.0 / D, mean[:, TB:2 * TB],
                     ALU.mult, ALU.add))
            settle()
            dve.reciprocal(mean[:, :], mean[:, :]).then_inc(var_ready, 1)
            dve.wait_ge(root_ready, 2)
            diagonals(root[:, 1, TB:2 * TB])
            dve.wait_ge(factor_ready, 2)
            normalise(1, RES, lambda t: g12[:, t:t + 1], obank[1][:, :])

            step(dve.memset(prob[:, :, 0:3], 0.0))
            settle()

            def convolve(c):
                xb, xc = prob[:, c % 2, :], prob[:, c % 2, 640:640 + S]
                refill.need(("xb", c))
                dve.wait_ge(*freed(("xb", c)))
                if c >= 2:
                    dve.wait_ge(mult_sq, c - 1)
                tap = lambda i: vcol(vec, "conv_w", 4 * c + i)
                for i in (2, 1):
                    step(STT(xc, xb[:, i:i + S], tap(i), xc, ALU.mult, ALU.add))
                    settle()
                STT(xc, xb[:, 0:S], tap(0), xc, ALU.mult, ALU.add).then_inc(xc_ready, 1)

            def conv_part(c):
                xc = prob[:, c % 2, 640:640 + S]
                dve.wait_ge(xc_ready, c + 1)
                dve.wait_ge(xc_hi, c + 1)
                cs = slice((c % 2) * S, (c % 2) * S + S)
                low(PTL[:, cs], xc, PTH[:, cs]).then_inc(xc_lo, 1)
                refill.after(("xb", c))

            def decays(c):
                j = c % LRU_G
                refill.need(("i", c))
                settle()
                dve.wait_ge(*freed(("i", c)))
                STT(LX[:, j, :], tmp[:, 1 + c % 2, :], 1.0, prob[:, c % 2, 640:640 + S], ALU.add, ALU.mult)

            def squared_mult(c):
                dve.wait_ge(decay_ready, c + 1)
                lv = LV[:, c % LRU_G, :]
                STT(lv, squared_decay(c), 1.0, lv, ALU.add, ALU.mult).then_inc(mult_sq, 1)

            def scan(c):
                j = c % LRU_G
                dve.wait_ge(mult_ready, c // LRU_G + 1)
                step(T(LX[:, j, :], LX[:, j, :], LV[:, j, :], ALU.mult))
                settle()
                step(dve.tensor_tensor_scan(LV[:, j, :], LA[:, j, :], LX[:, j, :], 0.0, ALU.mult, ALU.add))
                settle()
                dve.wait_ge(*freed(("gl", c)))
                STT(yt[:, c % 2, :], sg[:, c % 2, :], 0.5, LV[:, j, :], ALU.mult, ALU.mult).then_inc(yl_f32, 1)

            def yl_parts(c):
                tiles_y[0] += 1
                dve.wait_ge(yl_f32, c + 1)
                dve.wait_ge(y_hi, tiles_y[0])
                low(YLL[:, c, :], yt[:, c % 2, :], YLH[:, c, :]).then_inc(y_lo, 1)

            convolve(0)
            conv_part(0)
            for c in range(LRU_T):
                if c + 1 < LRU_T:
                    convolve(c + 1)
                decays(c)
                if c + 1 < LRU_T:
                    conv_part(c + 1)
                if c >= 3:
                    yl_parts(c - 3)
                squared_mult(c)
                refill.after(("i", c))
                if c >= 2:
                    scan(c - 2)
                if c >= 1:
                    evacuate(("gl", c - 1))
                if c == 1:
                    diagonals(root[:, 1, 0:TB])
            yl_parts(LRU_T - 3)
            scan(LRU_T - 2)
            yl_parts(LRU_T - 2)
            evacuate(("gl", LRU_T - 1))
            scan(LRU_T - 1)
            yl_parts(LRU_T - 1)
            dve.wait_ge(factor_ready, 3)
            residual("lo", RES, 3 * KD, 3 * ADDS, KD - 1)
            row_factors(2)

            evacuate(("f", 0))
            dve.wait_ge(gemm_steps, acc_done[("f_t", 0)])
            for t in range(TB):
                ts = slice(t * 16, t * 16 + 16)
                last = STT(sp[:, 0, ts], bank_of(("f_t", 0))[:, ts], root[:, 2, t:t + 1], bfb[:, :],
                           ALU.mult, ALU.add)
            last.then_inc(freed(("f_t", 0))[0], 1)
            dve.wait_ge(*freed(("f_t", 0)))
            log_sigmoid(sp[:, 0, :], 64, sp[:, 5, :], 2)
            dve.wait_ge(res_spilled, 16 * KD)
            dve.wait_ge(factor_ready, 4)
            normalise(2, RES, lambda t: vcol(vec, "gain3", t), obank[1][:, :], XNH, XNL)
            evacuate(("vf", 0))
            dve.wait_ge(gemm_steps, acc_done[("cum", 0)])
            rest = tmp[0:16, 0, :]
            dve.tensor_copy(rest, bank_of(("cum", 0))[0:16, :]).then_inc(freed(("cum", 0))[0], 1)
            dve.wait_ge(*freed(("cum", 0)))
            for j in range(3):
                step(dve.tensor_copy(cparts(0, j), rest))
                settle()
                if j < 2:
                    step(T(rest, rest, cparts(0, j), ALU.subtract))
                last = TS(cparts(1, j), cparts(0, j), -1.0, None, ALU.mult)
                settle()
            last.then_inc(cum_split, 1)
            evacuate(("vf", 1))
            evacuate(("q", PAIR_F0))
            evacuate(("k", PAIR_F0))
            attention(2 * PAIR_F0, 2 * PAIRS, slots_of_heads(PAIR_F0, PAIRS), [], lambda n: None)
            dve.wait_ge(res_back, 16)
            residual("fo", RES2, 4 * KD, 4 * ADDS, 2 * (KD - 1))
            row_factors(3)
            dve.wait_ge(factor_ready, 5)
            for t in range(KD):
                STT(RES2[:, t, :], RES2[:, t, :], vcol(vec, "final2", t), obank[1][:, :], ALU.mult, ALU.mult)\
                    .then_inc(out_ready, 1)


def constants():
    con = np.zeros((P, NCON), np.float32)
    con[:, 0:P] = np.eye(P)
    tables = np.zeros((P, 4, S), np.float32)
    for i, (head, rot) in enumerate(((HD, HD // 4), (32, 32 // 4))):
        half = rot // 2
        inv = (np.float32(500000.0) ** (-np.arange(half, dtype=np.float32) / np.float32(half))).astype(np.float32)
        ang = (np.arange(S, dtype=np.float32)[:, None] * inv[None, :]).astype(np.float32).astype(np.float64)
        tables[:, 2 * i] = 1.0
        for base in range(0, P, head):
            for j in range(half):
                a, b = base + j, base + half + j
                con[b, CON[("rot_b", "rot_i")[i]] + a] = -1.0
                con[a, CON[("rot_b", "rot_i")[i]] + b] = 1.0
                tables[a, 2 * i] = tables[b, 2 * i] = np.cos(ang[:, j])
                tables[a, 2 * i + 1] = tables[b, 2 * i + 1] = np.sin(ang[:, j])
    p = np.arange(P)[:, None]
    con[:, CON["tri"]:CON["tri"] + P] = np.where(np.arange(P)[None, :] > p, -1.0, 0.0)
    con[:, CON["half"]:CON["half"] + P] = np.where((np.arange(P)[None, :] >= CH) & (p < CH), -1.0, 0.0)
    con[:, CON["upto"]:CON["upto"] + S] = np.arange(S)[None, :] >= p
    return con, tables


def pack(w_in, w_a, w_b, w_out, lru_in, wa, wx, lru_out, fox_in, fox_out):
    stream = np.zeros((len(PLAN["units"]), P, KD * P), np.float32)

    def columns(w, c0, n, k0=0, k1=None):
        part = w[k0 * P:(w.shape[0] if k1 is None else k1 * P), c0:c0 + n]
        return part.reshape(-1, P, n).transpose(1, 0, 2).reshape(P, -1)

    lout = np.concatenate([columns(lru_out, t * P, P) for t in range(KD)], axis=1)
    for u, (kind, i) in enumerate(PLAN["units"]):
        if kind == "va":
            part = columns(w_in, 1024, S, 2 * i, 2 * i + 2)
        elif kind == "vbiw":
            part = np.concatenate([w_in[:, 2624:2688], w_in[:, 3488:3496]], axis=1)
            part = columns(part, 0, 72)
        elif kind == "ik":
            part = columns(np.concatenate([w_in[:, 3456:3488]] * 4, axis=1), 0, P)
        elif kind == "kb":
            part = columns(np.concatenate([w_in[:, 2560:2624]] * 2, axis=1), 0, P)
        elif kind == "iq":
            part = columns(w_in, 3200 + i * P, P)
        elif kind == "za":
            part = columns(w_in, 3496 + i * P, P)
        elif kind == "zb":
            part = columns(w_in, 4520 + i * P, P)
        elif kind in ("q", "k", "g") and i < PAIR_B0:
            part = columns(w_in, {"q": 0, "k": 512, "g": 1536}[kind] + i * P, P)
        elif kind in ("q", "g") and i < PAIR_F0:
            part = columns(w_in, {"q": 2048, "g": 2688}[kind] + (i - PAIR_B0) * P, P)
        elif kind in ("q", "k", "g"):
            part = columns(fox_in, {"q": 0, "k": 1024, "g": 3072}[kind] + (i - PAIR_F0) * P, P)
        elif kind == "branch":
            part = np.concatenate([columns(w_a, i * P, P), columns(w_b, i * P, P)], axis=1)
        elif kind == "wout":
            part = columns(w_out, i * P, P)
        elif kind == "wax":
            part = np.concatenate([wa[i], wx[i]], axis=1)
        elif kind == "xb":
            part = columns(lru_in, i * P, P)
        elif kind == "gl":
            part = columns(lru_in, LRU_T * P + i * P, P)
        elif kind == "lout":
            part = lout[:, i * KD * P:(i + 1) * KD * P]
        elif kind == "f":
            part = columns(fox_in, 4096, 16)
        elif kind in ("vf0", "vf1"):
            part = columns(fox_in, 2048 + S * int(kind[2]), S, 2 * i, 2 * i + 2)
        elif kind == "fo":
            part = columns(fox_out, i * P, P)
        stream[u, :, 0:part.shape[1]] = part
    return stream


def kernel(**inputs):
    import concourse.bacc as bacc
    from concourse import mybir
    from concourse.bass_utils import run_bass_kernel_spmd

    a = {k: np.asarray(v) for k, v in inputs.items()}
    tiles = lambda v: v.reshape(-1, P).T
    vecs = np.concatenate([
        tiles(a["norm_gain"][0]), tiles(a["final_norm_gain"]), tiles(a["norm_g_2"][0]),
        tiles(a["norm_g_2"][1]), tiles(a["final_g_2"]),
        a["lru_conv_w_2"][0].reshape(4, LRU_T, P).transpose(2, 1, 0).reshape(P, 4 * LRU_T),
        tiles(a["lru_conv_b_2"][0]), tiles(a["b_merge"][0, 0]), tiles(a["b_merge"][0, 1]),
        tiles(a["lru_ba_2"][0]), tiles(a["lru_bx_2"][0]),
        tiles(a["lru_a_param_2"][0])], axis=1)
    con, tables = constants()
    arrays = {
        "xT": a["x"][0].T.reshape(KD, P, S).transpose(1, 0, 2),
        "vecs": vecs,
        "rel_ext": np.concatenate([a["rel_bias"][0][:, -1:]] * (2 * P - 1)
                                  + [a["rel_bias"][0][:, ::-1][:, 0:3 * P + 1]], axis=1),
        "b_f": a["fox_b_f_2"],
        "consts": con,
        "rope_tables": tables,
        "wstream": pack(a["w_in"][0], a["w_branch_a"][0], a["w_branch_b"][0], a["w_out"][0],
                        a["lru_w_in_2"][0], a["lru_wa_2"][0], a["lru_wx_2"][0],
                        a["lru_w_out_2"][0], a["fox_w_in_2"][0], a["fox_w_out_2"][0]),
    }
    arrays = {k: np.ascontiguousarray(v) for k, v in arrays.items()}
    nc = bacc.Bacc("TRN2", target_bir_lowering=False, num_devices=1)
    args = [nc.dram_tensor("in_" + k, v.shape, mybir.dt.from_np(v.dtype), kind="ExternalInput").ap()
            for k, v in arrays.items()]
    out = nc.dram_tensor("outT", (P, KD, S), mybir.dt.float32, kind="ExternalOutput").ap()
    build_program(nc, *args, out)
    got = run_bass_kernel_spmd(nc, [{"in_" + k: v for k, v in arrays.items()}], core_ids=[0]).results[0]["outT"]
    return np.ascontiguousarray(got.transpose(2, 1, 0).reshape(1, S, D))
```
